# Optimizing a Trainium2 kernel written in Bass

```python
import math
import jax, jax.numpy as jnp
from jax import lax
import numpy as np

D_MODEL = 2048
BATCH = 1
SEQ = 256
DEPTH = 2

CHUNK = 64
N_MIXERS = 2
Q_BLOCK = 128

MLA_HEADS = 16
QK_NOPE = 128
QK_ROPE = 64
V_HEAD = 128
Q_LORA = 512
KV_LORA = 512
ROPE_THETA = 10000.0
MLA_QK = QK_NOPE + QK_ROPE
MLA_WIDTH = MLA_HEADS * V_HEAD
MLA_IN = Q_LORA + KV_LORA + QK_ROPE + MLA_WIDTH

ML_HEADS = 8
ML_QK = 128
ML_V = 256
ML_QK_WIDTH = ML_HEADS * ML_QK
ML_WIDTH = ML_HEADS * ML_V
CONV_W = 4
ML_IN = 2 * ML_QK_WIDTH + 2 * ML_WIDTH + 2 * ML_HEADS + ML_WIDTH

ALPHA = (2 * DEPTH) ** 0.25
BETA = (8 * DEPTH) ** -0.25
EPS = 1e-6


def _rmsnorm(x, w):
    xf = x.astype(jnp.float32)
    y = xf * lax.rsqrt(jnp.mean(xf * xf, axis=-1, keepdims=True) + EPS)
    return y.astype(x.dtype) * w

def _layernorm(x, w, b):
    xf = x.astype(jnp.float32)
    mu = jnp.mean(xf, axis=-1, keepdims=True)
    var = jnp.mean(jnp.square(xf - mu), axis=-1, keepdims=True)
    return ((xf - mu) * lax.rsqrt(var + EPS)).astype(x.dtype) * w + b

def _rope_tables(positions, dtype):
    inv_freq = ROPE_THETA ** (-jnp.arange(0, QK_ROPE, 2, dtype=jnp.float32) / QK_ROPE)
    ang = positions.astype(jnp.float32)[..., None] * inv_freq
    return jnp.cos(ang).astype(dtype), jnp.sin(ang).astype(dtype)

def _rope(x, cos, sin):
    half = x.shape[-1] // 2
    x1, x2 = x[..., :half], x[..., half:]
    return jnp.concatenate([x1 * cos - x2 * sin, x1 * sin + x2 * cos], axis=-1)

def _chunk_causal_attention(q, k, v):
    b, s, h, dk = q.shape
    nb = s // Q_BLOCK
    scale = dk ** -0.5
    q_blocks = q.reshape(b, nb, Q_BLOCK, h, dk).transpose(1, 0, 2, 3, 4)
    key_chunk = jnp.arange(s) // CHUNK

    def one_block(args):
        qb, bi = args
        q_chunk = (bi * Q_BLOCK + jnp.arange(Q_BLOCK)) // CHUNK
        mask = key_chunk[None, :] <= q_chunk[:, None]
        sc = jnp.einsum('bqhd,bkhd->bhqk', qb, k).astype(jnp.float32) * scale
        sc = jnp.where(mask, sc, -jnp.inf)
        p = jax.nn.softmax(sc, axis=-1).astype(v.dtype)
        return jnp.einsum('bhqk,bkhd->bqhd', p, v)

    out = lax.map(one_block, (q_blocks, jnp.arange(nb)))
    return out.transpose(1, 0, 2, 3, 4).reshape(b, s, h, v.shape[-1])

def _mla_mixer(x, cos, sin, w_in, q_norm, w_qb, kv_norm, w_kvb, w_out):
    b, s, _ = x.shape
    proj = x @ w_in
    c_q, c_kv, k_rope, z = jnp.split(
        proj, [Q_LORA, Q_LORA + KV_LORA, Q_LORA + KV_LORA + QK_ROPE], axis=-1)
    q = (_rmsnorm(c_q, q_norm) @ w_qb).reshape(b, s, MLA_HEADS, MLA_QK)
    q_nope, q_rope = q[..., :QK_NOPE], q[..., QK_NOPE:]
    kv = (_rmsnorm(c_kv, kv_norm) @ w_kvb).reshape(b, s, MLA_HEADS, QK_NOPE + V_HEAD)
    k_nope, v = kv[..., :QK_NOPE], kv[..., QK_NOPE:]
    q_rope = _rope(q_rope, cos[:, :, None, :], sin[:, :, None, :])
    k_rope = _rope(k_rope, cos, sin)
    q = jnp.concatenate([q_nope, q_rope], axis=-1)
    k = jnp.concatenate(
        [k_nope, jnp.broadcast_to(k_rope[:, :, None, :], (b, s, MLA_HEADS, QK_ROPE))], axis=-1)
    attn = _chunk_causal_attention(q, k, v).reshape(b, s, MLA_WIDTH)
    return (attn * jax.nn.silu(z)) @ w_out

def _causal_depthwise_conv(x, w, bias):
    c = x.shape[-1]
    y = lax.conv_general_dilated(
        x, w[:, None, :], window_strides=(1,), padding=[(CONV_W - 1, 0)],
        dimension_numbers=('NWC', 'WIO', 'NWC'), feature_group_count=c)
    return y + bias

def _mlstm_chunkwise(q, k, v, i_pre, f_pre):
    b, s, h, dk = q.shape
    dv = v.shape[-1]
    nc = s // CHUNK
    f32 = jnp.float32

    def chunks(t):
        return t.astype(f32).reshape(b, nc, CHUNK, h, -1).transpose(1, 0, 3, 2, 4)

    def gate_chunks(t):
        return t.astype(f32).reshape(b, nc, CHUNK, h).transpose(1, 0, 3, 2)

    qc = chunks(q)
    kc = chunks(k) * (dk ** -0.5)
    vc = chunks(v)
    log_i = gate_chunks(i_pre)
    log_f = jax.nn.log_sigmoid(gate_chunks(f_pre))
    tril = jnp.tril(jnp.ones((CHUNK, CHUNK), dtype=bool))

    def step(carry, xs):
        c_st, n_st, m_st = carry
        qx, kx, vx, li, lf = xs
        bcum = jnp.cumsum(lf, axis=-1)
        dmat = bcum[..., :, None] - bcum[..., None, :] + li[..., None, :]
        dmat = jnp.where(tril, dmat, -jnp.inf)
        m_inter = bcum + m_st[..., None]
        m_t = jnp.maximum(m_inter, jnp.max(dmat, axis=-1))
        w_inter = jnp.exp(m_inter - m_t)
        s_qk = jnp.einsum('bhtd,bhsd->bhts', qx, kx) * jnp.exp(dmat - m_t[..., None])
        num = (w_inter[..., None] * jnp.einsum('bhtd,bhdv->bhtv', qx, c_st)
               + jnp.einsum('bhts,bhsv->bhtv', s_qk, vx))
        den = w_inter * jnp.einsum('bhtd,bhd->bht', qx, n_st) + jnp.sum(s_qk, axis=-1)
        h_out = num / jnp.maximum(jnp.abs(den), jnp.exp(-m_t))[..., None]
        b_last = bcum[..., -1]
        g = b_last[..., None] - bcum + li
        m_new = jnp.maximum(b_last + m_st, jnp.max(g, axis=-1))
        decay = jnp.exp(b_last + m_st - m_new)
        wk = jnp.exp(g - m_new[..., None])
        c_new = decay[..., None, None] * c_st + jnp.einsum('bhs,bhsd,bhsv->bhdv', wk, kx, vx)
        n_new = decay[..., None] * n_st + jnp.einsum('bhs,bhsd->bhd', wk, kx)
        return (c_new, n_new, m_new), h_out

    init = (jnp.zeros((b, h, dk, dv), f32), jnp.zeros((b, h, dk), f32), jnp.zeros((b, h), f32))
    _, hs = lax.scan(step, init, (qc, kc, vc, log_i, log_f))
    return hs.transpose(1, 0, 3, 2, 4).reshape(b, s, h, dv)

def _mlstm_mixer(x, w_in, conv_w, conv_b, gate_b, head_norm, w_out):
    b, s, _ = x.shape
    proj = x @ w_in
    o1 = 2 * ML_QK_WIDTH
    o2 = o1 + ML_WIDTH
    o3 = o2 + ML_WIDTH
    o4 = o3 + 2 * ML_HEADS
    qk, v, o, gates, z = jnp.split(proj, [o1, o2, o3, o4], axis=-1)
    qk = jax.nn.silu(_causal_depthwise_conv(qk, conv_w, conv_b))
    q, k = jnp.split(qk, 2, axis=-1)
    gates = gates + gate_b
    i_pre, f_pre = gates[..., :ML_HEADS], gates[..., ML_HEADS:]
    cell = _mlstm_chunkwise(q.reshape(b, s, ML_HEADS, ML_QK), k.reshape(b, s, ML_HEADS, ML_QK),
                            v.reshape(b, s, ML_HEADS, ML_V), i_pre, f_pre)
    cell = _rmsnorm(cell.astype(x.dtype), head_norm.reshape(ML_HEADS, ML_V)).reshape(b, s, ML_WIDTH)
    hcell = jax.nn.sigmoid(o) * cell
    return (hcell * jax.nn.silu(z)) @ w_out

def first_inputs(seed: int = 0) -> dict:
    key = jax.random.key(seed)
    ks = jax.random.split(key, 20)
    n_a = (DEPTH + N_MIXERS - 1) // N_MIXERS
    n_b = DEPTH // N_MIXERS

    def nrm(k, shape, scale):
        return jax.random.normal(k, shape, jnp.float32) * scale

    x = nrm(ks[0], (BATCH, SEQ, D_MODEL), 1.0)
    offsets = jax.random.randint(ks[1], (BATCH, 1), 0, 4096, dtype=jnp.int32)
    positions = offsets + jnp.arange(SEQ, dtype=jnp.int32)[None, :]

    mla_w_in = nrm(ks[2], (n_a, D_MODEL, MLA_IN), D_MODEL ** -0.5)
    mla_q_norm = 1.0 + nrm(ks[3], (n_a, Q_LORA), 0.02)
    mla_w_qb = nrm(ks[4], (n_a, Q_LORA, MLA_HEADS * MLA_QK), Q_LORA ** -0.5)
    mla_kv_norm = 1.0 + nrm(ks[5], (n_a, KV_LORA), 0.02)
    mla_w_kvb = nrm(ks[6], (n_a, KV_LORA, MLA_HEADS * (QK_NOPE + V_HEAD)), KV_LORA ** -0.5)
    mla_w_out = nrm(ks[7], (n_a, MLA_WIDTH, D_MODEL), BETA * MLA_WIDTH ** -0.5)

    ml_w_in = nrm(ks[8], (n_b, D_MODEL, ML_IN), D_MODEL ** -0.5)
    ml_conv_w = nrm(ks[9], (n_b, CONV_W, 2 * ML_QK_WIDTH), CONV_W ** -0.5)
    ml_conv_b = nrm(ks[10], (n_b, 2 * ML_QK_WIDTH), 0.02)
    i_bias = nrm(ks[11], (n_b, ML_HEADS), 0.1)
    f_bias = jnp.linspace(3.0, 6.0, ML_HEADS, dtype=jnp.float32)[None, :] + nrm(ks[12], (n_b, ML_HEADS), 0.1)
    ml_gate_b = jnp.concatenate([i_bias, f_bias], axis=-1)
    ml_head_norm = 1.0 + nrm(ks[13], (n_b, ML_WIDTH), 0.02)
    ml_w_out = nrm(ks[14], (n_b, ML_WIDTH, D_MODEL), BETA * ML_WIDTH ** -0.5)

    ln_w = 1.0 + nrm(ks[15], (DEPTH, D_MODEL), 0.02)
    ln_b = nrm(ks[16], (DEPTH, D_MODEL), 0.02)
    return {'x': x, 'positions': positions,
            'mla_w_in': mla_w_in, 'mla_q_norm': mla_q_norm, 'mla_w_qb': mla_w_qb,
            'mla_kv_norm': mla_kv_norm, 'mla_w_kvb': mla_w_kvb, 'mla_w_out': mla_w_out,
            'ml_w_in': ml_w_in, 'ml_conv_w': ml_conv_w, 'ml_conv_b': ml_conv_b,
            'ml_gate_b': ml_gate_b, 'ml_head_norm': ml_head_norm, 'ml_w_out': ml_w_out,
            'ln_w': ln_w, 'ln_b': ln_b}

def first_block(x, positions, mla_w_in, mla_q_norm, mla_w_qb, mla_kv_norm, mla_w_kvb, mla_w_out,
              ml_w_in, ml_conv_w, ml_conv_b, ml_gate_b, ml_head_norm, ml_w_out, ln_w, ln_b):
    cos, sin = _rope_tables(positions, x.dtype)
    for layer in range(DEPTH):
        j = layer // N_MIXERS
        if layer % N_MIXERS == 0:
            y = _mla_mixer(x, cos, sin, mla_w_in[j], mla_q_norm[j], mla_w_qb[j],
                           mla_kv_norm[j], mla_w_kvb[j], mla_w_out[j])
        else:
            y = _mlstm_mixer(x, ml_w_in[j], ml_conv_w[j], ml_conv_b[j], ml_gate_b[j],
                             ml_head_norm[j], ml_w_out[j])
        x = _layernorm(ALPHA * x + y, ln_w[layer], ln_b[layer])
    return x


DEPTH_2 = 1

HEAD_DIM = 64
N_MIXERS_2 = 4
GROUP_WIDTH = D_MODEL // N_MIXERS_2
N_HEADS = GROUP_WIDTH // HEAD_DIM
NSA_KV_HEADS = 2
NSA_GQA = N_HEADS // NSA_KV_HEADS
CMP_LEN = 32
CMP_STRIDE = 16
SLC_LEN = 64
SLC_TOP = 16
WINDOW = 512
FORCE_BONUS = 1.0e3
N_BUCKETS = 32
MAX_DISTANCE = 1024
CONV_W_2 = 3
CHUNK_2 = 128
D_FF = -(-8 * D_MODEL // (3 * 256)) * 256
NEG_INF = -1.0e30

A_Q_COLS = N_HEADS * HEAD_DIM
A_KV_COLS = 6 * NSA_KV_HEADS * HEAD_DIM
A_GATE_COLS = 3 * N_HEADS
B_COLS = 3 * GROUP_WIDTH
C_COLS = 2 * GROUP_WIDTH
D_COLS = 3 * GROUP_WIDTH
SPLIT_POINTS = (A_Q_COLS, A_Q_COLS + A_KV_COLS, A_Q_COLS + A_KV_COLS + A_GATE_COLS, A_Q_COLS + A_KV_COLS + A_GATE_COLS + B_COLS, A_Q_COLS + A_KV_COLS + A_GATE_COLS + B_COLS + C_COLS)
W_IN_COLS = SPLIT_POINTS[-1] + D_COLS


def rms_norm(x, g, eps=1e-6):
    xf = x.astype(jnp.float32)
    y = xf * lax.rsqrt(jnp.mean(xf * xf, axis=-1, keepdims=True) + eps)
    return (y * g.astype(jnp.float32)).astype(x.dtype)

def layer_norm_noaffine(x, eps=1e-5):
    xf = x.astype(jnp.float32)
    mu = jnp.mean(xf, axis=-1, keepdims=True)
    var = jnp.mean(jnp.square(xf - mu), axis=-1, keepdims=True)
    return ((xf - mu) * lax.rsqrt(var + eps)).astype(x.dtype)

def gelu(x):
    return jax.nn.gelu(x, approximate=True)

def rel_bucket(dist):
    n = jnp.maximum(dist, 0)
    max_exact = N_BUCKETS // 2
    nf = jnp.maximum(n, 1).astype(jnp.float32)
    large = max_exact + (jnp.log(nf / max_exact) / math.log(MAX_DISTANCE / max_exact) * (N_BUCKETS - max_exact)).astype(jnp.int32)
    large = jnp.minimum(large, N_BUCKETS - 1)
    return jnp.where(n < max_exact, n, large)

def rel_bias_heads(dist, table):
    b = table[rel_bucket(dist)].astype(jnp.float32)
    b = jnp.moveaxis(b, -1, 0)
    return b.reshape(NSA_KV_HEADS, NSA_GQA, *dist.shape)

def masked_softmax(s, mask):
    s = jnp.where(mask, s, NEG_INF)
    p = jax.nn.softmax(s, axis=-1)
    return jnp.where(mask, p, 0.0)

def cmp_slc_overlap(n_cmp, n_slc):
    c0 = np.arange(n_cmp)[:, None] * CMP_STRIDE
    s0 = np.arange(n_slc)[None, :] * SLC_LEN
    ov = np.minimum(c0 + CMP_LEN, s0 + SLC_LEN) - np.maximum(c0, s0)
    return (np.maximum(ov, 0) / CMP_LEN).astype(np.float32)

def nsa_attention(q, k_c, v_c, k_s, v_s, k_w, v_w, gates, q_gain, k_gain, cmp_pos, cmp_w1, cmp_w2, rel_table):
    B, T = q.shape[0], q.shape[1]
    G, R, Dh = NSA_KV_HEADS, NSA_GQA, HEAD_DIM
    scale = Dh ** -0.5
    q = rms_norm(q, q_gain).reshape(B, T, G, R, Dh)
    k_s = rms_norm(k_s, k_gain)
    k_w = rms_norm(k_w, k_gain)
    t_pos = jnp.arange(T, dtype=jnp.int32)

    n_cmp = (T - CMP_LEN) // CMP_STRIDE + 1
    blk = np.arange(n_cmp)[:, None] * CMP_STRIDE + np.arange(CMP_LEN)[None, :]

    def compress(z, i):
        zb = z[:, blk] + cmp_pos[i][None, None, :, None, :]
        zb = zb.transpose(0, 1, 3, 2, 4).reshape(B, n_cmp, G, CMP_LEN * Dh)
        return gelu(zb @ cmp_w1[i]) @ cmp_w2[i]

    kc = rms_norm(compress(k_c, 0), k_gain)
    vc = compress(v_c, 1)
    cmp_end = jnp.asarray(blk[:, -1], jnp.int32)
    dist_c = t_pos[:, None] - cmp_end[None, :]
    s_c = jnp.einsum('btgrd,bngd->bgrtn', q, kc).astype(jnp.float32) * scale + rel_bias_heads(dist_c, rel_table)
    p_c = masked_softmax(s_c, dist_c >= 0)
    o_cmp = jnp.einsum('bgrtn,bngd->btgrd', p_c.astype(vc.dtype), vc)

    n_slc = T // SLC_LEN
    top = min(SLC_TOP, n_slc)
    imp = jnp.einsum('bgrtn,nj->bgtj', p_c, jnp.asarray(cmp_slc_overlap(n_cmp, n_slc)))
    j_idx = jnp.arange(n_slc, dtype=jnp.int32)
    cur = t_pos // SLC_LEN
    valid = (j_idx[None, :] * SLC_LEN) <= t_pos[:, None]
    forced = (j_idx[None, :] == 0) | (j_idx[None, :] == cur[:, None]) | (j_idx[None, :] == cur[:, None] - 1)
    score = jnp.where(valid, imp + jnp.where(forced, FORCE_BONUS, 0.0), NEG_INF)
    _, sel = lax.top_k(score, top)

    ks_blk = k_s.reshape(B, n_slc, SLC_LEN, G, Dh).transpose(0, 3, 1, 2, 4)
    vs_blk = v_s.reshape(B, n_slc, SLC_LEN, G, Dh).transpose(0, 3, 1, 2, 4)
    pad = ((0, 0), (WINDOW, 0), (0, 0), (0, 0))
    kw_pad = jnp.pad(k_w, pad)
    vw_pad = jnp.pad(v_w, pad)
    table_g = rel_table.reshape(N_BUCKETS, G, R)
    g_idx = jnp.arange(G)[None, :, None, None, None]
    gather_blocks = jax.vmap(jax.vmap(lambda blocks, ix: blocks[ix]))
    win_len = WINDOW + Q_BLOCK

    def block_fn(qb):
        qs = qb * Q_BLOCK
        qt = qs + jnp.arange(Q_BLOCK, dtype=jnp.int32)
        qblk = lax.dynamic_slice_in_dim(q, qs, Q_BLOCK, axis=1)
        ix = lax.dynamic_slice_in_dim(sel, qs, Q_BLOCK, axis=2)
        ksel = gather_blocks(ks_blk, ix)
        vsel = gather_blocks(vs_blk, ix)
        kpos = ix[..., None] * SLC_LEN + jnp.arange(SLC_LEN, dtype=jnp.int32)
        d_s = qt[None, None, :, None, None] - kpos
        b_s = jnp.moveaxis(table_g[rel_bucket(d_s), g_idx].astype(jnp.float32), -1, 2)
        s_s = jnp.einsum('btgrd,bgtkld->bgrtkl', qblk, ksel).astype(jnp.float32) * scale + b_s
        shp = s_s.shape
        p_s = masked_softmax(s_s.reshape(B, G, R, Q_BLOCK, -1), (d_s >= 0).reshape(B, G, 1, Q_BLOCK, -1)).reshape(shp)
        o_s = jnp.einsum('bgrtkl,bgtkld->btgrd', p_s.astype(vsel.dtype), vsel)
        kw = lax.dynamic_slice_in_dim(kw_pad, qs, win_len, axis=1)
        vw = lax.dynamic_slice_in_dim(vw_pad, qs, win_len, axis=1)
        kp = qs - WINDOW + jnp.arange(win_len, dtype=jnp.int32)
        d_w = qt[:, None] - kp[None, :]
        m_w = (d_w >= 0) & (d_w < WINDOW) & (kp[None, :] >= 0)
        s_w = jnp.einsum('btgrd,bsgd->bgrts', qblk, kw).astype(jnp.float32) * scale + rel_bias_heads(d_w, rel_table)
        p_w = masked_softmax(s_w, m_w)
        o_w = jnp.einsum('bgrts,bsgd->btgrd', p_w.astype(vw.dtype), vw)
        return o_s, o_w

    o_slc, o_win = lax.map(block_fn, jnp.arange(T // Q_BLOCK, dtype=jnp.int32))
    o_slc = jnp.moveaxis(o_slc, 0, 1).reshape(B, T, G, R, Dh)
    o_win = jnp.moveaxis(o_win, 0, 1).reshape(B, T, G, R, Dh)

    g = jax.nn.sigmoid(gates.astype(jnp.float32)).astype(q.dtype).reshape(B, T, G, R, 3)
    o = g[..., 0:1] * o_cmp + g[..., 1:2] * o_slc + g[..., 2:3] * o_win
    return o.reshape(B, T, G * R * Dh)

def short_conv_mixer(cols, conv_w):
    b_gate, c_gate, h = jnp.split(cols, 3, axis=-1)
    z = c_gate * h
    T = z.shape[1]
    zp = jnp.pad(z, ((0, 0), (CONV_W_2 - 1, 0), (0, 0)))
    y = conv_w[0] * zp[:, 0:T]
    for i in range(1, CONV_W_2):
        y = y + conv_w[i] * zp[:, i:i + T]
    return b_gate * y

def spatial_gating_mixer(cols, sgu_w, sgu_b):
    B, T = cols.shape[0], cols.shape[1]
    u, v = jnp.split(gelu(cols), 2, axis=-1)
    v = layer_norm_noaffine(v).reshape(B, T // CHUNK_2, CHUNK_2, N_HEADS, HEAD_DIM)
    w = sgu_w * jnp.asarray(np.tril(np.ones((CHUNK_2, CHUNK_2), np.float32)), sgu_w.dtype)
    s = jnp.einsum('hpq,bcqhe->bcphe', w, v) + sgu_b.T[None, None, :, :, None]
    return u * s.reshape(B, T, GROUP_WIDTH)

def stick_breaking_attention(q, k, v):
    B, T, H, Dh = q.shape
    scale = Dh ** -0.5
    outs = []
    for qb in range(T // Q_BLOCK):
        qs, qe = qb * Q_BLOCK, (qb + 1) * Q_BLOCK
        z = jnp.einsum('bthd,bshd->bhts', q[:, qs:qe], k[:, :qe]).astype(jnp.float32) * scale
        mask = jnp.asarray(np.arange(qe)[None, :] < np.arange(qs, qe)[:, None])
        log_beta = jax.nn.log_sigmoid(z)
        log_1m = jnp.where(mask, log_beta - z, 0.0)
        tail = lax.cumsum(log_1m, axis=3, reverse=True) - log_1m
        a = jnp.where(mask, jnp.exp(log_beta + tail), 0.0)
        outs.append(jnp.einsum('bhts,bshd->bthd', a.astype(v.dtype), v[:, :qe]))
    return jnp.concatenate(outs, axis=1).reshape(B, T, H * Dh)

def second_inputs(seed: int = 0) -> dict:
    key = jax.random.key(seed)
    ks = jax.random.split(key, 18)
    f32 = jnp.float32

    def nrm(k, shape, scale):
        return jax.random.normal(k, shape, f32) * scale

    res_scale = (2 * DEPTH_2) ** -0.5
    return {
        'x': nrm(ks[0], (BATCH, SEQ, D_MODEL), 1.0),
        'w_in': nrm(ks[1], (DEPTH_2, D_MODEL, W_IN_COLS), D_MODEL ** -0.5),
        'w_out': nrm(ks[2], (DEPTH_2, D_MODEL, D_MODEL), D_MODEL ** -0.5 * res_scale),
        'norm_mix': 1.0 + nrm(ks[3], (DEPTH_2, D_MODEL), 0.05),
        'norm_ffn': 1.0 + nrm(ks[4], (DEPTH_2, D_MODEL), 0.05),
        'q_gain': 1.0 + nrm(ks[5], (DEPTH_2, HEAD_DIM), 0.05),
        'k_gain': 1.0 + nrm(ks[6], (DEPTH_2, HEAD_DIM), 0.05),
        'cmp_pos': nrm(ks[7], (DEPTH_2, 2, CMP_LEN, HEAD_DIM), 0.1),
        'cmp_w1': nrm(ks[8], (DEPTH_2, 2, CMP_LEN * HEAD_DIM, HEAD_DIM), (CMP_LEN * HEAD_DIM) ** -0.5),
        'cmp_w2': nrm(ks[9], (DEPTH_2, 2, HEAD_DIM, HEAD_DIM), HEAD_DIM ** -0.5),
        'rel_table': nrm(ks[10], (N_BUCKETS, N_HEADS), 0.5),
        'conv_w': nrm(ks[11], (DEPTH_2, CONV_W_2, GROUP_WIDTH), CONV_W_2 ** -0.5),
        'sgu_w': nrm(ks[12], (DEPTH_2, N_HEADS, CHUNK_2, CHUNK_2), CHUNK_2 ** -0.5),
        'sgu_b': 1.0 + nrm(ks[13], (DEPTH_2, N_HEADS, CHUNK_2), 0.1),
        'group_gain': 1.0 + nrm(ks[14], (DEPTH_2, D_MODEL), 0.05),
        'w_ffn_gate': nrm(ks[15], (DEPTH_2, D_MODEL, D_FF), D_MODEL ** -0.5),
        'w_ffn_up': nrm(ks[16], (DEPTH_2, D_MODEL, D_FF), D_MODEL ** -0.5),
        'w_ffn_down': nrm(ks[17], (DEPTH_2, D_FF, D_MODEL), D_FF ** -0.5 * res_scale),
    }

def second_block(x, w_in, w_out, norm_mix, norm_ffn, q_gain, k_gain, cmp_pos, cmp_w1, cmp_w2, rel_table, conv_w, sgu_w, sgu_b, group_gain, w_ffn_gate, w_ffn_up, w_ffn_down):
    B, T = x.shape[0], x.shape[1]
    for l in range(DEPTH_2):
        h = rms_norm(x, norm_mix[l])
        proj = h @ w_in[l]
        a_q, a_kv, a_g, b_cols, c_cols, d_cols = jnp.split(proj, SPLIT_POINTS, axis=-1)
        kv = a_kv.reshape(B, T, 6, NSA_KV_HEADS, HEAD_DIM)
        o_a = nsa_attention(a_q.reshape(B, T, N_HEADS, HEAD_DIM), kv[:, :, 0], kv[:, :, 1], kv[:, :, 2], kv[:, :, 3], kv[:, :, 4], kv[:, :, 5], a_g.reshape(B, T, N_HEADS, 3), q_gain[l], k_gain[l], cmp_pos[l], cmp_w1[l], cmp_w2[l], rel_table)
        o_b = short_conv_mixer(b_cols, conv_w[l])
        o_c = spatial_gating_mixer(c_cols, sgu_w[l], sgu_b[l])
        dq, dk, dv = jnp.split(d_cols, 3, axis=-1)
        o_d = stick_breaking_attention(dq.reshape(B, T, N_HEADS, HEAD_DIM), dk.reshape(B, T, N_HEADS, HEAD_DIM), dv.reshape(B, T, N_HEADS, HEAD_DIM))
        mixed = jnp.stack([o_a, o_b, o_c, o_d], axis=2)
        mixed = rms_norm(mixed, group_gain[l].reshape(N_MIXERS_2, GROUP_WIDTH))
        x = x + mixed.reshape(B, T, D_MODEL) @ w_out[l]
        h = rms_norm(x, norm_ffn[l])
        x = x + (jax.nn.silu(h @ w_ffn_gate[l]) * (h @ w_ffn_up[l])) @ w_ffn_down[l]
    return x


def setup_inputs(seed=0):
    out = dict(first_inputs(seed))
    for name, value in second_inputs(seed + 1).items():
        if name != "x":
            out[name + "_2"] = value
    return out


def reference(
    x, positions, mla_w_in, mla_q_norm, mla_w_qb, mla_kv_norm, mla_w_kvb, mla_w_out, ml_w_in,
    ml_conv_w, ml_conv_b, ml_gate_b, ml_head_norm, ml_w_out, ln_w, ln_b, w_in_2, w_out_2,
    norm_mix_2, norm_ffn_2, q_gain_2, k_gain_2, cmp_pos_2, cmp_w1_2, cmp_w2_2, rel_table_2,
    conv_w_2, sgu_w_2, sgu_b_2, group_gain_2, w_ffn_gate_2, w_ffn_up_2, w_ffn_down_2,
):
    x = first_block(
        x, positions, mla_w_in, mla_q_norm, mla_w_qb, mla_kv_norm, mla_w_kvb, mla_w_out,
        ml_w_in, ml_conv_w, ml_conv_b, ml_gate_b, ml_head_norm, ml_w_out, ln_w, ln_b,
    )
    return second_block(
        x, w_in_2, w_out_2, norm_mix_2, norm_ffn_2, q_gain_2, k_gain_2, cmp_pos_2, cmp_w1_2,
        cmp_w2_2, rel_table_2, conv_w_2, sgu_w_2, sgu_b_2, group_gain_2, w_ffn_gate_2,
        w_ffn_up_2, w_ffn_down_2,
    )


_drawn_inputs = setup_inputs


def setup_inputs(seed=0):
    import zlib

    import numpy as np

    out = dict(_drawn_inputs(seed))
    spreads = {}
    factors = {'mla_q_norm': 8.0,
     'mla_kv_norm': 8.0,
     'ml_conv_b': 8.0,
     'ml_head_norm': 8.0,
     'q_gain_2': 4.564,
     'k_gain_2': 6.325}
    for name, (base, spread) in spreads.items():
        noise = np.random.default_rng([zlib.crc32(name.encode()), seed]).standard_normal(out[name].shape)
        drawn = base * np.exp(spread * noise) if base else spread * noise
        out[name] = __import__('jax').numpy.asarray(drawn.astype(out[name].dtype))
    for name, factor in factors.items():
        out[name] = (out[name] * factor).astype(out[name].dtype)
    return out
```

```python
from contextlib import ExitStack

import numpy as np
import concourse.bass as bass
from concourse import mybir

F32 = mybir.dt.float32
I32 = mybir.dt.int32
ALU = mybir.AluOpType
ACT = mybir.ActivationFunctionType
AX = mybir.AxisListType.X

T = 256
DM = 2048
NEG = -1.0e30
EPS = 1e-6
ALPHA = 4.0 ** 0.25
UCOLS = 2048
NSLOT = 6
FFN_BLOCKS = 44


def weight_tiles():
    tiles = []

    def t_blocks(src, blocks, rows, perm=None):
        for cols in blocks:
            for k in range(rows // 128):
                tiles.append((src, k * 128, cols, perm))

    def r(a, n):
        return list(range(a, a + n))

    t_blocks("mla_w_in", [r(128 * b, 128) for b in range(8)] + [r(1024, 64)], DM)
    t_blocks("mla_w_qb", [r(192 * h, 128) for h in range(16)], 512)
    for half in range(2):
        t_blocks("mla_w_qb", [[192 * (4 * g + i) + 128 + 32 * half + j for i in range(4) for j in range(32)]
                              for g in range(4)], 512)
    t_blocks("mla_w_kvb", [r(256 * h, 128) for h in range(16)], 512)
    t_blocks("mla_w_kvb", [[256 * (4 * n + i) + 128 + j for i in range(4) for j in range(128)]
                           for n in range(4)], 512)
    t_blocks("mla_w_in", [r(1088 + 128 * b, 128) for b in range(16)], DM)
    t_blocks("mla_w_out", [r(128 * b, 128) for b in range(16)], DM)

    t_blocks("ml_w_in", [r(6144, 8), r(6152, 8)], DM)
    t_blocks("ml_w_in", [r(128 * b, 128) for b in range(16)], DM)
    t_blocks("ml_w_in", [r(2048 + 512 * n, 512) for n in range(4)], DM)
    t_blocks("ml_w_in", [r(4096 + 128 * b, 128) for b in range(16)], DM)
    t_blocks("ml_w_in", [r(6160 + 128 * b, 128) for b in range(16)], DM)
    t_blocks("ml_w_out", [r(128 * b, 128) for b in range(16)], DM)

    t_blocks("w_in_2", [r(64 * i, 64) + r(64 * (4 + i), 64) for i in range(4)], DM)
    kv = 512
    t_blocks("w_in_2", [r(kv + 128 * i, 128) for i in (0, 1, 2, 4)], DM)
    t_blocks("w_in_2", [r(kv + 128 * 3, 128) + r(kv + 128 * 5, 128) + r(1280, 24)], DM)
    for i in range(2):
        for l in range(32):
            tiles.append(("cmp_w1_2", i, [l], "bd"))
    tiles.append(("cmp_w2_2", 0, [0], "bd"))
    tiles.append(("cmp_w2_2", 1, [0], "bd"))
    b0 = 1304
    t_blocks("w_in_2", [r(b0 + 128 * b, 128) for b in range(12)], DM)
    c0 = b0 + 1536
    t_blocks("w_in_2", [r(c0 + 128 * b, 128) for b in range(4)], DM)
    t_blocks("w_in_2", [r(c0 + 512, 512)], DM)
    d0 = c0 + 1024
    t_blocks("w_in_2", [r(d0 + 128 * b, 128) for b in range(8)], DM)
    t_blocks("w_in_2", [r(d0 + 1024, 512)], DM)
    t_blocks("w_out_2", [r(128 * b, 128) for b in range(16)], DM, "mix")
    for b in range(FFN_BLOCKS):
        t_blocks("w_ffn_gate_2", [r(128 * b, 128)], DM)
        t_blocks("w_ffn_up_2", [r(128 * b, 128)], DM)
    t_blocks("w_ffn_down_2", [r(128 * b, 128) for b in range(16)], 128 * FFN_BLOCKS)
    return tiles


def tile_width(t):
    return 128 if t[3] == "bd" else len(t[2])


def pack_tiles(tiles):
    places, u, c = [], 0, 0
    for t in tiles:
        w = tile_width(t)
        if c + w > UCOLS:
            u, c = u + 1, 0
        places.append((u, c))
        c += w
    return places, u + 1


def mix_rows():
    rows = []
    for i in range(4):
        rows += list(range(64 * i, 64 * i + 64)) + list(range(64 * (4 + i), 64 * (4 + i) + 64))
    return np.array(rows + list(range(512, 2048)))


PCOL = {}
_n = 0
for _name, _w in [("q_norm", 4), ("kv_norm", 4), ("ln_w", 32), ("ln_b", 32), ("conv_w", 64), ("conv_b", 16),
                  ("head_norm", 16), ("norm_mix", 16), ("norm_ffn", 16), ("q_gain", 1), ("k_gain", 1),
                  ("cmp_pos", 64), ("conv2", 12), ("group_gain", 16), ("ib", 1), ("fb", 1), ("table", 8),
                  ("sgu_w", 1024), ("sgu_b", 512)]:
    PCOL[_name] = (_n, _w)
    _n += _w
NP = _n
CCOL = {}
_n = 0
for _name, _w in [("ident", 128), ("bones", 128), ("U", 128), ("mC", 256), ("mS", 384), ("tril", 128),
                  ("onehot", 383), ("negm", 383), ("E", 1024), ("R12", 256), ("u", 128), ("v", 128),
                  ("invf", 1), ("rowv", 1), ("ones", 128), ("J", 128), ("eps", 4)]:
    CCOL[_name] = (_n, _w)
    _n += _w
NC_ = _n


def rel_bucket(n):
    n = np.maximum(n, 0)
    nf = np.maximum(n, 1).astype(np.float32)
    large = 16 + (np.log(nf / np.float32(16)) / np.float32(np.log(64.0)) * np.float32(16)).astype(np.int32)
    return np.where(n < 16, n, np.minimum(large, 31))


def constants():
    c = np.zeros((128, NC_), np.float32)

    def put(name, a):
        a = np.asarray(a, np.float32)
        o, w = CCOL[name]
        c[:a.shape[0], o:o + a.shape[1]] = a

    i = np.arange(128)
    put("ident", np.eye(128))
    put("bones", (i[:, None] // 64) == (i[None, :] // 64))
    put("U", i[:, None] > i[None, :])
    put("mC", np.concatenate([np.where(i[:, None] <= i[None, :], 0.0, NEG), np.zeros((128, 128))], 1))
    strict = (i[:, None] < i[None, :]) * 1.0
    put("mS", np.concatenate([strict, np.ones((128, 128)), strict], 1))
    put("tril", i[:, None] <= i[None, :])
    dist = 255 - np.arange(383)
    hot = (np.arange(32)[:, None] == rel_bucket(dist)[None, :]) & (dist >= 0)[None, :]
    put("onehot", hot)
    put("negm", np.where(dist >= 0, 0.0, NEG)[None, :].repeat(8, 0))
    put("E", np.repeat(np.eye(8), 128, axis=1))
    r12 = np.zeros((64, 256))
    for m in range(128):
        r12[m % 32, m] = 1.0
        r12[32 + m % 32, 128 + m] = 1.0
    put("R12", r12)
    put("u", (i < 64)[None, :])
    put("v", np.where(i >= 64, NEG, 0.0)[None, :])
    f = (np.float64(10000.0) ** (-np.arange(0, 64, 2, dtype=np.float64) / 64)).astype(np.float32)
    put("invf", np.tile(f, 4)[:, None])
    put("rowv", (i >= 31)[:, None])
    put("ones", np.ones((128, 128)))
    put("J", np.eye(128)[::-1])
    put("eps", np.tile([[1e-6, 1e-5, np.pi / 2, 0.0]], (128, 1)))
    return c


class Queue:

    def __init__(self, eng, sem):
        self.eng, self.sem, self.n, self.seen = eng, sem, 0, {}

    def wait(self, *toks):
        for t in toks:
            if t is None:
                continue
            if isinstance(t, list):
                self.wait(*t)
                continue
            s, v = t
            if self.seen.get(id(s), 0) < v:
                self.eng.wait_ge(s, v)
                self.seen[id(s)] = v

    def mark(self, ins):
        ins.then_inc(self.sem, 1)
        self.n += 1
        return (self.sem, self.n)

    def last(self):
        return (self.sem, self.n) if self.n else None


def build(nc, dr, out, dumps):
    ctx = ExitStack()
    with ctx:
        def sb(name, cols, dt=F32, rows=128):
            return ctx.enter_context(nc.sbuf_tensor(name, [rows, cols], dt))

        def sem(name):
            return ctx.enter_context(nc.semaphore(name))

        R = [sb(f"R{i}", 4096) for i in range(8)]
        ring = sb("ring", NSLOT * UCOLS)
        pv = sb("pv", NP)
        cst = sb("cst", NC_)
        posi = sb("posi", T, I32)
        small = sb("small", 320)
        bank = [ctx.enter_context(nc.psum_tensor(f"bank{i}", [128, 512], F32)) for i in range(8)]

        PE = Queue(nc.tensor, sem("s_pe"))
        DV = Queue(nc.vector, sem("s_dve"))
        AC = Queue(nc.scalar, sem("s_act"))
        SP = Queue(nc.sync, sem("s_sp"))
        s_slot = [sem(f"s_slot{i}") for i in range(NSLOT)]
        s_cst, s_pv, s_pos, s_x, s_rv, s_bt, s_out = (sem(n) for n in
                                                      ("s_cst", "s_pv", "s_pos", "s_x", "s_rv", "s_bt", "s_out"))

        def V(name, *a, w=(), **k):
            DV.wait(DV.last(), *w)
            return DV.mark(vec[name](*a, **k))

        def A(out_, in_, func, w=(), **k):
            AC.wait(AC.last(), *w)
            return AC.mark(nc.scalar.activation(out_, in_, func, **k))

        vec = {"ts": nc.vector.tensor_scalar, "tt": nc.vector.tensor_tensor,
                          "stt": nc.vector.scalar_tensor_tensor, "copy": nc.vector.tensor_copy,
                          "red": nc.vector.tensor_reduce, "recip": nc.vector.reciprocal,
                          "memset": nc.vector.memset, "scan": nc.vector.tensor_tensor_scan,
                          "bns": nc.vector.bn_stats, "bna": nc.vector.bn_aggr}

        def mm(o, lhsT, rhs, start, stop):
            return nc.tensor.matmul(o, lhsT, rhs, start=start, stop=stop)

        def P(name, rows=128):
            o, w = PCOL[name]
            return pv[0:rows, o:o + w]

        def C(name, rows=128):
            o, w = CCOL[name]
            return cst[0:rows, o:o + w]

        def blk(t, i, n=1):
            return t[:, i * T:(i + n) * T]

        nc.sync.dma_start(R[0][:, :], dr["x"][:, :]).then_inc(s_x, 16)
        nc.sync.dma_start(cst[:, :], dr["cst"][:, :]).then_inc(s_cst, 16)
        nc.scalar.dma_start(pv[:, :], dr["pv"][:, :]).then_inc(s_pv, 16)
        nc.scalar.dma_start(posi[:, :], dr["pos"][0:1, :].broadcast_to([128, T])).then_inc(s_pos, 16)
        t_x, t_cst, t_pv, t_pos = (s_x, 16), (s_cst, 16), (s_pv, 16), (s_pos, 16)

        tiles = weight_tiles()
        places, n_units = pack_tiles(tiles)
        last_of = {}
        for i, (u, c) in enumerate(places):
            last_of[u] = i
        pos_ = [0]

        def load(u, freed=None):
            SP.wait(freed)
            nc.sync.dma_start(ring[:, (u % NSLOT) * UCOLS:(u % NSLOT + 1) * UCOLS],
                              dr["W"][u]).then_inc(s_slot[u % NSLOT], 16)

        for u in range(NSLOT):
            load(u)

        def take():
            i = pos_[0]
            pos_[0] += 1
            u, c = places[i]
            PE.wait((s_slot[u % NSLOT], 16 * (u // NSLOT + 1)))
            w = tile_width(tiles[i])
            return ring[:, (u % NSLOT) * UCOLS + c:(u % NSLOT) * UCOLS + c + w]

        def used(ins):
            i = pos_[0] - 1
            u = places[i][0]
            if last_of[u] == i:
                t = PE.mark(ins)
                if u + NSLOT < n_units:
                    load(u + NSLOT, t)
                return t
            return None

        free = {i: None for i in range(8)}
        BIG = [0, 1, 2]
        turn = [0]

        def next_bank():
            b = BIG[turn[0] % len(BIG)]
            turn[0] += 1
            PE.wait(free[b])
            return b

        def proj(n_blocks, rhs, nk, evac, w=(), width=128):
            PE.wait(*w)
            for n0 in range(0, n_blocks, 2):
                b = next_bank()
                cnt = min(2, n_blocks - n0)
                for n in range(cnt):
                    for k in range(nk):
                        wt = take()
                        ins = mm(bank[b][0:width, n * T:(n + 1) * T], wt, rhs(k), k == 0, k == nk - 1)
                        tu = used(ins)
                tk = tu or PE.mark(ins)
                free[b] = evac(n0, cnt, bank[b], tk)

        def proj_tm(n_blocks, lhs, nk, width, evac, w=()):
            PE.wait(*w)
            for n in range(n_blocks):
                bs = [next_bank(), next_bank()]
                for k in range(nk):
                    wt = take()
                    for tb in range(2):
                        ins = mm(bank[bs[tb]][:, 0:width], lhs(k)[:, tb * 128:(tb + 1) * 128], wt,
                                 k == 0, k == nk - 1)
                    tu = used(ins)
                tk = tu or PE.mark(ins)
                for tb in range(2):
                    free[bs[tb]] = evac(n, tb, bank[bs[tb]], tk)

        ones = C("ones")
        ident = C("ident")

        def colsum(chunks, w=(), lhs=None, half=0, b=None):
            if b is None:
                b = next_bank()
            PE.wait(*w)
            for k, c in enumerate(chunks):
                ins = mm(bank[b][:, half * T:(half + 1) * T], ones if lhs is None else lhs, c,
                         k == 0, k == len(chunks) - 1)
            return b, PE.mark(ins)

        def rstd(dst, src, n, eps_col, w=()):
            o = CCOL["eps"][0] + eps_col
            rows = dst.shape[0]
            A(dst, src, ACT.Ln, scale=1.0 / n, bias=cst[0:rows, o:o + 1], w=w)
            return A(dst, dst, ACT.Exp, scale=-0.5)

        dump_n = [0]

        def dump(name, ap, *w):
            if name in dumps:
                nc.scalar.wait_ge(DV.sem, DV.n)
                nc.scalar.wait_ge(AC.sem, AC.n)
                nc.scalar.dma_start(dumps[name], ap).then_inc(s_out, 16)
                dump_n[0] += 1
                nc.scalar.wait_ge(s_out, 16 * dump_n[0])
                DV.wait(AC.last())
                t = AC.mark(nc.scalar.activation(small[:, 319:320], cst[:, 0:1], ACT.Copy))
                DV.wait(t)
                PE.wait(t)

        def prev(d, i):
            return d[i] if i >= 0 else None

        def pipe(n, stages):
            for step in range(n + len(stages) - 1):
                for s in range(len(stages) - 1, -1, -1):
                    if 0 <= step - s < n:
                        stages[s](step - s)

        for q in (DV, AC, PE):
            q.wait(t_cst, t_pv)

        X = R[0]

        posf, ang, cos, sin, tmp = (R[6][:, 2560 + 256 * i:2560 + 256 * (i + 1)] for i in range(5))
        V("copy", posf, posi[:, :], w=[t_pos])
        o = CCOL["invf"][0]
        V("ts", ang, posf, cst[:, o:o + 1], None, ALU.mult)
        TWO_PI = 2 * np.pi
        P1 = float(np.float32(6.28125))
        P2 = float(np.float32(TWO_PI - 6.28125).view(np.uint32).__and__(np.uint32(0xFFFFF000)).view(np.float32))
        P3 = float(np.float32(TWO_PI - P1 - P2))
        MAGIC = 12582912.0

        def reduce_angle():
            V("ts", tmp, ang, float(1.0 / TWO_PI), MAGIC, ALU.mult, ALU.add)
            V("ts", tmp, tmp, MAGIC, None, ALU.subtract)
            for p in (P1, P2, P3):
                V("stt", ang, tmp, -p, ang, ALU.mult, ALU.add)

        reduce_angle()
        LIM = 3.1415925
        V("ts", tmp, ang, LIM, -LIM, ALU.min, ALU.max)
        tsin = A(sin, tmp, ACT.Sin, w=[DV.last()])
        V("stt", ang, ang, -1.0, ang, ALU.mult, ALU.min)
        V("ts", ang, ang, float(np.pi / 2), None, ALU.add)
        tcos = A(cos, ang, ACT.Sin, w=[DV.last()])
        DV.wait(tcos)

        cq, ckv = R[5][:, 0:1024], R[5][:, 1024:2048]
        qr = [R[5][:, 2048:3072], R[5][:, 3072:4096]]
        krm = R[6][:, 0:2048]
        sq = R[7][:, 0:1024]
        krT = R[7][0:64, 1024:1280]
        kr12 = R[7][:, 1280:1792]
        rt = [R[7][:, 1792:2048], R[7][:, 2048:2304]]
        rsx = R[7][:, 2304:2560]
        rsy = R[7][:, 2560:2816]
        xk = lambda k: blk(X, k)

        def ev_c(n0, cnt, ps, tk):
            if n0 < 4:
                dst = cq[:, n0 * T:(n0 + 2) * T]
            elif n0 < 8:
                dst = ckv[:, (n0 - 4) * T:(n0 - 2) * T]
            return V("copy", dst, ps[:, 0:512], w=[tk])

        proj(8, xk, 16, ev_c, w=[t_x])
        t_c = DV.last()

        def ev_kr(n0, cnt, ps, tk):
            return V("copy", krT, ps[0:64, 0:T], w=[tk])

        proj(1, xk, 16, ev_kr, width=64)

        for src, rs, g in ((cq, rsx, "q_norm"), (ckv, rsy, "kv_norm")):
            tsq = A(sq, src, ACT.Square, w=[t_c, PE.last()])
            b, tk = colsum([sq[:, k * T:(k + 1) * T] for k in range(4)], w=[tsq])
            free[b] = t = rstd(rs, bank[b][:, 0:T], 512, 0, w=[tk])
            for k in range(4):
                V("stt", src[:, k * T:(k + 1) * T], src[:, k * T:(k + 1) * T], P(g)[:, k:k + 1], rs,
                  ALU.mult, ALU.mult, w=[t])
        t_cn = DV.last()

        b = next_bank()
        PE.wait(t_cn)
        mm(bank[b][:, 0:T], C("R12", 64)[:, 0:128], krT, True, True)
        tk = PE.mark(mm(bank[b][:, T:2 * T], C("R12", 64)[:, 128:256], krT, True, True))
        free[b] = V("copy", kr12, bank[b][:, :], w=[tk])
        V("memset", krm, 0.0)

        def rotate(x1, x2, o1, o2):
            V("tt", rt[0], x1, cos, ALU.mult)
            V("tt", rt[1], x2, sin, ALU.mult)
            V("tt", o1, rt[0], rt[1], ALU.subtract)
            V("tt", rt[0], x1, sin, ALU.mult)
            V("tt", rt[1], x2, cos, ALU.mult)
            V("tt", o2, rt[0], rt[1], ALU.add)

        ko = R[7][:, 2816:3328]
        rotate(kr12[:, 0:T], kr12[:, T:2 * T], ko[:, 0:T], ko[:, T:2 * T])
        for i in range(4):
            for half in range(2):
                V("copy", krm[32 * i:32 * i + 32, (2 * i + half) * T:(2 * i + half + 1) * T],
                  ko[32 * i:32 * i + 32, half * T:(half + 1) * T])
        t_krm = DV.last()

        qn, kn, Vt, Z = R[1], R[2], R[3], R[4]
        cqk = lambda k: cq[:, k * T:(k + 1) * T]
        ckvk = lambda k: ckv[:, k * T:(k + 1) * T]

        def ev_qb(n0, cnt, ps, tk):
            if n0 < 16:
                return A(blk(qn, n0, 2), ps[:, :], ACT.Copy, w=[tk])
            j = n0 - 16
            dst = qr[j // 4][:, (j % 4) * T:(j % 4 + 2) * T]
            return A(dst, ps[:, :], ACT.Copy, w=[tk])

        proj(24, cqk, 4, ev_qb, w=[t_cn])
        DV.wait(AC.last())
        for g in range(4):
            s = slice(g * T, (g + 1) * T)
            x1, x2 = qr[0][:, s], qr[1][:, s]
            V("tt", rt[0], x2, sin, ALU.mult)
            V("tt", rt[1], x1, sin, ALU.mult)
            V("tt", x1, x1, cos, ALU.mult)
            V("tt", x1, x1, rt[0], ALU.subtract)
            V("tt", x2, x2, cos, ALU.mult)
            V("tt", x2, x2, rt[1], ALU.add)
        t_rope = DV.last()

        proj(16, ckvk, 4, lambda n0, cnt, ps, tk: A(blk(kn, n0, 2), ps[:, :], ACT.Copy, w=[tk]))
        proj_tm(4, ckvk, 4, 512,
                lambda n, tb, ps, tk: A(Vt[:, tb * 2048 + n * 512:tb * 2048 + (n + 1) * 512], ps[:, :],
                                        ACT.Copy, w=[tk]))
        proj(16, xk, 16, lambda n0, cnt, ps, tk: A(blk(Z, n0, 2), ps[:, :], ACT.Silu, w=[tk]))
        t_z = AC.last()

        dump("cq", cq)
        dump("qn", qn[:, :])
        dump("qr", R[5][:, 2048:4096])
        dump("krm", krm)
        dump("V", Vt[:, :])
        dump("Z", Z[:, :])

        sc = float(192 ** -0.5)
        Pm = [R[7][:, 384 * i:384 * (i + 1)] for i in range(2)]
        PT = [R[7][:, 768 + 384 * i:768 + 384 * (i + 1)] for i in range(2)]
        mx = [small[:, 8 * i:8 * i + 2] for i in range(2)]
        ss = [small[:, 16 + 8 * i:16 + 8 * i + 2] for i in range(2)]
        tk_s, tk_e, tk_r, tk_t, tk_c, tk_o, tk_n = {}, {}, {}, {}, {}, {}, {}

        def st_scores(h):
            S = bank[3 + h % 2]
            PE.wait(free[3 + h % 2], t_krm, t_rope, t_z)
            g, i = h // 4, h % 4
            a = [qn[:, h * T:(h + 1) * T], qr[0][:, g * T:(g + 1) * T], qr[1][:, g * T:(g + 1) * T]]
            k = [kn[:, h * T:(h + 1) * T], krm[:, 2 * i * T:(2 * i + 1) * T], krm[:, (2 * i + 1) * T:(2 * i + 2) * T]]
            for j in range(3):
                mm(S[:, 0:128], a[j][:, 0:128], k[j][:, 0:128], j == 0, False)
            mm(S[:, 0:128], C("u", 1), C("v", 1), False, True)
            for j in range(3):
                mm(S[:, 128:384], a[j][:, 128:256], k[j], j == 0, False)
            tk_s[h] = PE.mark(mm(S[:, 256:384], C("u", 1), C("v", 1), False, True))

        def st_max(h):
            S, m = bank[3 + h % 2], mx[h % 2]
            V("red", m[:, 0:1], S[:, 0:128], AX, ALU.max, w=[tk_s[h], prev(tk_e, h - 2)])
            V("red", m[:, 1:2], S[:, 128:384], AX, ALU.max)
            tk_n[h] = V("ts", m, m, -sc, None, ALU.mult)

        def st_exp(h):
            S, m = bank[3 + h % 2], mx[h % 2]
            A(Pm[h % 2][:, 0:128], S[:, 0:128], ACT.Exp, scale=sc, bias=m[:, 0:1], accum_out=ss[h % 2][:, 0:1],
              w=[tk_n[h], prev(tk_t, h - 2), prev(tk_r, h - 2)])
            tk_e[h] = A(Pm[h % 2][:, 128:384], S[:, 128:384], ACT.Exp, scale=sc, bias=m[:, 1:2],
                        accum_out=ss[h % 2][:, 1:2])
            free[3 + h % 2] = tk_e[h]

        def st_norm(h):
            s, p = ss[h % 2], Pm[h % 2]
            V("recip", s, s, w=[tk_e[h]])
            V("ts", p[:, 0:128], p[:, 0:128], s[:, 0:1], None, ALU.mult)
            tk_r[h] = V("ts", p[:, 128:384], p[:, 128:384], s[:, 1:2], None, ALU.mult)

        def st_turn(h):
            b, p = bank[5 + h % 2], Pm[h % 2]
            PE.wait(free[5 + h % 2], tk_r[h])
            for j in range(3):
                ins = nc.tensor.transpose(b[:, 128 * j:128 * j + 128], p[:, 128 * j:128 * j + 128], ident)
            tk_t[h] = PE.mark(ins)

        def st_copy(h):
            tk_c[h] = free[5 + h % 2] = A(PT[h % 2], bank[5 + h % 2][:, 0:384], ACT.Copy, w=[tk_t[h], prev(tk_o, h - 2)])

        def st_pv(h):
            PE.wait(tk_c[h], free[7])
            mm(bank[7][:, 0:T], Vt[:, h * 128:(h + 1) * 128], PT[h % 2][:, 0:256], True, False)
            tk_o[h] = PE.mark(mm(bank[7][:, 128:T], Vt[:, 2048 + h * 128:2048 + (h + 1) * 128],
                                 PT[h % 2][:, 256:384], False, True))

        def st_gate(h):
            free[7] = V("tt", blk(Z, h), bank[7][:, 0:T], blk(Z, h), ALU.mult, w=[tk_o[h]])

        AC.wait(DV.last(), PE.last())
        DV.wait(AC.last(), PE.last())
        pipe(16, [st_scores, st_max, st_exp, st_norm, st_turn, st_copy, st_pv, st_gate])
        dump("G", Z[:, :])

        def layer_norm(layer, D, SQ):
            b, tk = colsum([blk(D, k) for k in range(16)], w=[DV.last()])
            mu = small[:, 64:320]
            V("ts", mu, bank[b][:, 0:T], -1.0 / DM, None, ALU.mult, w=[tk])
            free[b] = DV.last()
            toks = []
            for q in range(4):
                d4 = D[:, q * 1024:(q + 1) * 1024]
                t = V("tt", d4.rearrange("p (c t) -> p c t", c=4), d4.rearrange("p (c t) -> p c t", c=4),
                      mu.rearrange("p (o t) -> p o t", o=1).broadcast_to([128, 4, T]), ALU.add, w=[])
                toks.append(A(SQ[:, q * 1024:(q + 1) * 1024], d4, ACT.Square, w=[t]))
            b = next_bank()
            for k in range(16):
                PE.wait(toks[k // 4])
                ins = mm(bank[b][:, 0:T], ones, blk(SQ, k), k == 0, k == 15)
            tk = PE.mark(ins)
            t = free[b] = rstd(mu, bank[b][:, 0:T], DM, 0, w=[tk])
            ow, ob = PCOL["ln_w"][0] + 16 * layer, PCOL["ln_b"][0] + 16 * layer
            for k in range(16):
                t2 = V("stt", blk(D, k), blk(D, k), pv[:, ow + k:ow + k + 1], mu, ALU.mult, ALU.mult, w=[t])
                t3 = A(blk(X, k), blk(D, k), ACT.Identity, bias=pv[:, ob + k:ob + k + 1], w=[t2])
            return t3

        def ev_res(D):
            def ev(n0, cnt, ps, tk):
                return V("stt", blk(D, n0, 2), blk(X, n0, 2), ALPHA, ps[:, :], ALU.mult, ALU.add, w=[tk])
            return ev

        proj(16, lambda k: blk(Z, k), 16, ev_res(R[1]), w=[DV.last()])
        t_x1 = layer_norm(0, R[1], R[2])
        dump("x1", X[:, :])

        QK, Vm, G, H = R[1], R[2], R[3], R[4]
        gs = R[5]
        fr = lambda i: gs[0:8, i * T:(i + 1) * T]
        gi = next_bank()
        PE.wait(t_x1)
        for half in range(2):
            for k in range(16):
                wt = take()
                ins = mm(bank[gi][0:8, half * T:(half + 1) * T], wt, blk(X, k), k == 0, k == 15)
                tu = used(ins)
        tk = tu or PE.mark(ins)
        ip, fp, ab, e1, lf, Fc, ai, Mx, one8 = (gs[0:8, i * T:(i + 1) * T] for i in range(9))
        GR = gs[0:8, 9 * T:11 * T]
        oib, ofb = PCOL["ib"][0], PCOL["fb"][0]
        V("ts", ip, bank[gi][0:8, 0:T], pv[0:8, oib:oib + 1], None, ALU.add, w=[tk])
        V("ts", fp, bank[gi][0:8, T:2 * T], pv[0:8, ofb:ofb + 1], None, ALU.add)
        free[gi] = DV.last()
        V("stt", ab, fp, -1.0, fp, ALU.mult, ALU.min)
        t = A(e1, ab, ACT.Exp, w=[DV.last()])
        t = A(e1, e1, ACT.Ln, bias=cst[0:8, CCOL["ones"][0]:CCOL["ones"][0] + 1])
        V("ts", lf, fp, 0.0, None, ALU.min)
        V("tt", lf, lf, e1, ALU.subtract, w=[t])
        V("memset", one8, 1.0)
        V("scan", Fc, one8, lf, 0.0, ALU.mult, ALU.add)
        V("tt", ai, ip, Fc, ALU.subtract)
        V("scan", Mx, ai, ai, 0.0, ALU.max, ALU.max)
        V("ts", GR[:, 0:T], Mx, -1.0, None, ALU.mult)
        t_gr = V("tt", GR[:, T:2 * T], GR[:, 0:T], Fc, ALU.subtract)
        b = next_bank()
        PE.wait(t_gr)
        nc.tensor.transpose(bank[b][:, 0:8], ai[:, 0:128], ident[0:8, 0:8])
        tk = PE.mark(nc.tensor.transpose(bank[b][:, 8:16], ai[:, 128:256], ident[0:8, 0:8]))
        aT = small[:, 0:16]
        t_aT = free[b] = V("copy", aT, bank[b][:, 0:16], w=[tk])

        ocw, ocb = PCOL["conv_w"][0], PCOL["conv_b"][0]

        def ev_conv(n0, cnt, ps, tk):
            for j in range(2):
                n = n0 + j
                y, p = blk(QK, n), ps[:, j * T:(j + 1) * T]
                cw = lambda i: pv[:, ocw + 16 * i + n:ocw + 16 * i + n + 1]
                V("ts", y, p, cw(3), pv[:, ocb + n:ocb + n + 1], ALU.mult, ALU.add, w=[tk])
                for s in (1, 2, 3):
                    V("stt", y[:, s:T], p[:, 0:T - s], cw(3 - s), y[:, s:T], ALU.mult, ALU.add)
            t = DV.last()
            A(blk(QK, n0, 2), blk(QK, n0, 2), ACT.Silu, w=[t])
            return t

        proj(16, xk, 16, ev_conv)
        t_qk = AC.last()
        proj_tm(4, xk, 16, 512,
                lambda n, tb, ps, tk: V("copy", Vm[:, tb * 2048 + n * 512:tb * 2048 + (n + 1) * 512], ps[:, :],
                                        w=[tk]))
        proj(16, xk, 16, lambda n0, cnt, ps, tk: A(blk(G, n0, 2), ps[:, :], ACT.Sigmoid, w=[tk]))
        zt = [R[6][:, 0:512], R[6][:, 512:1024]]
        tzv = {}

        def ev_z(n0, cnt, ps, tk):
            t = A(zt[n0 // 2 % 2], ps[:, :], ACT.Silu, w=[tk, prev(tzv, n0 // 2 - 2)])
            tzv[n0 // 2] = V("tt", blk(G, n0, 2), blk(G, n0, 2), zt[n0 // 2 % 2], ALU.mult, w=[t])
            return t

        proj(16, xk, 16, ev_z)
        dump("QK", QK[:, :])
        dump("Vm", Vm[:, :])
        dump("Gm", G[:, :])

        dk = float(128 ** -0.5)
        Dt = [R[6][:, 1024 + 384 * i:1024 + 384 * (i + 1)] for i in range(2)]
        At = [R[6][:, 1792 + 384 * i:1792 + 384 * (i + 1)] for i in range(2)]
        cap = [R[6][:, 2560 + 256 * i:2560 + 256 * (i + 1)] for i in range(4)]
        rcp = [R[6][:, 3584 + 256 * i:3584 + 256 * (i + 1)] for i in range(2)]
        hv = [R[7][:, 512 * i:512 * (i + 1)] for i in range(4)]
        sqh = [R[7][:, 2048 + 512 * i:2048 + 512 * (i + 1)] for i in range(2)]
        rsh = [R[7][:, 3072 + 256 * i:3072 + 256 * (i + 1)] for i in range(2)]
        t1, t2, t3, t4, t5, t6, t7, t8 = ({} for _ in range(8))
        mC = C("mC")

        def m0(h):
            br, bs = h % 2, 2 + h % 2
            PE.wait(free[br], free[bs], t_qk, t_gr)
            mm(bank[br][:, 0:512], C("E", 8)[:, 128 * h:128 * (h + 1)], GR, True, True)
            q, k = blk(QK, h), blk(QK, 8 + h)
            mm(bank[bs][:, 0:256], k[:, 0:128], q, True, True)
            t1[h] = PE.mark(mm(bank[bs][:, 256:384], k[:, 128:256], q[:, 128:256], True, True))

        def m1(h):
            D, br = Dt[h % 2], h % 2
            V("tt", D[:, 0:256], bank[br][:, 0:256], mC, ALU.add, w=[t1[h], prev(t3, h - 2)])
            t2[h] = V("tt", D[:, 256:384], bank[br][:, 128:256], mC[:, 0:128], ALU.add)
            A(D[:, 0:256], D[:, 0:256], ACT.Exp, bias=aT[:, h:h + 1], w=[t2[h], t_aT])
            A(D[:, 256:384], D[:, 256:384], ACT.Exp, bias=aT[:, 8 + h:9 + h])
            t4[h] = A(cap[h % 4], bank[br][:, 256:512], ACT.Exp, w=[prev(t6, h - 4)])
            free[br] = t4[h]

        def m3(h):
            bs = 2 + h % 2
            t3[h] = V("stt", At[h % 2], bank[bs][:, 0:384], dk, Dt[h % 2], ALU.mult, ALU.mult,
                      w=[t4[h], prev(t5, h - 2)])
            free[bs] = t3[h]

        def m4(h):
            N, a = bank[5 + h % 2], At[h % 2]
            PE.wait(t3[h], free[5 + h % 2], free[7])
            for c in range(2):
                vo = h * 256 + c * 128
                mm(N[:, c * T:(c + 1) * T], Vm[:, vo:vo + 128], a[:, 0:256], True, False)
                mm(N[:, c * T + 128:(c + 1) * T], Vm[:, 2048 + vo:2048 + vo + 128], a[:, 256:384], False, True)
            mm(bank[7][:, 0:T], ones, a[:, 0:256], True, False)
            t5[h] = PE.mark(mm(bank[7][:, 128:T], ones, a[:, 256:384], False, True))

        def m5(h):
            r = rcp[h % 2]
            V("tt", r, bank[7][:, 0:T], cap[h % 4], ALU.max, w=[t5[h]])
            t6[h] = free[7] = V("stt", r, bank[7][:, 0:T], -1.0, r, ALU.mult, ALU.max)
            V("recip", r, r)
            free[5 + h % 2] = V("tt", hv[h % 4].rearrange("p (c t) -> p c t", c=2),
                                bank[5 + h % 2][:, :].rearrange("p (c t) -> p c t", c=2),
                                r.rearrange("p (o t) -> p o t", o=1).broadcast_to([128, 2, T]), ALU.mult)
            t7[h] = A(sqh[h % 2], hv[h % 4], ACT.Square, w=[DV.last(), prev(t8, h - 2)])

        def m6(h):
            PE.wait(t7[h], free[4])
            mm(bank[4][:, 0:T], ones, sqh[h % 2][:, 0:T], True, False)
            t8[h] = PE.mark(mm(bank[4][:, 0:T], ones, sqh[h % 2][:, T:2 * T], False, True))

        def m7(h):
            t = free[4] = rstd(rsh[h % 2], bank[4][:, 0:T], 256, 0, w=[t8[h], DV.last()])
            on = PCOL["head_norm"][0] + 2 * h
            for c in range(2):
                V("stt", blk(H, 2 * h + c), hv[h % 4][:, c * T:(c + 1) * T], pv[:, on + c:on + c + 1], rsh[h % 2],
                  ALU.mult, ALU.mult, w=[t])
            V("tt", blk(H, 2 * h, 2), blk(H, 2 * h, 2), blk(G, 2 * h, 2), ALU.mult)

        AC.wait(DV.last(), PE.last())
        DV.wait(AC.last(), PE.last())
        pipe(8, [m0, m1, m3, m4, m5, m6, m7])
        dump("H", H[:, :])

        proj(16, lambda k: blk(H, k), 16, ev_res(R[1]), w=[DV.last()])
        t_x2 = layer_norm(1, R[1], R[2])
        dump("x2", X[:, :])

        def rms_all(gain, D, SQ, t_in):
            toks = []
            for q in range(4):
                toks.append(A(SQ[:, q * 1024:(q + 1) * 1024], X[:, q * 1024:(q + 1) * 1024], ACT.Square, w=[t_in]))
            b = next_bank()
            for k in range(16):
                PE.wait(toks[k // 4])
                ins = mm(bank[b][:, 0:T], ones, blk(SQ, k), k == 0, k == 15)
            rs = small[:, 64:320]
            t = free[b] = rstd(rs, bank[b][:, 0:T], DM, 0, w=[PE.mark(ins)])
            og = PCOL[gain][0]
            for k in range(16):
                V("stt", blk(D, k), blk(X, k), pv[:, og + k:og + k + 1], rs, ALU.mult, ALU.mult, w=[t])
            return DV.last()

        HX = R[1]
        t_h = rms_all("norm_mix", HX, R[2], t_x2)
        hk = lambda k: blk(HX, k)

        rv = R[3][0:8, 0:383]
        b = next_bank()
        ins = mm(bank[b][0:8, 0:383], P("table", 32), C("onehot", 32), True, True)
        t = free[b] = V("tt", rv, bank[b][0:8, 0:383], C("negm", 8), ALU.add, w=[PE.mark(ins)])
        AC.wait(t)
        nc.scalar.dma_start(dr["rv"][:, :], rv).then_inc(s_rv, 16)
        nc.scalar.wait_ge(s_rv, 16)
        BT = R[4][:, 0:2048]
        band = bass.AP(dr["rv"].tensor, 0, [[1, 128], [383, 8], [1, 256]])
        BR = R[6][:, 0:2048]
        nc.scalar.dma_start(BR.rearrange("p (h k) -> p h k", h=8), band).then_inc(s_bt, 16)
        DV.wait((s_rv, 16))

        RAW, QZ = R[2][:, 0:2048], R[2][:, 2048:4096]
        VSW, DVt, CV = R[3][:, 0:512], R[3][:, 512:1536], R[3][:, 1536:2560]
        GA = R[3][:, 2560:2608]
        GX = R[3][:, 2608:2656]
        kcr = R[3][:, 2688:3648]
        sgt = R[4][:, 2048:3072]
        U_ = R[4][:, 3072:4096]
        DQ, DK = R[5][:, 0:2048], R[5][:, 2048:3072]
        RS5 = R[5][:, 3072:4096]
        MIX = R[6]
        WK = R[7]

        PE.wait((s_bt, 16))
        for i in range(4):
            b = next_bank()
            tk = PE.mark(mm(bank[b][:, :], C("J"), BR[:, 512 * i:512 * (i + 1)], True, True))
            free[b] = V("copy", BT[:, 512 * i:512 * (i + 1)], bank[b][:, :], w=[tk])
        proj(8, hk, 16, lambda n0, cnt, ps, tk: A(RAW[:, n0 * T:(n0 + 2) * T], ps[:, :], ACT.Copy, w=[tk]), w=[t_h])
        t_raw = AC.last()

        def ev_vsw(n, tb, ps, tk):
            A(VSW[:, tb * 256:(tb + 1) * 256], ps[:, 0:256], ACT.Copy, w=[tk])
            return A(GA[:, tb * 24:(tb + 1) * 24], ps[:, 256:280], ACT.Sigmoid)

        proj_tm(1, hk, 16, 280, ev_vsw)
        DV.wait(AC.last())
        for tb, c in ((1, 0), (0, 2)):
            for j in range(2):
                V("copy", GX.rearrange("p (h s) -> p h s", s=6)[:, :, c + j],
                  GA[:, tb * 24:(tb + 1) * 24].rearrange("p (h s) -> p h s", s=3)[:, :, 1 + j])
        V("copy", GX.rearrange("p (h s) -> p h s", s=6)[:, :, 4], GA[:, 24:48].rearrange("p (h s) -> p h s", s=3)[:, :, 0])
        orv = CCOL["rowv"][0]
        V("ts", GX.rearrange("p (h s) -> p h s", s=6)[:, :, 5], GA[:, 0:24].rearrange("p (h s) -> p h s", s=3)[:, :, 0],
          cst[:, orv:orv + 1], None, ALU.mult)

        ksn, kwn = blk(RAW, 6), blk(RAW, 7)
        V("memset", QZ, 0.0)
        obones = C("bones")
        SQ6 = WK[:, 0:512]
        tt_ = None
        for pr in (0, 2, 6):
            t = A(SQ6, RAW[:, pr * T:(pr + 2) * T], ACT.Square, w=[tt_])
            b = next_bank()
            PE.wait(t)
            tt_ = PE.mark(mm(bank[b][:, :], obones, SQ6, True, True))
            rs = RS5[:, 0:512]
            t = free[b] = rstd(rs, bank[b][:, :], 64, 0, w=[tt_, DV.last()])
            for j in range(2):
                n = pr + j
                src = blk(RAW, n)
                if n < 4:
                    og = PCOL["q_gain"][0]
                    for g in range(2):
                        sl = slice(64 * g, 64 * g + 64)
                        V("stt", QZ[sl, (n + 4 * g) * T:(n + 4 * g + 1) * T], src[sl, :], pv[sl, og:og + 1],
                          rs[sl, j * T:(j + 1) * T], ALU.mult, ALU.mult, w=[t])
                else:
                    og = PCOL["k_gain"][0]
                    V("stt", src, src, pv[:, og:og + 1], rs[:, j * T:(j + 1) * T], ALU.mult, ALU.mult, w=[t])

        zb = [WK[:, 1024:1504], WK[:, 1536:2016]]
        for i in range(2):
            src = blk(RAW, 4 + i)
            win = bass.AP(src.tensor, src.offset, [list(src.ap[0]), [1, 32], [16, 15]])
            opos = PCOL["cmp_pos"][0] + 32 * i
            posb = pv[:, opos:opos + 32].rearrange("p (l o) -> p l o", o=1).broadcast_to([128, 32, 15])
            V("tt", zb[i].rearrange("p (l n) -> p l n", l=32), win, posb, ALU.add)
        t_zb = DV.last()
        b = next_bank()
        PE.wait(t_zb)
        for i in range(2):
            for l in range(32):
                ins = mm(bank[b][:, 16 * i:16 * i + 15], take(), zb[i][:, 15 * l:15 * l + 15], l == 0, l == 31)
                tu = used(ins)
        tk = tu or PE.mark(ins)
        ge = WK[:, 2048:2080]
        for i in range(2):
            A(ge[:, 16 * i:16 * i + 15], bank[b][:, 16 * i:16 * i + 15], ACT.Gelu_apprx_tanh, w=[tk])
        free[b] = t = AC.last()
        b = next_bank()
        PE.wait(t)
        used(mm(bank[b][:, 0:15], take(), ge[:, 0:15], True, True))
        ins = mm(bank[b][0:15, 128:256], ge[:, 16:31], take(), True, True)
        tk = used(ins) or PE.mark(ins)
        kcn, sqk = WK[:, 2080:2095], WK[:, 2096:2111]
        vc = WK[0:15, 2112:2240]
        V("copy", vc, bank[b][0:15, 128:256], w=[tk])
        V("copy", kcn, bank[b][:, 0:15])
        free[b] = DV.last()
        t = A(sqk, kcn, ACT.Square, w=[DV.last()])
        b = next_bank()
        PE.wait(t)
        tk = PE.mark(mm(bank[b][:, 0:15], obones, sqk, True, True))
        t = free[b] = rstd(sqk, bank[b][:, 0:15], 64, 0, w=[tk])
        og = PCOL["k_gain"][0]
        t_kc = V("stt", kcn, kcn, pv[:, og:og + 1], sqk, ALU.mult, ALU.mult, w=[t])
        dump("QZ", QZ)
        dump("RAW", RAW)

        bg, cg = R[5][:, 0:1024], R[5][:, 1024:2048]
        o2 = PCOL["conv2"][0]

        def ev_b(n0, cnt, ps, tk):
            if n0 < 8:
                d = (bg if n0 < 4 else cg)[:, (n0 % 4) * T:(n0 % 4 + 2) * T]
                return A(d, ps[:, :], ACT.Copy, w=[tk])
            j0 = n0 - 8
            z = cg[:, j0 * T:(j0 + 2) * T]
            r = V("tt", z, z, ps[:, :], ALU.mult, w=[tk, AC.last()])
            for j in (j0, j0 + 1):
                zz, y = cg[:, j * T:(j + 1) * T], blk(MIX, 4 + j)
                cw = lambda i: pv[:, o2 + 4 * i + j:o2 + 4 * i + j + 1]
                V("ts", y, zz, cw(2), None, ALU.mult)
                V("stt", y[:, 1:T], zz[:, 0:T - 1], cw(1), y[:, 1:T], ALU.mult, ALU.add)
                V("stt", y[:, 2:T], zz[:, 0:T - 2], cw(0), y[:, 2:T], ALU.mult, ALU.add)
                V("tt", y, y, bg[:, j * T:(j + 1) * T], ALU.mult)
            return r

        AC.wait(PE.last(), DV.last())
        DV.wait(AC.last())
        proj(12, hk, 16, ev_b)

        proj(4, hk, 16, lambda n0, cnt, ps, tk: A(U_[:, n0 * T:(n0 + 2) * T], ps[:, :], ACT.Gelu_apprx_tanh, w=[tk]))
        proj_tm(1, hk, 16, 512, lambda n, tb, ps, tk: A(CV[:, tb * 512:(tb + 1) * 512], ps[:, :],
                                                        ACT.Gelu_apprx_tanh, w=[tk]))
        t = AC.last()
        ost = 32
        for tb in range(2):
            st = small[:, ost + 16 * tb:ost + 16 * tb + 6]
            mv = small[:, ost + 16 * tb + 8:ost + 16 * tb + 10]
            v = CV[:, tb * 512:(tb + 1) * 512]
            V("bns", st, v, w=[t])
            V("bna", mv, st)
            rstd(mv[:, 1:2], mv[:, 1:2], 1, 1, w=[DV.last()])
            V("ts", v, v, mv[:, 0:1], mv[:, 1:2], ALU.subtract, ALU.mult, w=[AC.last()])
        osw, otr, osb = PCOL["sgu_w"][0], CCOL["tril"][0], PCOL["sgu_b"][0]
        sgw = pv[:, osw:osw + 1024]
        V("tt", sgw.rearrange("p (h q) -> p h q", h=8), sgw.rearrange("p (h q) -> p h q", h=8),
          cst[:, otr:otr + 128].rearrange("p (o q) -> p o q", o=1).broadcast_to([128, 8, 128]), ALU.mult)
        t = DV.last()
        for j in range(4):
            b = next_bank()
            PE.wait(t)
            for c in range(2):
                ins = mm(bank[b][:, c * 256:(c + 1) * 256], CV[:, c * 512 + j * 128:c * 512 + (j + 1) * 128],
                         sgw[:, j * 256:(j + 1) * 256], True, True)
            tk = PE.mark(ins)
            ps3 = bank[b][:, :].rearrange("p (c q) -> p c q", c=2)
            d3 = sgt[:, j * T:(j + 1) * T].rearrange("p (c q) -> p c q", c=2)
            for half in range(2):
                sl = slice(64 * half, 64 * half + 64)
                bias = pv[sl, osb + 128 * j:osb + 128 * (j + 1)].rearrange("p (o q) -> p o q", o=1)
                V("tt", d3[sl], ps3[sl, :, 128 * half:128 * half + 128], bias.broadcast_to([64, 2, 128]), ALU.add,
                  w=[tk])
            free[b] = DV.last()
            V("tt", blk(MIX, 8 + j), sgt[:, j * T:(j + 1) * T], U_[:, j * T:(j + 1) * T], ALU.mult)
        dump("MIXc", MIX[:, 1024:3072])

        V("memset", DQ, 0.0)

        def ev_d(n0, cnt, ps, tk):
            if n0 >= 4:
                return V("copy", DK[:, (n0 - 4) * T:(n0 - 2) * T], ps[:, :], w=[tk])
            for j in range(2):
                for half in range(2):
                    sl = slice(64 * half, 64 * half + 64)
                    h = 2 * (n0 + j) + half
                    V("copy", DQ[sl, h * T:(h + 1) * T], ps[sl, j * T:(j + 1) * T], w=[tk])
            return DV.last()

        proj(8, hk, 16, ev_d)
        t_dqk = DV.last()
        proj_tm(1, hk, 16, 512, lambda n, tb, ps, tk: V("copy", DVt[:, tb * 512:(tb + 1) * 512], ps[:, :], w=[tk]))
        t_dv = DV.last()

        ds = float(64 ** -0.5)
        zA = [HX[:, 384 * i:384 * (i + 1)] for i in range(4)]
        lA = [HX[:, 1536 + 384 * i:1536 + 384 * (i + 1)] for i in range(4)]
        eA = [HX[:, 3072 + 384 * i:3072 + 384 * (i + 1)] for i in range(2)]
        mS = C("mS")
        g1, g2, g3, g4, g5, g6 = ({} for _ in range(6))

        def d0(h):
            S = bank[3 + h % 2]
            PE.wait(free[3 + h % 2], t_dqk, t_dv)
            q, k = blk(DQ, h), blk(DK, h // 2)
            mm(S[:, 0:256], k[:, 0:128], q, True, True)
            g1[h] = PE.mark(mm(S[:, 256:384], k[:, 128:256], q[:, 128:256], True, True))

        def d1(h):
            S, z, e = bank[3 + h % 2], zA[h % 4], eA[h % 2]
            A(z, S[:, 0:384], ACT.Copy, scale=ds, w=[g1[h]])
            free[3 + h % 2] = A(e, S[:, 0:384], ACT.Abs, scale=ds, w=[prev(g3, h - 2)])
            A(e, e, ACT.Exp, scale=-1.0)
            g2[h] = A(e, e, ACT.Ln, bias=ones[:, 0:1])

        def d2(h):
            z, e, l = zA[h % 4], eA[h % 2], lA[h % 4]
            V("stt", e, z, 0.0, e, ALU.max, ALU.add, w=[g2[h]])
            V("tt", z, z, e, ALU.subtract)
            g3[h] = V("stt", l, e, -1.0, mS, ALU.mult, ALU.mult, w=[prev(g5, h - 4)])

        def d3_(h):
            l = lA[h % 4]
            PE.wait(free[5], g3[h])
            mm(bank[5][:, 0:256], C("U"), l[:, 0:256], True, False)
            mm(bank[5][:, 128:256], ones, l[:, 256:384], False, True)
            g4[h] = PE.mark(mm(bank[5][:, 256:384], C("U"), l[:, 256:384], True, True))

        def d4(h):
            z, a = zA[h % 4], lA[h % 4]
            free[5] = V("tt", z, z, bank[5][:, 0:384], ALU.add, w=[g4[h]])
            t = A(a, z, ACT.Exp, w=[DV.last()])
            g6[h] = V("tt", a, a, mS, ALU.mult, w=[t])

        def d5(h):
            a, j = lA[h % 4], h // 2
            PE.wait(free[6 + h % 2], g6[h])
            O = bank[6 + h % 2]
            mm(O[:, 0:256], DVt[:, j * 128:(j + 1) * 128], a[:, 0:256], True, False)
            g5[h] = PE.mark(mm(O[:, 128:256], DVt[:, 512 + j * 128:512 + (j + 1) * 128], a[:, 256:384], False, True))

        def d6(h):
            sl = slice(64 * (h % 2), 64 * (h % 2) + 64)
            free[6 + h % 2] = V("copy", MIX[sl, (12 + h // 2) * T:(13 + h // 2) * T], bank[6 + h % 2][sl, 0:256],
                                w=[g5[h]])

        AC.wait(PE.last(), DV.last())
        DV.wait(AC.last(), PE.last())
        pipe(8, [d0, d1, d2, d3_, d4, d5, d6])
        dump("MIXd", MIX[:, 3072:4096])

        BS = HX
        SX = [BS[:, 1024 * i:1024 * i + 512] for i in range(4)]
        SY = [BS[:, 1024 * i + 512:1024 * i + 768] for i in range(4)]
        SC = [BS[:, 1024 * i + 768:1024 * i + 800] for i in range(4)]
        PA = [R[5][:, 832 * i:832 * i + 768] for i in range(2)]
        PC = [R[5][0:15, 3072 + 256 * i:3072 + 256 * (i + 1)] for i in range(2)]
        nm = [small[:, 8 * i:8 * i + 6] for i in range(4)]
        sm = [small[:, 32 + 8 * i:32 + 8 * i + 6] for i in range(4)]
        n1, n2, n3, n4, n5, n6, n7 = ({} for _ in range(7))

        def seg(h):
            i = h % 4
            return [SX[i][:, 0:256], SX[i][:, 256:512], SY[i][:, 0:128], SY[i][:, 128:256],
                    SC[i][:, 0:15], SC[i][:, 16:23]]

        def a0(h):
            X1, Y1 = bank[0], bank[1]
            PE.wait(free[0], free[1], t_kc)
            q = blk(QZ, h)
            mm(X1[:, 0:256], q[:, 128:256], ksn, True, True)
            mm(X1[:, 256:512], q[:, 128:256], kwn, True, True)
            mm(Y1[:, 0:128], q[:, 0:128], ksn[:, 0:128], True, True)
            mm(Y1[:, 128:256], q[:, 0:128], kwn[:, 0:128], True, True)
            mm(Y1[:, 256:271], q[:, 128:256], kcn, True, True)
            n1[h] = PE.mark(mm(Y1[:, 272:279], q[:, 0:128], kcn[:, 0:7], True, True))

        def a1(h):
            i = h % 4
            X1, Y1 = bank[0], bank[1]
            bt = BT[:, h * 256:(h + 1) * 256]
            r2 = lambda ap, n: ap.rearrange("p (s k) -> p s k", s=n)
            V("stt", r2(SX[i], 2), r2(X1[:, 0:512], 2), ds, r2(bt, 1).broadcast_to([128, 2, 256]), ALU.mult, ALU.add,
              w=[n1[h], prev(n5, h - 4)])
            V("stt", r2(SY[i], 2), r2(Y1[:, 0:256], 2), ds, r2(bt[:, 128:256], 1).broadcast_to([128, 2, 128]),
              ALU.mult, ALU.add)
            V("stt", SC[i][:, 0:15], Y1[:, 256:271], ds, bt[:, 31:256:16], ALU.mult, ALU.add)
            V("stt", SC[i][:, 16:23], Y1[:, 272:279], ds, bt[:, 128 + 31:256:16], ALU.mult, ALU.add)
            free[0] = free[1] = DV.last()
            m = nm[i]
            V("red", m[:, 0:2], r2(SX[i], 2), AX, ALU.max)
            V("red", m[:, 2:4], r2(SY[i], 2), AX, ALU.max)
            V("red", m[:, 4:5], SC[i][:, 0:15], AX, ALU.max)
            V("red", m[:, 5:6], SC[i][:, 16:23], AX, ALU.max)
            n2[h] = V("ts", m, m, -1.0, None, ALU.mult)

        def a2(h):
            i = h % 4
            for s, ap in enumerate(seg(h)):
                n3[h] = A(ap, ap, ACT.Exp, bias=nm[i][:, s:s + 1], accum_out=sm[i][:, s:s + 1], w=[n2[h]])

        def a3(h):
            i = h % 4
            V("recip", sm[i], sm[i], w=[n3[h]])
            V("tt", sm[i], sm[i], GX[:, 6 * h:6 * h + 6], ALU.mult)
            for s, ap in enumerate(seg(h)):
                n4[h] = V("ts", ap, ap, sm[i][:, s:s + 1], None, ALU.mult)

        def a4(h):
            i = h % 4
            B1, B2 = bank[2], bank[3]
            PE.wait(free[2], free[3], free[4], n4[h])
            for s, B in ((0, B1), (1, B2)):
                nc.tensor.transpose(B[:, 0:128], SY[i][:, s * 128:(s + 1) * 128], ident)
                nc.tensor.transpose(B[:, 128:256], SX[i][:, s * 256:s * 256 + 128], ident)
                nc.tensor.transpose(B[:, 256:384], SX[i][:, s * 256 + 128:s * 256 + 256], ident)
            nc.tensor.transpose(bank[4][0:7, 0:128], SC[i][:, 16:23], ident)
            n5[h] = PE.mark(nc.tensor.transpose(bank[4][0:15, 128:256], SC[i][:, 0:15], ident))

        def a5(h):
            i = h % 2
            A(PA[i][:, 0:384], bank[2][:, 0:384], ACT.Copy, w=[n5[h], prev(n6, h - 2)])
            free[2] = A(PA[i][:, 384:768], bank[3][:, 0:384], ACT.Copy)
            free[3] = free[2]
            A(PC[i][0:7, 0:128], bank[4][0:7, 0:128], ACT.Copy)
            n7[h] = free[4] = A(PC[i][0:15, 128:256], bank[4][0:15, 128:256], ACT.Copy)

        def a6(h):
            i = h % 2
            O = bank[5 + h % 2]
            PE.wait(free[5 + h % 2], n7[h])
            mm(O[:, 0:256], VSW[:, 0:128], PA[i][:, 0:256], True, False)
            mm(O[:, 128:256], VSW[:, 256:384], PA[i][:, 256:384], False, False)
            mm(O[:, 0:256], VSW[:, 128:256], PA[i][:, 384:640], False, False)
            mm(O[:, 128:256], VSW[:, 384:512], PA[i][:, 640:768], False, False)
            mm(O[:, 0:128], vc[0:7, :], PC[i][0:7, 0:128], False, False)
            n6[h] = PE.mark(mm(O[:, 128:256], vc[0:15, :], PC[i][0:15, 128:256], False, True))

        def a7(h):
            g = h // 4
            sl = slice(64 * g, 64 * g + 64)
            free[5 + h % 2] = V("copy", MIX[sl, (h % 4) * T:(h % 4 + 1) * T], bank[5 + h % 2][sl, 0:256], w=[n6[h]])

        AC.wait(PE.last(), DV.last())
        DV.wait(AC.last(), PE.last())
        pipe(8, [a0, a1, a2, a3, a4, a5, a6, a7])
        dump("MIXa", MIX[:, 0:1024])

        og = PCOL["group_gain"][0]
        t_mix = DV.last()
        for g in range(4):
            sq = R[2][:, g * 1024:(g + 1) * 1024]
            t = A(sq, MIX[:, g * 1024:(g + 1) * 1024], ACT.Square, w=[t_mix, PE.last()])
            b, tk = colsum([sq[:, k * T:(k + 1) * T] for k in range(4)], w=[t])
            rs = RS5[:, g * T:(g + 1) * T]
            t = free[b] = rstd(rs, bank[b][:, 0:T], 512, 0, w=[tk])
            for k in range(4 * g, 4 * g + 4):
                V("stt", blk(MIX, k), blk(MIX, k), pv[:, og + k:og + k + 1], rs, ALU.mult, ALU.mult, w=[t])
        proj(16, lambda k: blk(MIX, k), 16,
             lambda n0, cnt, ps, tk: V("tt", blk(X, n0, 2), blk(X, n0, 2), ps[:, :], ALU.add, w=[tk]),
             w=[DV.last()])
        t_x3 = DV.last()
        dump("x3", X[:, :])
        t_f = rms_all("norm_ffn", R[1], R[2], t_x3)
        fchunk = lambda i: R[2 + i // 16][:, (i % 16) * T:(i % 16 + 1) * T]
        sg = [R[7][:, 256 * i:256 * (i + 1)] for i in range(2)]
        tf = {}
        AC.wait(PE.last())

        def ev_f(n0, cnt, ps, tk):
            i = n0 // 2
            t = A(sg[i % 2], ps[:, 0:T], ACT.Silu, w=[tk, prev(tf, i - 2)])
            tf[i] = V("tt", fchunk(i), ps[:, T:2 * T], sg[i % 2], ALU.mult, w=[t])
            return tf[i]

        proj(2 * FFN_BLOCKS, lambda k: blk(R[1], k), 16, ev_f, w=[t_f])
        OUT = R[5]
        n_out = [0]

        def ev_out(n0, cnt, ps, tk):
            t = V("tt", blk(OUT, n0, 2), blk(X, n0, 2), ps[:, :], ALU.add, w=[tk])
            AC.wait(t)
            nc.scalar.dma_start(out[:, n0 * T:(n0 + 2) * T], blk(OUT, n0, 2)).then_inc(s_fin, 16)
            n_out[0] += 1
            return t

        s_fin = sem("s_fin")
        proj(16, fchunk, FFN_BLOCKS, ev_out, w=[DV.last()])
        nc.scalar.wait_ge(s_fin, 16 * n_out[0])
        nc.sync.wait_ge(s_fin, 16 * n_out[0])
        assert pos_[0] == len(tiles)


def pack(inputs):
    w = {k: np.asarray(v) for k, v in inputs.items()}
    tiles = weight_tiles()
    places, n_units = pack_tiles(tiles)
    W = np.zeros((n_units, 128, UCOLS), np.float32)
    mix = mix_rows()
    mats = {n: w[n].reshape(w[n].shape[-2:]) for n in
            ("mla_w_in", "mla_w_qb", "mla_w_kvb", "mla_w_out", "ml_w_in", "ml_w_out", "w_in_2", "w_out_2",
             "w_ffn_gate_2", "w_ffn_up_2", "w_ffn_down_2")}
    mats["w_out_2"] = mats["w_out_2"][mix]
    w1 = w["cmp_w1_2"].reshape(2, 32, 64, 64)
    w2 = w["cmp_w2_2"].reshape(2, 64, 64)
    for (src, k, cols, kind), (u, c) in zip(tiles, places):
        if kind == "bd":
            m = w1[k, cols[0]] if src == "cmp_w1_2" else w2[k]
            W[u, 0:64, c:c + 64] = m
            W[u, 64:128, c + 64:c + 128] = m
        elif cols[-1] - cols[0] == len(cols) - 1:
            W[u, :, c:c + len(cols)] = mats[src][k:k + 128, cols[0]:cols[0] + len(cols)]
        else:
            W[u, :, c:c + len(cols)] = mats[src][k:k + 128][:, cols]
    pvec = np.zeros((128, NP), np.float32)

    def put(name, a):
        o, n = PCOL[name]
        pvec[:a.shape[0], o:o + a.shape[1]] = a

    def fm(a):
        return a.reshape(-1, 128).T

    put("q_norm", fm(w["mla_q_norm"]))
    put("kv_norm", fm(w["mla_kv_norm"]))
    put("ln_w", fm(w["ln_w"]))
    put("ln_b", fm(w["ln_b"]))
    put("conv_w", fm(w["ml_conv_w"]))
    put("conv_b", fm(w["ml_conv_b"]))
    put("head_norm", fm(w["ml_head_norm"]))
    put("norm_mix", fm(w["norm_mix_2"]))
    put("norm_ffn", fm(w["norm_ffn_2"]))
    for n in ("q_gain", "k_gain"):
        g = w[n + "_2"].reshape(64, 1)
        put(n, np.concatenate([g, g], 0))
    p = w["cmp_pos_2"].reshape(2, 32, 64).transpose(2, 0, 1).reshape(64, 64)
    put("cmp_pos", np.concatenate([p, p], 0))
    put("conv2", fm(w["conv_w_2"]))
    put("group_gain", fm(w["group_gain_2"].reshape(-1)[mix]))
    gb = w["ml_gate_b"].reshape(16, 1)
    put("ib", gb[0:8])
    put("fb", gb[8:16])
    put("table", w["rel_table_2"])
    put("sgu_w", w["sgu_w_2"].reshape(8, 128, 128).transpose(2, 0, 1).reshape(128, 1024))
    sb_ = w["sgu_b_2"].reshape(4, 2, 128)
    put("sgu_b", np.repeat(sb_.transpose(1, 0, 2), 64, axis=0).reshape(128, 512))
    x = w["x"].reshape(T, 16, 128).transpose(2, 1, 0).reshape(128, 4096)
    return {"W": W, "pv": pvec, "cst": constants(), "x": np.ascontiguousarray(x),
            "pos": np.ascontiguousarray(w["positions"].reshape(1, T).astype(np.int32))}


DUMPS = {}


def kernel(**inputs):
    import concourse.bacc as _bacc
    from concourse.bass_utils import run_bass_kernel_spmd as _run

    nc = _bacc.Bacc("TRN2", target_bir_lowering=False, num_devices=1)
    arrays = pack(inputs)
    dr = {}
    for name, a in arrays.items():
        dr[name] = nc.dram_tensor("in_" + name, a.shape, I32 if name == "pos" else F32, kind="ExternalInput").ap()
    dr["rv"] = nc.dram_tensor("rv", (8, 383), F32, kind="Internal").ap()
    out = nc.dram_tensor("out_0", (128, 4096), F32, kind="ExternalOutput").ap()
    dumps = {k: nc.dram_tensor("dump_" + k, s, F32, kind="ExternalOutput").ap() for k, s in DUMPS.items()}
    build(nc, dr, out, dumps)
    r = _run(nc, [{"in_" + k: a for k, a in arrays.items()}], core_ids=[0])
    y = np.asarray(r.results[0]["out_0"]).reshape(128, 16, T).transpose(2, 1, 0).reshape(1, T, DM)
    return np.ascontiguousarray(y)
```

```python
from contextlib import ExitStack

import numpy as np
import concourse.bass as bass
from concourse import mybir

F32 = mybir.dt.float32
I32 = mybir.dt.int32
FR = mybir.dt.float32r
ALU = mybir.AluOpType
ACT = mybir.ActivationFunctionType
AX = mybir.AxisListType.X

T = 256
DM = 2048
NEG = -1.0e30
EPS = 1e-6
ALPHA = 4.0 ** 0.25
HCOLS = 1024
NRAW = 4
NW = 4
FFN_HALF = 22


KO = 4


def tile_order(n_blocks, nk, ko):
    order = [(b, k) for k in range(nk) for b in range(ko)]
    return order + [(b, k) for b in range(ko, n_blocks) for k in range(nk)]


def weight_tiles():
    tiles = []

    def t_blocks(src, blocks, rows, ko=0, row0=0):
        for b, k in tile_order(len(blocks), rows // 128, ko):
            tiles.append((src, row0 + k * 128, blocks[b], "w"))

    def r(a, n):
        return list(range(a, a + n))

    t_blocks("mla_w_in", [r(128 * b, 128) for b in range(8)] + [r(1024, 64) * 2], DM, KO)
    t_blocks("mla_w_in", [r(1088 + 128 * b, 128) for b in range(16)], DM)
    for g in range(4):
        t_blocks("mla_w_qb", [[192 * (4 * g + i) + 128 + 32 * half + j for i in range(4) for j in range(32)]
                              for half in range(2)], 512)
        t_blocks("mla_w_qb", [r(192 * (4 * g + i), 128) for i in range(4)], 512)
        t_blocks("mla_w_kvb", [r(256 * (4 * g + i), 128) for i in range(4)], 512)
        t_blocks("mla_w_kvb", [[256 * (4 * g + i) + 128 + j for i in range(4) for j in range(128)]], 512)
    t_blocks("mla_w_out", [r(128 * b, 128) for b in range(16)], DM, KO)

    t_blocks("ml_w_in", [r(128 * b, 128) for b in range(16)], DM, KO)
    t_blocks("ml_w_in", [r(6144, 16)], DM)
    t_blocks("ml_w_in", [r(2048 + 512 * n, 512) for n in range(4)], DM)
    t_blocks("ml_w_in", [r(4096 + 128 * b, 128) for b in range(16)], DM)
    t_blocks("ml_w_in", [r(6160 + 128 * b, 128) for b in range(16)], DM)
    t_blocks("ml_w_out", [r(128 * b, 128) for b in range(16)], DM, KO)

    kv = 512
    t_blocks("w_in_2", [r(64 * i, 64) + r(64 * (4 + i), 64) for i in range(4)] +
             [r(kv + 128 * i, 128) for i in (0, 1, 2, 4)], DM, KO)
    t_blocks("w_in_2", [r(kv + 128 * 3, 128) + r(kv + 128 * 5, 128) + r(1280, 24)], DM)
    b0 = 1304
    c0 = b0 + 1536
    d0 = c0 + 1024
    t_blocks("w_in_2", [r(c0 + 128 * b, 128) for b in range(4)], DM)
    t_blocks("w_in_2", [r(c0 + 512, 512)], DM)
    for i in range(2):
        for l in range(32):
            tiles.append(("cmp_w1_2", i, [l], "bd"))
    tiles.append(("cmp_w2_2", 0, [0], "bd"))
    tiles.append(("cmp_w2_2", 1, [0], "bd"))
    t_blocks("w_in_2", [r(d0 + 128 * b, 128) for b in range(8)], DM)
    t_blocks("w_in_2", [r(d0 + 1024, 512)], DM)
    t_blocks("w_in_2", [r(b0 + 128 * b, 128) for b in range(12)], DM)
    t_blocks("w_out_2", [r(128 * b, 128) for b in range(16)], DM, KO)
    for half in range(2):
        blocks = []
        for b in range(FFN_HALF * half, FFN_HALF * (half + 1)):
            blocks += [("w_ffn_gate_2", r(128 * b, 128)), ("w_ffn_up_2", r(128 * b, 128))]
        for b, k in tile_order(len(blocks), 16, 0 if half else KO):
            tiles.append((blocks[b][0], k * 128, blocks[b][1], "w"))
        t_blocks("w_ffn_down_2", [r(128 * b, 128) for b in range(16)], 128 * FFN_HALF, KO,
                 128 * FFN_HALF * half)
    return tiles


def tile_width(t):
    return 128 if t[3] == "bd" else len(t[2])


def pack_tiles(tiles):
    places, kinds, c = [], [tiles[0][3]], 0
    for t in tiles:
        w = tile_width(t)
        if c + w > HCOLS or t[3] != kinds[-1]:
            kinds.append(t[3])
            c = 0
        places.append((len(kinds) - 1, c))
        c += w
    if len(kinds) % 2:
        kinds.append("none")
    return places, kinds


def mix_rows():
    rows = []
    for i in range(4):
        rows += list(range(64 * i, 64 * i + 64)) + list(range(64 * (4 + i), 64 * (4 + i) + 64))
    return np.array(list(range(512, 2048)) + rows)


PCOL = {}
_n = 0
for _name, _w in [("q_norm", 4), ("kv_norm", 4), ("ln_w", 32), ("ln_b", 32), ("conv_w", 64), ("conv_b", 16),
                  ("head_norm", 16), ("norm_mix", 16), ("norm_ffn", 16), ("q_gain", 1), ("k_gain", 1),
                  ("cmp_pos", 64), ("conv2", 12), ("group_gain", 16), ("ib", 1), ("fb", 1), ("table", 8)]:
    PCOL[_name] = (_n, _w)
    _n += _w
NP = _n
CCOL = {}
_n = 0
for _name, _w in [("ident", 128), ("bones", 128), ("U", 128), ("mC", 256), ("mS", 384), ("tril", 128),
                  ("R12", 256), ("u", 128), ("v", 128), ("invf", 1), ("rowv", 1), ("ones", 128), ("J", 128),
                  ("eps", 4)]:
    CCOL[_name] = (_n, _w)
    _n += _w
NC_ = _n

def rel_bucket(n):
    n = np.maximum(n, 0)
    nf = np.maximum(n, 1).astype(np.float32)
    large = 16 + (np.log(nf / np.float32(16)) / np.float32(np.log(64.0)) * np.float32(16)).astype(np.int32)
    return np.where(n < 16, n, np.minimum(large, 31))


def constants():
    c = np.zeros((128, NC_), np.float32)

    def put(name, a):
        a = np.asarray(a, np.float32)
        o, w = CCOL[name]
        c[:a.shape[0], o:o + a.shape[1]] = a

    i = np.arange(128)
    put("ident", np.eye(128))
    put("bones", (i[:, None] // 64) == (i[None, :] // 64))
    put("U", i[:, None] > i[None, :])
    put("mC", np.concatenate([np.where(i[:, None] <= i[None, :], 0.0, NEG), np.zeros((128, 128))], 1))
    strict = (i[:, None] < i[None, :]) * 1.0
    put("mS", np.concatenate([strict, np.ones((128, 128)), strict], 1))
    put("tril", i[:, None] <= i[None, :])
    dist = 255 - np.arange(383)
    hot = (np.arange(32)[:, None] == rel_bucket(dist)[None, :]) & (dist >= 0)[None, :]
    late = np.zeros((32, 766 + 1024), np.float32)
    late[:, 0:383] = hot
    late[0:8, 383:766] = np.where(dist >= 0, 0.0, NEG)
    late[0:8, 766:] = np.repeat(np.eye(8), 128, axis=1)
    r12 = np.zeros((64, 256))
    for m in range(128):
        r12[m % 32, m] = 1.0
        r12[32 + m % 32, 128 + m] = 1.0
    put("R12", r12)
    put("u", (i < 64)[None, :])
    put("v", np.where(i >= 64, NEG, 0.0)[None, :])
    f = (np.float64(10000.0) ** (-np.arange(0, 64, 2, dtype=np.float64) / 64)).astype(np.float32)
    put("invf", np.tile(f, 4)[:, None])
    put("rowv", (i >= 31)[:, None])
    put("ones", np.ones((128, 128)))
    put("J", np.eye(128)[::-1])
    put("eps", np.tile([[1e-6, 1e-5, np.pi / 2, 0.0]], (128, 1)))
    return c, late


class Queue:

    def __init__(self, eng, sem):
        self.eng, self.sem, self.n, self.seen = eng, sem, 0, {}

    def wait(self, *toks):
        for t in toks:
            if t is None:
                continue
            if isinstance(t, list):
                self.wait(*t)
                continue
            s, v = t
            if self.seen.get(id(s), 0) < v:
                self.eng.wait_ge(s, v)
                self.seen[id(s)] = v

    def mark(self, ins):
        ins.then_inc(self.sem, 1)
        self.n += 1
        return (self.sem, self.n)

    def last(self):
        return (self.sem, self.n) if self.n else None


def build(nc, dr, out, dumps):
    with ExitStack() as ctx:
        def sem(name):
            return ctx.enter_context(nc.semaphore(name))

        top = [nc.sbuf_base + 31 & ~31]

        def sb(name, cols, dt=F32, at=None):
            if at is None:
                at = top[0]
                top[0] += -(-4 * cols // 32) * 32
            return nc.alloc_sbuf_tensor_at(name, [128, cols], dt, offset=at)

        pv = sb("pv", NP)
        cst = sb("cst", NC_)
        small = sb("small", 64)
        mu = sb("mu", T)
        acc = sb("acc", T)
        X = sb("X", 4096)
        xh0 = top[0]
        XH = sb("XH", 4096, FR)
        xl0 = top[0]
        XL = sb("XL", 4096, FR)
        raw = sb("raw", NRAW * 2 * HCOLS)
        WH = sb("WH", NW * HCOLS, FR)
        WL = sb("WL", NW * HCOLS, FR)
        a0_ = top[0]
        n_ar = (nc.sbuf_usable_end - a0_) // 4
        assert n_ar >= 21504, n_ar
        AR = sb("AR", 21504, at=a0_)

        def ar(o, n):
            return AR[:, o:o + n]

        def ar_r(name, o, n):
            return sb(name, n, FR, at=a0_ + 4 * o)

        bank = [ctx.enter_context(nc.psum_tensor(f"bank{i}", [128, 512], F32)) for i in range(8)]
        PE = Queue(nc.tensor, sem("s_pe"))
        DV = Queue(nc.vector, sem("s_dve"))
        AC = Queue(nc.scalar, sem("s_act"))
        SP = Queue(nc.sync, sem("s_sp"))
        s_raw = [sem(f"s_raw{i}") for i in range(NRAW)]
        s_x = [sem(f"s_x{i}") for i in range(4)]
        s_cst, s_pv, s_pos, s_rv, s_bt, s_E, s_oh, s_sgu, s_out, s_fin = (
            sem(n) for n in ("s_cst", "s_pv", "s_pos", "s_rv", "s_bt", "s_E", "s_oh", "s_sgu", "s_out", "s_fin"))

        vec = {"ts": nc.vector.tensor_scalar, "tt": nc.vector.tensor_tensor,
               "stt": nc.vector.scalar_tensor_tensor, "copy": nc.vector.tensor_copy,
               "red": nc.vector.tensor_reduce, "recip": nc.vector.reciprocal,
               "memset": nc.vector.memset, "scan": nc.vector.tensor_tensor_scan,
               "bns": nc.vector.bn_stats, "bna": nc.vector.bn_aggr}

        def V_(name, *a, w=(), **k):
            DV.wait(*w)
            return DV.mark(vec[name](*a, **k))

        def V(name, *a, w=(), **k):
            DV.wait(DV.last())
            return V_(name, *a, w=w, **k)

        def A_(out_, in_, func, w=(), **k):
            AC.wait(*w)
            return AC.mark(nc.scalar.activation(out_, in_, func, **k))

        def A(out_, in_, func, w=(), **k):
            AC.wait(AC.last())
            return A_(out_, in_, func, w=w, **k)

        def mm(o, lhsT, rhs, start, stop):
            return nc.tensor.matmul(o, lhsT, rhs, start=start, stop=stop)

        def P(name, rows=128):
            o, w = PCOL[name]
            return pv[0:rows, o:o + w]

        def C(name, rows=128):
            o, w = CCOL[name]
            return cst[0:rows, o:o + w]

        def blk(t, i, n=1):
            return t[:, i * T:(i + n) * T]

        def prev(d, i):
            return d[i] if i >= 0 else None

        def pipe(n, stages, filler=None, per=0):
            for step in range(n + len(stages) - 1):
                for s in range(len(stages) - 1, -1, -1):
                    if 0 <= step - s < n:
                        stages[s](step - s)
                go(filler, per)

        def go(gen, n=None):
            while gen is not None and (n is None or n > 0):
                if next(gen, "end") == "end":
                    return
                n = None if n is None else n - 1

        tiles = weight_tiles()
        places, kinds = pack_tiles(tiles)
        n_units = len(kinds) // 2
        last_tile = {}
        for i, (hf, c) in enumerate(places):
            last_tile[hf] = i
        split_no, n_ = {}, 0
        for hf, kd in enumerate(kinds):
            if kd == "w":
                split_no[hf] = n_
                n_ += 1
        st = {"tile": 0, "split": 0, "loaded": -1}
        left = {u: [kd != "none" for kd in kinds[2 * u:2 * u + 2]].count(True) for u in range(n_units)}
        freed = {u: [] for u in range(n_units)}
        read_by_pe, split_done = {}, {}

        def raw_half(hf):
            o = (hf // 2 % NRAW) * 2 * HCOLS + (hf % 2) * HCOLS
            return raw[:, o:o + HCOLS]

        def landed(hf):
            u = hf // 2
            return (s_raw[u % NRAW], 16 * (u // NRAW + 1))

        def load(u):
            if u >= NRAW:
                SP.wait(freed[u - NRAW])
            o = (u % NRAW) * 2 * HCOLS
            nc.sync.dma_start(raw[:, o:o + 2 * HCOLS], dr["W"][u]).then_inc(s_raw[u % NRAW], 16)
            st["loaded"] = u

        def raw_read(hf, tok):
            u = hf // 2
            left[u] -= 1
            freed[u].append(tok)
            if left[u] == 0 and u + NRAW < n_units:
                load(u + NRAW)

        def pump():
            while st["split"] < len(kinds):
                hf = st["split"]
                if kinds[hf] != "w":
                    st["split"] += 1
                    continue
                i = split_no[hf]
                if hf // 2 > st["loaded"] or (i >= NW and i - NW not in read_by_pe):
                    return
                o = (i % NW) * HCOLS
                wh, wl = WH[:, o:o + HCOLS], WL[:, o:o + HCOLS]
                free_ = read_by_pe[i - NW] if i >= NW else None
                t = A_(wh, raw_half(hf), ACT.Copy, w=[landed(hf), free_])
                split_done[hf] = V_("tt", wl, raw_half(hf), wh.bitcast(F32), ALU.subtract, w=[t, landed(hf), free_])
                st["split"] += 1
                raw_read(hf, split_done[hf])

        def take():
            i = st["tile"]
            st["tile"] += 1
            hf, c = places[i]
            w = tile_width(tiles[i])
            if kinds[hf] == "w":
                PE.wait(split_done[hf])
                o = (split_no[hf] % NW) * HCOLS + c
                return WH[:, o:o + w], WL[:, o:o + w]
            PE.wait(landed(hf))
            return raw_half(hf)[:, c:c + w]

        def used(ins):
            i = st["tile"] - 1
            hf = places[i][0]
            if last_tile[hf] != i:
                return None
            t = PE.mark(ins)
            if kinds[hf] == "w":
                read_by_pe[split_no[hf]] = t
            else:
                raw_read(hf, t)
            pump()
            return t

        free = {i: None for i in range(8)}
        BIG = [0, 1, 2]
        turn = [0]

        def next_bank():
            b = BIG[turn[0] % len(BIG)]
            turn[0] += 1
            PE.wait(free[b])
            return b

        def mul(o, wt, xh, xl, first, last):
            wh, wl = wt
            mm(o, wh, xh, first, False)
            mm(o, wh, xl, False, False)
            return mm(o, wl, xh, False, last)

        def proj(n_blocks, xh, xl, nk, evac, ko=0, rdy=None, pre=None):
            last = {}
            kb = [0, 1, 2, 3]
            at = {}
            for n, k in tile_order(n_blocks, nk, ko):
                if k == 0:
                    if n < ko:
                        at[n] = kb[n]
                        PE.wait(free[kb[n]])
                    else:
                        at[n] = next_bank()
                if rdy is not None:
                    PE.wait(rdy[k])
                wt = take()
                ins = mul(bank[at[n]][:, 0:T], wt, blk(xh, k), blk(xl, k), k == 0, k == nk - 1)
                t = used(ins)
                if k == nk - 1:
                    last[n] = t or PE.mark(ins)
                    if n == ko - 1 and pre is not None:
                        pre()
                    if n >= ko:
                        free[at[n]] = evac(n, bank[at[n]][:, 0:T], last[n])
                    elif n == ko - 1:
                        for m in range(ko):
                            free[at[m]] = evac(m, bank[at[m]][:, 0:T], last[m])
                if k % 4 == 3:
                    yield

        def proj_tm(n_blocks, xh, xl, nk, width, evac):
            for n in range(n_blocks):
                bs = [next_bank(), next_bank()]
                for k in range(nk):
                    wh, wl = take()
                    for tb in range(2):
                        o = bank[bs[tb]][:, 0:width]
                        s = slice(k * T + tb * 128, k * T + (tb + 1) * 128)
                        mm(o, xh[:, s], wh, k == 0, False)
                        mm(o, xh[:, s], wl, False, False)
                        ins = mm(o, xl[:, s], wh, False, k == nk - 1)
                    t = used(ins)
                    if k % 4 == 3 and k < nk - 1:
                        yield
                tk = t or PE.mark(ins)
                for tb in range(2):
                    free[bs[tb]] = evac(n, tb, bank[bs[tb]], tk)
                yield

        ones = C("ones")
        ident = C("ident")

        def total(src, w, n=1, b=4):
            PE.wait(free[b], *w)
            for k in range(n):
                ins = mm(bank[b][:, 0:T], ones, src[:, k * T:(k + 1) * T], k == 0, k == n - 1)
            return PE.mark(ins)

        def rstd(dst, src, n, eps_col, w=()):
            o = CCOL["eps"][0] + eps_col
            rows = dst.shape[0]
            A(dst, src, ACT.Ln, scale=1.0 / n, bias=cst[0:rows, o:o + 1], w=w)
            return A(dst, dst, ACT.Exp, scale=-0.5)

        def halves(src, hi, lo, w=(), scale=None):
            if scale is None:
                t = A_(hi, src, ACT.Copy, w=w)
                return V_("tt", lo, src, hi.bitcast(F32), ALU.subtract, w=[t])
            t = A_(hi, src, ACT.Copy, scale=scale, w=w)
            return V_("stt", lo, src, scale, hi.bitcast(F32), ALU.mult, ALU.subtract, w=[t])

        dump_n = [0]

        def dump(name, ap):
            if name in dumps:
                nc.scalar.wait_ge(DV.sem, DV.n)
                nc.scalar.wait_ge(AC.sem, AC.n)
                nc.scalar.dma_start(dumps[name], ap).then_inc(s_out, 16)
                dump_n[0] += 1
                nc.scalar.wait_ge(s_out, 16 * dump_n[0])
                t = AC.mark(nc.scalar.activation(small[:, 63:64], cst[:, 0:1], ACT.Copy))
                DV.wait(t)
                PE.wait(t)

        for q in range(4):
            nc.sync.dma_start(X[:, q * 1024:(q + 1) * 1024], dr["x"][:, q * 1024:(q + 1) * 1024]).then_inc(s_x[q], 16)
            if q == 0:
                load(0)
        posi = sb("posi", T, I32, at=a0_ + 4 * 19456)
        for u in range(1, NRAW):
            load(u)
        nc.scalar.dma_start(posi[:, :], dr["pos"][0:1, :].broadcast_to([128, T])).then_inc(s_pos, 16)
        nc.scalar.dma_start(pv[:, :], dr["pv"][:, :]).then_inc(s_pv, 16)
        nc.scalar.dma_start(cst[:, :], dr["cst"][:, :]).then_inc(s_cst, 16)
        t_cst, t_pv = (s_cst, 16), (s_pv, 16)
        rdy = {}
        for q in range(4):
            s = slice(q * 1024, (q + 1) * 1024)
            t = halves(X[:, s], XH[:, s], XL[:, s], w=[(s_x[q], 16)])
            if q == 0:
                pump()
            for k in range(4 * q, 4 * q + 4):
                rdy[k] = t

        Vt, Z = ar(0, 4096), ar(4096, 4096)
        CH, CL, KH, KL = (ar_r(n, 8192 + 1024 * i, 1024) for i, n in enumerate(("CH", "CL", "KH", "KL")))
        qr = [ar(12288, 1024), ar(13312, 1024)]
        krm = ar(14336, 2048)
        cos, sin = ar(16384, 256), ar(16640, 256)
        Pm = [ar(16896 + 384 * i, 384) for i in range(2)]
        PT = [ar(17664 + 384 * i, 384) for i in range(2)]
        gt = [ar(18432 + 256 * i, 256) for i in range(2)]
        rt = [ar(18944 + 256 * i, 256) for i in range(2)]
        posf, ang, tmp = ar(19712, 256), ar(19968, 256), ar(20224, 256)
        rsx, rsy = ar(20480, 256), ar(20736, 256)
        ko_ = ar(20992, 512)
        qn = sb("QN", 4096, at=xh0)
        kn = sb("KN", 4096, at=xl0)
        cq, ckv, sqc, krT, kr12 = ar(0, 1024), ar(1024, 1024), ar(2048, 1024), AR[0:64, 3072:3328], ar(3328, 512)

        def ev_c(n, ps, tk):
            if n == 8:
                return V_("copy", krT, ps[0:64, :], w=[tk])
            return V_("copy", (cq if n < 4 else ckv)[:, n % 4 * T:(n % 4 + 1) * T], ps, w=[tk])

        go(proj(9, XH, XL, 16, ev_c, ko=KO, rdy=rdy))
        t_c = DV.last()
        zp = proj(16, XH, XL, 16, lambda n, ps, tk: A_(blk(Z, n), ps, ACT.Silu, w=[tk]))
        DV.wait(t_cst, t_pv)
        AC.wait(t_cst, t_pv)
        PE.wait(t_cst, t_pv)

        V("copy", posf, posi[:, :], w=[(s_pos, 16)])
        o = CCOL["invf"][0]
        V("ts", ang, posf, cst[:, o:o + 1], None, ALU.mult)
        two_pi = 2 * np.pi
        p1 = float(np.float32(6.28125))
        p2 = float((np.float32(two_pi - 6.28125).view(np.uint32) & np.uint32(0xFFFFF000)).view(np.float32))
        p3 = float(np.float32(two_pi - p1 - p2))
        magic = 12582912.0
        V("ts", tmp, ang, float(1.0 / two_pi), magic, ALU.mult, ALU.add)
        V("ts", tmp, tmp, magic, None, ALU.subtract)
        for p in (p1, p2, p3):
            V("stt", ang, tmp, -p, ang, ALU.mult, ALU.add)
        V("ts", tmp, ang, 3.1415925, -3.1415925, ALU.min, ALU.max)
        t_sin = A_(sin, tmp, ACT.Sin, w=[DV.last()])
        V("stt", ang, ang, -1.0, ang, ALU.mult, ALU.min)
        V("ts", ang, ang, float(np.pi / 2), None, ALU.add)
        t_cos = A_(cos, ang, ACT.Sin, w=[DV.last()])
        DV.wait(t_cos)

        nc.scalar.preload_act_table_set("natural_log_exp_and_others")
        for src, rs, g, hi, lo in ((cq, rsx, "q_norm", CH, CL), (ckv, rsy, "kv_norm", KH, KL)):
            t = A(sqc, src, ACT.Square, w=[t_c, PE.last()])
            go(zp, 3)
            tk = total(sqc, [t], 4)
            free[4] = t = rstd(rs, bank[4][:, 0:T], 512, 0, w=[tk])
            for k in range(4):
                s = slice(k * T, (k + 1) * T)
                t2 = V_("stt", src[:, s], src[:, s], P(g)[:, k:k + 1], rs, ALU.mult, ALU.mult, w=[t])
                t_cn = halves(src[:, s], hi[:, s], lo[:, s], w=[t2])
            go(zp, 3)

        PE.wait(free[5])
        mm(bank[5][:, 0:T], C("R12", 64)[:, 0:128], krT, True, True)
        tk = PE.mark(mm(bank[5][:, T:2 * T], C("R12", 64)[:, 128:256], krT, True, True))
        free[5] = V("copy", kr12, bank[5][:, :], w=[tk])
        V("memset", krm, 0.0)
        V("tt", rt[0], kr12[:, 0:T], cos, ALU.mult)
        V("tt", rt[1], kr12[:, T:2 * T], sin, ALU.mult)
        V("tt", ko_[:, 0:T], rt[0], rt[1], ALU.subtract)
        V("tt", rt[0], kr12[:, 0:T], sin, ALU.mult)
        V("tt", rt[1], kr12[:, T:2 * T], cos, ALU.mult)
        V("tt", ko_[:, T:2 * T], rt[0], rt[1], ALU.add)
        for i in range(4):
            for half in range(2):
                V("copy", krm[32 * i:32 * i + 32, (2 * i + half) * T:(2 * i + half + 1) * T],
                  ko_[32 * i:32 * i + 32, half * T:(half + 1) * T])
        t_krm = DV.last()
        go(zp)
        t_z = AC.last()
        dump("Z", Z)

        t_grp = {}

        def mla_groups():
            for g in range(4):
                yield from proj(2, CH, CL, 4, lambda n, ps, tk: A_(qr[n][:, g * T:(g + 1) * T], ps, ACT.Copy, w=[tk]))
                x1, x2 = (qr[n][:, g * T:(g + 1) * T] for n in range(2))
                V("tt", rt[0], x2, sin, ALU.mult, w=[AC.last()])
                V_("tt", rt[1], x1, sin, ALU.mult)
                V("tt", x1, x1, cos, ALU.mult)
                V("tt", x1, x1, rt[0], ALU.subtract)
                V("tt", x2, x2, cos, ALU.mult)
                V("tt", x2, x2, rt[1], ALU.add)
                yield from proj(4, CH, CL, 4, lambda n, ps, tk: A_(blk(qn, 4 * g + n), ps, ACT.Copy, w=[tk]))
                yield from proj(4, KH, KL, 4, lambda n, ps, tk: V_("copy", blk(kn, 4 * g + n), ps, w=[tk]))
                yield from proj_tm(1, KH, KL, 4, 512, lambda n, tb, ps, tk:
                                   A_(Vt[:, tb * 2048 + g * 512:tb * 2048 + (g + 1) * 512], ps[:, :], ACT.Copy,
                                      w=[tk]))
                t_grp[g] = [AC.last(), DV.last()]

        DV.wait(PE.last(), t_z)
        AC.wait(PE.last(), DV.last())
        PE.wait(t_cn)
        gen = mla_groups()
        while 0 not in t_grp:
            go(gen, 1)

        sc = float(192 ** -0.5)
        mx = [small[:, 8 * i:8 * i + 2] for i in range(2)]
        ss = [small[:, 16 + 8 * i:16 + 8 * i + 2] for i in range(2)]
        tk_s, tk_e, tk_r, tk_t, tk_c, tk_o, tk_n, tk_h, tk_g, rdy = ({} for _ in range(10))

        def st_scores(h):
            while h // 4 not in t_grp:
                go(gen, 1)
            S = bank[3 + h % 2]
            PE.wait(free[3 + h % 2], t_krm, *t_grp[h // 4])
            g, i = h // 4, h % 4
            a = [blk(qn, h), blk(qr[0], g), blk(qr[1], g)]
            k = [blk(kn, h), blk(krm, 2 * i), blk(krm, 2 * i + 1)]
            for j in range(3):
                mm(S[:, 0:128], a[j][:, 0:128], k[j][:, 0:128], j == 0, False)
            mm(S[:, 0:128], C("u", 1), C("v", 1), False, True)
            for j in range(3):
                mm(S[:, 128:384], a[j][:, 128:256], k[j], j == 0, False)
            tk_s[h] = PE.mark(mm(S[:, 256:384], C("u", 1), C("v", 1), False, True))

        def st_max(h):
            S, m = bank[3 + h % 2], mx[h % 2]
            V_("red", m[:, 0:1], S[:, 0:128], AX, ALU.max, w=[tk_s[h], prev(tk_e, h - 2)])
            V_("red", m[:, 1:2], S[:, 128:384], AX, ALU.max)
            tk_n[h] = V("ts", m, m, -sc, None, ALU.mult)

        def st_exp(h):
            S, m = bank[3 + h % 2], mx[h % 2]
            A_(Pm[h % 2][:, 0:128], S[:, 0:128], ACT.Exp, scale=sc, bias=m[:, 0:1], accum_out=ss[h % 2][:, 0:1],
               w=[tk_n[h], prev(tk_t, h - 2), prev(tk_r, h - 2)])
            tk_e[h] = A_(Pm[h % 2][:, 128:384], S[:, 128:384], ACT.Exp, scale=sc, bias=m[:, 1:2],
                         accum_out=ss[h % 2][:, 1:2])
            free[3 + h % 2] = tk_e[h]

        def st_norm(h):
            s, p = ss[h % 2], Pm[h % 2]
            V_("recip", s, s, w=[tk_e[h]])
            V("ts", p[:, 0:128], p[:, 0:128], s[:, 0:1], None, ALU.mult)
            tk_r[h] = V_("ts", p[:, 128:384], p[:, 128:384], s[:, 1:2], None, ALU.mult)

        def st_turn(h):
            b, p = bank[5 + h % 2], Pm[h % 2]
            PE.wait(free[5 + h % 2], tk_r[h])
            for j in range(3):
                ins = nc.tensor.transpose(b[:, 128 * j:128 * j + 128], p[:, 128 * j:128 * j + 128], ident)
            tk_t[h] = PE.mark(ins)

        def st_copy(h):
            tk_c[h] = free[5 + h % 2] = A_(PT[h % 2], bank[5 + h % 2][:, 0:384], ACT.Copy,
                                           w=[tk_t[h], prev(tk_o, h - 2)])

        def st_pv(h):
            PE.wait(tk_c[h], free[7])
            mm(bank[7][:, 0:T], Vt[:, h * 128:(h + 1) * 128], PT[h % 2][:, 0:256], True, False)
            tk_o[h] = PE.mark(mm(bank[7][:, 128:T], Vt[:, 2048 + h * 128:2048 + (h + 1) * 128],
                                 PT[h % 2][:, 256:384], False, True))

        def st_gate(h):
            tk_g[h] = free[7] = V_("tt", gt[h % 2], bank[7][:, 0:T], blk(Z, h), ALU.mult,
                                   w=[tk_o[h], prev(tk_h, h - 2), t_z])
            rdy[h] = halves(gt[h % 2], blk(XH, h), blk(XL, h), w=[tk_g[h], tk_o[h]])
            tk_h[h] = rdy[h]

        nc.scalar.preload_act_table_set("natural_log_exp_and_others")
        pipe(16, [st_scores, st_max, st_exp, st_norm, st_turn, st_copy, st_pv, st_gate], gen, 4)
        go(gen)
        dump("cos", cos)
        dump("qn", qn[:, :])
        dump("V", Vt)

        def ev_res(D):
            def ev(n, ps, tk):
                t = V_("stt", blk(D, n), blk(X, n), ALPHA, ps, ALU.mult, ALU.add, w=[tk])
                if n == 0:
                    V("copy", acc[:, :], blk(D, 0))
                else:
                    V("tt", acc[:, :], acc[:, :], blk(D, n), ALU.add)
                return t
            return ev

        def layer_norm(layer, D, SQ, gain):
            tk = total(acc, [DV.last()])
            V("ts", mu[:, :], bank[4][:, 0:T], -1.0 / DM, None, ALU.mult, w=[tk])
            free[4] = DV.last()
            toks = []
            m3_ = mu[:, :].rearrange("p (o t) -> p o t", o=1).broadcast_to([128, 4, T])
            for q in range(4):
                s = slice(q * 1024, (q + 1) * 1024)
                d4 = D[:, s].rearrange("p (c t) -> p c t", c=4)
                t = V_("tt", d4, d4, m3_, ALU.add, w=[DV.last()] if q == 0 else [])
                toks.append(A_(SQ[:, s], D[:, s], ACT.Square, w=[t]))
            PE.wait(free[4])
            for k in range(16):
                PE.wait(toks[k // 4])
                ins = mm(bank[4][:, 0:T], ones, blk(SQ, k), k == 0, k == 15)
            tk = PE.mark(ins)
            t = free[4] = rstd(mu[:, :], bank[4][:, 0:T], DM, 0, w=[tk, DV.last()])
            ow, ob = PCOL["ln_w"][0] + 16 * layer, PCOL["ln_b"][0] + 16 * layer
            ready, th = {}, {}
            AC.wait(PE.last())
            for k in range(18):
                if k < 16:
                    t2 = V_("stt", blk(D, k), blk(D, k), pv[:, ow + k:ow + k + 1], mu[:, :], ALU.mult, ALU.mult,
                            w=[t])
                    t3 = A_(blk(X, k), blk(D, k), ACT.Identity, bias=pv[:, ob + k:ob + k + 1], w=[t2])
                    if gain is None:
                        th[k] = A_(blk(XH, k), blk(D, k), ACT.Identity, bias=pv[:, ob + k:ob + k + 1])
                    else:
                        og = PCOL[gain][0]
                        th[k] = A(blk(XH, k), blk(X, k), ACT.Copy, scale=pv[:, og + k:og + k + 1])
                j = k - 2
                if j >= 0:
                    hi = blk(XH, j).bitcast(F32)
                    if gain is None:
                        ready[j] = V_("tt", blk(XL, j), blk(X, j), hi, ALU.subtract, w=[th[j]])
                    else:
                        ready[j] = V_("stt", blk(XL, j), blk(X, j), pv[:, og + j:og + j + 1], hi, ALU.mult,
                                      ALU.subtract, w=[th[j]])
            return ready

        go(proj(16, XH, XL, 16, ev_res(ar(0, 4096)), ko=KO, rdy=rdy))
        rdy = layer_norm(0, ar(0, 4096), ar(4096, 4096), None)
        dump("x1", X[:, :])

        QK, Vm, O, HN = ar(0, 4096), ar(4096, 4096), ar(8192, 4096), ar(12288, 4096)
        E8 = AR[0:8, 15360:16384]
        GR = AR[0:8, 20992:21504]
        AC.wait(DV.last())
        nc.scalar.dma_start(E8, dr["late"][0:8, 766:1790]).then_inc(s_E, 16)
        ocw, ocb = PCOL["conv_w"][0], PCOL["conv_b"][0]

        def ev_conv(n, ps, tk):
            y = blk(QK, n)
            cw = lambda i: pv[:, ocw + 16 * i + n:ocw + 16 * i + n + 1]
            V_("ts", y, ps, cw(3), pv[:, ocb + n:ocb + n + 1], ALU.mult, ALU.add, w=[tk])
            for s in (1, 2, 3):
                t = V("stt", y[:, s:T], ps[:, 0:T - s], cw(3 - s), y[:, s:T], ALU.mult, ALU.add)
            A_(y, y, ACT.Silu, w=[t])
            return t

        go(proj(16, XH, XL, 16, ev_conv, ko=KO, rdy=rdy))
        t_qk = AC.last()

        gtm = [AR[:, 12288 + 16 * i:12304 + 16 * i] for i in range(2)]
        go(proj_tm(1, XH, XL, 16, 16, lambda n, tb, ps, tk: V_("copy", gtm[tb], ps[:, 0:16], w=[tk])))
        vp = proj_tm(4, XH, XL, 16, 512, lambda n, tb, ps, tk:
                     A_(Vm[:, tb * 2048 + n * 512:tb * 2048 + (n + 1) * 512], ps[:, :], ACT.Copy, w=[tk]))
        go(vp, 1)
        PE.wait(DV.last(), free[5])
        for i in range(2):
            for tb in range(2):
                ins = nc.tensor.transpose(bank[5][0:8, i * T + tb * 128:i * T + (tb + 1) * 128],
                                          gtm[tb][:, 8 * i:8 * i + 8], ident)
        tk = PE.mark(ins)
        ip, fp, ab, e1, lf, Fc, ai, Mx, one8 = (AR[0:8, 12544 + i * T:12544 + (i + 1) * T] for i in range(9))
        oib, ofb = PCOL["ib"][0], PCOL["fb"][0]
        nc.scalar.preload_act_table_set("natural_log_exp_and_others")
        V("ts", ip, bank[5][0:8, 0:T], pv[0:8, oib:oib + 1], None, ALU.add, w=[tk])
        V("ts", fp, bank[5][0:8, T:2 * T], pv[0:8, ofb:ofb + 1], None, ALU.add)
        free[5] = DV.last()
        V("stt", ab, fp, -1.0, fp, ALU.mult, ALU.min)
        A(e1, ab, ACT.Exp, w=[DV.last()])
        t = A(e1, e1, ACT.Ln, bias=cst[0:8, CCOL["ones"][0]:CCOL["ones"][0] + 1])
        go(vp, 1)
        V("ts", lf, fp, 0.0, None, ALU.min)
        V("tt", lf, lf, e1, ALU.subtract, w=[t])
        V("memset", one8, 1.0)
        V("scan", Fc, one8, lf, 0.0, ALU.mult, ALU.add)
        V("tt", ai, ip, Fc, ALU.subtract)
        V("scan", Mx, ai, ai, 0.0, ALU.max, ALU.max)
        V("ts", GR[:, 0:T], Mx, -1.0, None, ALU.mult)
        t_gr = V("tt", GR[:, T:2 * T], GR[:, 0:T], Fc, ALU.subtract)
        go(vp, 2)
        PE.wait(t_gr, free[5])
        nc.tensor.transpose(bank[5][:, 0:8], ai[:, 0:128], ident[0:8, 0:8])
        tk = PE.mark(nc.tensor.transpose(bank[5][:, 8:16], ai[:, 128:256], ident[0:8, 0:8]))
        aT = small[:, 0:16]
        t_aT = free[5] = V("copy", aT, bank[5][:, 0:16], w=[tk])
        go(vp)
        t_v = AC.last()

        dk = float(128 ** -0.5)
        Dt = [ar(16384 + 384 * i, 384) for i in range(2)]
        At = [ar(17152 + 384 * i, 384) for i in range(2)]
        cap = [ar(17920 + 256 * i, 256) for i in range(4)]
        rcp = [ar(18944 + 256 * i, 256) for i in range(2)]
        sqh = [ar(19456 + 512 * i, 512) for i in range(2)]
        rsh = [ar(20480 + 256 * i, 256) for i in range(2)]
        t0, t1, t2, t3, t4, t5, t6, t7, t8 = ({} for _ in range(9))
        mC = C("mC")

        def m0(h):
            PE.wait(free[3], t_gr, (s_E, 16))
            t0[h] = PE.mark(mm(bank[3][:, 0:512], E8[:, 128 * h:128 * (h + 1)], GR, True, True))

        def m1(h):
            D = Dt[h % 2]
            PE.wait(free[4], t_qk, t_v)
            q, k = blk(QK, h), blk(QK, 8 + h)
            mm(bank[4][:, 0:256], k[:, 0:128], q, True, True)
            t1[h] = PE.mark(mm(bank[4][:, 256:384], k[:, 128:256], q[:, 128:256], True, True))
            V_("tt", D[:, 0:256], bank[3][:, 0:256], mC, ALU.add, w=[t0[h]])
            t2[h] = V_("tt", D[:, 256:384], bank[3][:, 128:256], mC[:, 0:128], ALU.add)
            A_(D[:, 0:256], D[:, 0:256], ACT.Exp, bias=aT[:, h:h + 1], w=[t2[h], t_aT])
            A_(D[:, 256:384], D[:, 256:384], ACT.Exp, bias=aT[:, 8 + h:9 + h])
            t4[h] = A_(cap[h % 4], bank[3][:, 256:512], ACT.Exp, w=[prev(t6, h - 4)])
            free[3] = t4[h]

        def m3(h):
            t3[h] = free[4] = V_("stt", At[h % 2], bank[4][:, 0:384], dk, Dt[h % 2], ALU.mult, ALU.mult,
                                 w=[t1[h], t4[h], prev(t5, h - 2)])

        def m4(h):
            N, a = bank[5 + h % 2], At[h % 2]
            PE.wait(t3[h], free[5 + h % 2], free[7])
            for c in range(2):
                vo = h * 256 + c * 128
                mm(N[:, c * T:(c + 1) * T], Vm[:, vo:vo + 128], a[:, 0:256], True, False)
                mm(N[:, c * T + 128:(c + 1) * T], Vm[:, 2048 + vo:2048 + vo + 128], a[:, 256:384], False, True)
            mm(bank[7][:, 0:T], ones, a[:, 0:256], True, False)
            t5[h] = PE.mark(mm(bank[7][:, 128:T], ones, a[:, 256:384], False, True))

        def m5(h):
            r, hv = rcp[h % 2], HN[:, 512 * h:512 * (h + 1)]
            V_("tt", r, bank[7][:, 0:T], cap[h % 4], ALU.max, w=[t5[h]])
            t6[h] = free[7] = V("stt", r, bank[7][:, 0:T], -1.0, r, ALU.mult, ALU.max)
            V("recip", r, r)
            free[5 + h % 2] = V("tt", hv.rearrange("p (c t) -> p c t", c=2),
                                bank[5 + h % 2][:, :].rearrange("p (c t) -> p c t", c=2),
                                r.rearrange("p (o t) -> p o t", o=1).broadcast_to([128, 2, T]), ALU.mult)
            t7[h] = A_(sqh[h % 2], hv, ACT.Square, w=[DV.last(), prev(t8, h - 2)])

        def m6(h):
            PE.wait(t7[h], free[2])
            mm(bank[2][:, 0:T], ones, sqh[h % 2][:, 0:T], True, False)
            t8[h] = PE.mark(mm(bank[2][:, 0:T], ones, sqh[h % 2][:, T:2 * T], False, True))

        def m7(h):
            t = free[2] = rstd(rsh[h % 2], bank[2][:, 0:T], 256, 0, w=[t8[h], DV.last()])
            on = PCOL["head_norm"][0] + 2 * h
            for c in range(2):
                hb = HN[:, 512 * h + c * T:512 * h + (c + 1) * T]
                V_("stt", hb, hb, pv[:, on + c:on + c + 1], rsh[h % 2], ALU.mult, ALU.mult, w=[t])

        def ev_o(n, ps, tk):
            t = A_(blk(O, n), ps, ACT.Exp, scale=-1.0, w=[tk])
            V_("ts", blk(O, n), blk(O, n), 1.0, None, ALU.add, w=[t])
            return t

        BIG[:] = [0, 1]
        op_ = proj(16, XH, XL, 16, ev_o)
        DV.wait(PE.last())
        pipe(8, [m0, m1, m3, m4, m5, m6, m7], op_, 5)
        go(op_)
        BIG[:] = [0, 1, 2]
        dump("HN", HN)
        dump("O", O)

        HH, HL = ar_r("HH", 0, 4096), ar_r("HL", 4096, 4096)
        ez = [ar(16384 + 256 * i, 256) for i in range(3)]
        hz = [ar(17152 + 256 * i, 256) for i in range(3)]
        rdy, tq = {}, {}

        def ev_z(n, ps, tk):
            e, h_ = ez[n % 3], hz[n % 3]
            t = A_(e, ps, ACT.Exp, scale=-1.0, w=[tk, prev(tq, n - 3)])
            V("stt", e, e, 1.0, blk(O, n), ALU.add, ALU.mult, w=[t])
            V("recip", e, e)
            r = V("tt", h_, ps, e, ALU.mult, w=[prev(rdy, n - 3)])
            tq[n] = V("tt", h_, h_, blk(HN, n), ALU.mult)
            rdy[n] = halves(h_, blk(HH, n), blk(HL, n), w=[tq[n]])
            return r

        AC.wait(DV.last(), PE.last())
        DV.wait(PE.last(), AC.last())
        go(proj(16, XH, XL, 16, ev_z))
        go(proj(16, HH, HL, 16, ev_res(ar(8192, 4096)), ko=KO, rdy=rdy))
        rdy = layer_norm(1, ar(8192, 4096), ar(12288, 4096), "norm_mix")
        dump("x2", X[:, :])

        MIX = ar(0, 4096)
        QZ, RAW, BT, VSW, DVt, DQ, DK = (ar(4096, 2048), ar(6144, 2048), ar(8192, 2048), ar(10240, 512),
                                         ar(10752, 1024), ar(11776, 2048), ar(13824, 1024))
        WK = 14848
        U_, CV, sgt, sgu = ar(WK, 1024), ar(WK + 1024, 1024), ar(WK + 2048, 1024), ar(WK + 4096, 1536)
        kcn, vc, GX, GA, sqk, ge, rsP, rsT = (ar(WK + 6080, 16), AR[0:15, WK + 6096:WK + 6224],
                                              ar(WK + 6224, 48), ar(WK + 6272, 48), ar(WK + 6320, 16),
                                              ar(WK + 6336, 32), ar(WK + 6368, 256), ar(WK + 6624, 2))
        SQ2 = ar(8192, 4096)
        AC.wait(DV.last(), PE.last())
        DV.wait(AC.last(), PE.last())
        for q in range(4):
            s = slice(q * 1024, (q + 1) * 1024)
            t = A_(SQ2[:, s], X[:, s], ACT.Square, w=[AC.last()])
        t_acc = V("red", acc[:, :], SQ2.rearrange("p (c t) -> p t c", c=16), AX, ALU.add, w=[t])
        t_rs = {}

        def pre_rs():
            tk = total(acc, [t_acc])
            free[4] = t_rs[0] = rstd(rsP, bank[4][:, 0:T], DM, 0, w=[tk])
            DV.wait(t_rs[0])

        hot = ar(11776 + 512, 766)
        rv = AR[0:8, 13824:13824 + 383]
        BR = ar(WK, 2048)

        def band_out():
            AC.wait(t_acc)
            nc.scalar.dma_start(hot[0:32, :], dr["late"][:, 0:766]).then_inc(s_oh, 16)
            nc.scalar.dma_start(sgu, dr["sgu"][:, :]).then_inc(s_sgu, 16)
            PE.wait((s_oh, 16), free[5])
            tk = PE.mark(mm(bank[5][0:8, 0:383], P("table", 32), hot[0:32, 0:383], True, True))
            t = free[5] = V("tt", rv, bank[5][0:8, 0:383], hot[0:8, 383:766], ALU.add, w=[tk, (s_oh, 16)])
            SP.wait(t)
            nc.sync.dma_start(dr["rv"][:, :], rv).then_inc(s_rv, 16)

        def band_in():
            SP.wait((s_rv, 16))
            DV.wait((s_rv, 16))
            band = bass.AP(dr["rv"].tensor, 0, [[1, 128], [383, 8], [1, 256]])
            nc.sync.dma_start(BR.rearrange("p (h k) -> p h k", h=8), band).then_inc(s_bt, 16)

        def band_turn():
            PE.wait((s_bt, 16), t_acc)
            for i in range(4):
                b = 5 + i % 2
                PE.wait(free[b])
                tk = PE.mark(mm(bank[b][:, :], C("J"), BR[:, 512 * i:512 * (i + 1)], True, True))
                free[b] = V_("copy", BT[:, 512 * i:512 * (i + 1)], bank[b][:, :], w=[tk])

        p1_ = proj(8, XH, XL, 16, lambda n, ps, tk: V_("tt", blk(RAW, n), ps, rsP, ALU.mult, w=[tk]),
                   ko=KO, rdy=rdy, pre=pre_rs)
        go(p1_, 16)
        band_out()
        go(p1_, 8)
        band_in()
        go(p1_)

        PE.wait(t_rs[0], free[7])
        nc.tensor.transpose(bank[7][:, 0:128], rsP[:, 0:128], ident)
        tk = PE.mark(nc.tensor.transpose(bank[7][:, 128:256], rsP[:, 128:256], ident))
        free[7] = t_rst = V("copy", rsT, bank[7][:, 0:256:128], w=[tk])
        AC.wait(t_rst)

        def ev_vsw(n, tb, ps, tk):
            V_("ts", VSW[:, tb * 256:(tb + 1) * 256], ps[:, 0:256], rsT[:, tb:tb + 1], None, ALU.mult, w=[tk])
            return V_("ts", GA[:, tb * 24:(tb + 1) * 24], ps[:, 256:280], rsT[:, tb:tb + 1], None, ALU.mult)

        pvs = proj_tm(1, XH, XL, 16, 280, ev_vsw)
        go(pvs, 2)
        band_turn()
        go(pvs)
        A(GA, GA, ACT.Exp, scale=-1.0, w=[DV.last()])
        V("ts", GA, GA, 1.0, None, ALU.add, w=[AC.last()])
        V("recip", GA, GA)
        gx3 = GX.rearrange("p (h s) -> p h s", s=6)
        ga3 = [GA[:, tb * 24:(tb + 1) * 24].rearrange("p (h s) -> p h s", s=3) for tb in range(2)]
        for tb, c in ((1, 0), (0, 2)):
            for j in range(2):
                V("copy", gx3[:, :, c + j], ga3[tb][:, :, 1 + j])
        V("copy", gx3[:, :, 4], ga3[1][:, :, 0])
        orv = CCOL["rowv"][0]
        V("ts", gx3[:, :, 5], ga3[0][:, :, 0], cst[:, orv:orv + 1], None, ALU.mult)

        obones = C("bones")
        ksn, kwn = blk(RAW, 6), blk(RAW, 7)
        sq6, rs6 = ar(WK + 2048, 512), ar(WK + 2560, 512)
        V("memset", QZ, 0.0)
        tt_ = None
        t_gelu = {}

        def ev_u(n, ps, tk):
            r = V_("tt", U_[:, n * T:(n + 1) * T], ps, rsP, ALU.mult, w=[tk, (s_bt, 16), t_bt])
            t_gelu[n] = r
            return r

        t_bt = PE.last()
        up = proj(4, XH, XL, 16, ev_u)
        for pr in (0, 2, 6):
            t = A(sq6, RAW[:, pr * T:(pr + 2) * T], ACT.Square, w=[tt_, DV.last()])
            go(up, 1)
            PE.wait(t, free[7])
            tt_ = PE.mark(mm(bank[7][:, :], obones, sq6, True, True))
            t = free[7] = rstd(rs6, bank[7][:, :], 64, 0, w=[tt_, DV.last()])
            go(up, 1)
            for j in range(2):
                n = pr + j
                src = blk(RAW, n)
                if n < 4:
                    og = PCOL["q_gain"][0]
                    for g in range(2):
                        sl = slice(64 * g, 64 * g + 64)
                        V("stt", QZ[sl, (n + 4 * g) * T:(n + 4 * g + 1) * T], src[sl, :], pv[sl, og:og + 1],
                          rs6[sl, j * T:(j + 1) * T], ALU.mult, ALU.mult, w=[t])
                else:
                    og = PCOL["k_gain"][0]
                    V("stt", src, src, pv[:, og:og + 1], rs6[:, j * T:(j + 1) * T], ALU.mult, ALU.mult, w=[t])

        zb = [ar(WK + 2048, 480), ar(WK + 2560, 480)]
        for i in range(2):
            src = blk(RAW, 4 + i)
            win = bass.AP(src.tensor, src.offset, [list(src.ap[0]), [1, 32], [16, 15]])
            opos = PCOL["cmp_pos"][0] + 32 * i
            posb = pv[:, opos:opos + 32].rearrange("p (l o) -> p l o", o=1).broadcast_to([128, 32, 15])
            V("tt", zb[i].rearrange("p (l n) -> p l n", l=32), win, posb, ALU.add, w=[PE.last()])
        t_zb = DV.last()
        go(up)
        A(U_, U_, ACT.Gelu_apprx_tanh, w=[DV.last()])
        go(proj_tm(1, XH, XL, 16, 512, lambda n, tb, ps, tk:
                   A_(CV[:, tb * 512:(tb + 1) * 512], ps[:, :], ACT.Gelu_apprx_tanh, scale=rsT[:, tb:tb + 1],
                      w=[tk, t_bt])))
        t_cv = AC.last()
        PE.wait(t_zb, free[7])
        for i in range(2):
            for l in range(32):
                ins = mm(bank[7][:, 16 * i:16 * i + 15], take(), zb[i][:, 15 * l:15 * l + 15], l == 0, l == 31)
                tu = used(ins)
        tk = tu or PE.mark(ins)
        for i in range(2):
            A(ge[:, 16 * i:16 * i + 15], bank[7][:, 16 * i:16 * i + 15], ACT.Gelu_apprx_tanh, w=[tk])
        free[7] = t = AC.last()
        nc.scalar.preload_act_table_set("natural_log_exp_and_others")
        wk_ = take()
        PE.wait(t, free[7])
        used(mm(bank[7][:, 0:15], wk_, ge[:, 0:15], True, True))
        ins = mm(bank[7][0:15, 128:256], ge[:, 16:31], take(), True, True)
        tk_kc = used(ins) or PE.mark(ins)

        V("memset", DQ, 0.0)

        def ev_d(n, ps, tk):
            if n >= 4:
                return V_("tt", DK[:, (n - 4) * T:(n - 3) * T], ps, rsP, ALU.mult, w=[tk])
            for half in range(2):
                sl = slice(64 * half, 64 * half + 64)
                h = 2 * n + half
                r = V_("tt", DQ[sl, h * T:(h + 1) * T], ps[sl, :], rsP[sl, :], ALU.mult, w=[tk])
            return r

        dp = proj(8, XH, XL, 16, ev_d)
        kcn_, sqk_ = kcn[:, 0:15], sqk[:, 0:15]
        V("copy", vc, bank[7][0:15, 128:256], w=[tk_kc])
        V("copy", kcn_, bank[7][:, 0:15])
        t = A(sqk_, kcn_, ACT.Square, w=[DV.last()])
        go(dp, 2)
        PE.wait(t, DV.last())
        tk = PE.mark(mm(bank[7][:, 256:271], obones, sqk_, True, True))
        t = free[7] = rstd(sqk_, bank[7][:, 256:271], 64, 0, w=[tk])
        og = PCOL["k_gain"][0]
        t_kc = V("stt", kcn_, kcn_, pv[:, og:og + 1], sqk_, ALU.mult, ALU.mult, w=[t])

        for tb in range(2):
            st_ = small[:, 16 * tb:16 * tb + 6]
            mv = small[:, 16 * tb + 8:16 * tb + 10]
            v = CV[:, tb * 512:(tb + 1) * 512]
            V("bns", st_, v, w=[t_cv])
            V("bna", mv, st_)
            rstd(mv[:, 1:2], mv[:, 1:2], 1, 1, w=[DV.last()])
            V("ts", v, v, mv[:, 0:1], mv[:, 1:2], ALU.subtract, ALU.mult, w=[AC.last()])
        otr = CCOL["tril"][0]
        sgw = sgu[:, 0:1024]
        sg3 = sgw.rearrange("p (h q) -> p h q", h=8)
        t = V("tt", sg3, sg3, cst[:, otr:otr + 128].rearrange("p (o q) -> p o q", o=1).broadcast_to([128, 8, 128]),
              ALU.mult, w=[(s_sgu, 16)])
        for j in range(4):
            b = 5 + j % 2
            go(dp, 1)
            PE.wait(t, free[b])
            for c in range(2):
                ins = mm(bank[b][:, c * 256:(c + 1) * 256], CV[:, c * 512 + j * 128:c * 512 + (j + 1) * 128],
                         sgw[:, j * 256:(j + 1) * 256], True, True)
            tk = PE.mark(ins)
            ps3 = bank[b][:, :].rearrange("p (c q) -> p c q", c=2)
            d3 = sgt[:, j * T:(j + 1) * T].rearrange("p (c q) -> p c q", c=2)
            for half in range(2):
                sl = slice(64 * half, 64 * half + 64)
                bias = sgu[sl, 1024 + 128 * j:1024 + 128 * (j + 1)].rearrange("p (o q) -> p o q", o=1)
                free[b] = V_("tt", d3[sl], ps3[sl, :, 128 * half:128 * half + 128], bias.broadcast_to([64, 2, 128]),
                             ALU.add, w=[tk])
            V("tt", blk(MIX, 4 + j), sgt[:, j * T:(j + 1) * T], U_[:, j * T:(j + 1) * T], ALU.mult)
        go(dp)
        go(proj_tm(1, XH, XL, 16, 512, lambda n, tb, ps, tk:
                   V_("ts", DVt[:, tb * 512:(tb + 1) * 512], ps[:, :], rsT[:, tb:tb + 1], None, ALU.mult, w=[tk])))
        t_d = DV.last()
        dump("MIXc", MIX[:, 1024:2048])
        dump("QZ", QZ)

        bg, ztmp = RAW[:, 0:1024], blk(RAW, 4)
        o2 = PCOL["conv2"][0]

        def ev_b(n, ps, tk):
            j = n % 4
            if n < 4:
                return V_("tt", bg[:, j * T:(j + 1) * T], ps, rsP, ALU.mult, w=[tk])
            y = blk(MIX, j)
            if n < 8:
                return V_("tt", y, ps, rsP, ALU.mult, w=[tk])
            r = V_("tt", ztmp, ps, rsP, ALU.mult, w=[tk])
            V("tt", ztmp, ztmp, y, ALU.mult)
            cw = lambda i: pv[:, o2 + 4 * i + j:o2 + 4 * i + j + 1]
            V("ts", y, ztmp, cw(2), None, ALU.mult)
            V("stt", y[:, 1:T], ztmp[:, 0:T - 1], cw(1), y[:, 1:T], ALU.mult, ALU.add)
            V("stt", y[:, 2:T], ztmp[:, 0:T - 2], cw(0), y[:, 2:T], ALU.mult, ALU.add)
            V("tt", y, y, bg[:, j * T:(j + 1) * T], ALU.mult)
            return r

        bp = proj(12, XH, XL, 16, ev_b)

        ds = float(64 ** -0.5)
        zA = [ar(WK + 384 * i, 384) for i in range(4)]
        lA = [ar(WK + 1536 + 384 * i, 384) for i in range(4)]
        eA = [ar(WK + 3072 + 384 * i, 384) for i in range(2)]
        mS = C("mS")
        g1, g2, g3, g4, g5, g6 = ({} for _ in range(6))

        def d0(h):
            S = bank[3 + h % 2]
            PE.wait(free[3 + h % 2], t_d)
            q, k = blk(DQ, h), blk(DK, h // 2)
            mm(S[:, 0:256], k[:, 0:128], q, True, True)
            g1[h] = PE.mark(mm(S[:, 256:384], k[:, 128:256], q[:, 128:256], True, True))

        def d1(h):
            S, z, e = bank[3 + h % 2], zA[h % 4], eA[h % 2]
            A_(z, S[:, 0:384], ACT.Copy, scale=ds, w=[g1[h]])
            free[3 + h % 2] = A_(e, S[:, 0:384], ACT.Abs, scale=ds, w=[prev(g3, h - 2)])
            A(e, e, ACT.Exp, scale=-1.0)
            g2[h] = A(e, e, ACT.Ln, bias=ones[:, 0:1])

        def d2(h):
            z, e, l = zA[h % 4], eA[h % 2], lA[h % 4]
            V_("stt", e, z, 0.0, e, ALU.max, ALU.add, w=[g2[h]])
            V("tt", z, z, e, ALU.subtract)
            g3[h] = V_("stt", l, e, -1.0, mS, ALU.mult, ALU.mult, w=[prev(g5, h - 4)])

        def d3_(h):
            l = lA[h % 4]
            PE.wait(free[5], g3[h])
            mm(bank[5][:, 0:256], C("U"), l[:, 0:256], True, False)
            mm(bank[5][:, 128:256], ones, l[:, 256:384], False, True)
            g4[h] = PE.mark(mm(bank[5][:, 256:384], C("U"), l[:, 256:384], True, True))

        def d4(h):
            z, a = zA[h % 4], lA[h % 4]
            free[5] = V_("tt", z, z, bank[5][:, 0:384], ALU.add, w=[g4[h]])
            t = A_(a, z, ACT.Exp, w=[DV.last()])
            g6[h] = V_("tt", a, a, mS, ALU.mult, w=[t])

        def d5(h):
            a, j = lA[h % 4], h // 2
            PE.wait(free[6 + h % 2], g6[h])
            Ob = bank[6 + h % 2]
            mm(Ob[:, 0:256], DVt[:, j * 128:(j + 1) * 128], a[:, 0:256], True, False)
            g5[h] = PE.mark(mm(Ob[:, 128:256], DVt[:, 512 + j * 128:512 + (j + 1) * 128], a[:, 256:384], False,
                               True))

        def d6(h):
            sl = slice(64 * (h % 2), 64 * (h % 2) + 64)
            free[6 + h % 2] = V_("copy", MIX[sl, (8 + h // 2) * T:(9 + h // 2) * T], bank[6 + h % 2][sl, 0:256],
                                 w=[g5[h]])

        AC.wait(DV.last(), PE.last())
        DV.wait(AC.last(), PE.last())
        pipe(8, [d0, d1, d2, d3_, d4, d5, d6], bp, 2)

        SX = [ar(WK + 1024 * i, 512) for i in range(4)]
        SY = [ar(WK + 1024 * i + 512, 256) for i in range(4)]
        SC = [ar(WK + 1024 * i + 768, 32) for i in range(4)]
        PA = [ar(11776 + 768 * i, 768) for i in range(2)]
        PC = [AR[0:15, 13824 + 256 * i:13824 + 256 * (i + 1)] for i in range(2)]
        nm = [small[:, 8 * i:8 * i + 6] for i in range(4)]
        sm = [small[:, 32 + 8 * i:32 + 8 * i + 6] for i in range(4)]
        n1, n2, n3, n4, n5, n6, n7 = ({} for _ in range(7))

        def seg(h):
            i = h % 4
            return [SX[i][:, 0:256], SX[i][:, 256:512], SY[i][:, 0:128], SY[i][:, 128:256],
                    SC[i][:, 0:15], SC[i][:, 16:23]]

        def a0(h):
            X1, Y1 = bank[3], bank[4]
            PE.wait(free[3], free[4], t_kc)
            q = blk(QZ, h)
            mm(X1[:, 0:256], q[:, 128:256], ksn, True, True)
            mm(X1[:, 256:512], q[:, 128:256], kwn, True, True)
            mm(Y1[:, 0:128], q[:, 0:128], ksn[:, 0:128], True, True)
            mm(Y1[:, 128:256], q[:, 0:128], kwn[:, 0:128], True, True)
            mm(Y1[:, 256:271], q[:, 128:256], kcn_, True, True)
            n1[h] = PE.mark(mm(Y1[:, 272:279], q[:, 0:128], kcn_[:, 0:7], True, True))

        def a1(h):
            i = h % 4
            X1, Y1 = bank[3], bank[4]
            bt = BT[:, h * 256:(h + 1) * 256]
            r2 = lambda ap, n: ap.rearrange("p (s k) -> p s k", s=n)
            V_("stt", r2(SX[i], 2), r2(X1[:, 0:512], 2), ds, r2(bt, 1).broadcast_to([128, 2, 256]), ALU.mult,
               ALU.add, w=[n1[h], prev(n5, h - 4)])
            V_("stt", r2(SY[i], 2), r2(Y1[:, 0:256], 2), ds, r2(bt[:, 128:256], 1).broadcast_to([128, 2, 128]),
               ALU.mult, ALU.add)
            V_("stt", SC[i][:, 0:15], Y1[:, 256:271], ds, bt[:, 31:256:16], ALU.mult, ALU.add)
            V_("stt", SC[i][:, 16:23], Y1[:, 272:279], ds, bt[:, 128 + 31:256:16], ALU.mult, ALU.add)
            free[3] = free[4] = DV.last()
            m = nm[i]
            V("red", m[:, 0:2], r2(SX[i], 2), AX, ALU.max)
            V_("red", m[:, 2:4], r2(SY[i], 2), AX, ALU.max)
            V_("red", m[:, 4:5], SC[i][:, 0:15], AX, ALU.max)
            V_("red", m[:, 5:6], SC[i][:, 16:23], AX, ALU.max)
            n2[h] = V("ts", m, m, -1.0, None, ALU.mult)

        def a2(h):
            i = h % 4
            for s, ap in enumerate(seg(h)):
                n3[h] = A_(ap, ap, ACT.Exp, bias=nm[i][:, s:s + 1], accum_out=sm[i][:, s:s + 1], w=[n2[h]])

        def a3(h):
            i = h % 4
            V("recip", sm[i], sm[i], w=[n3[h]])
            V("tt", sm[i], sm[i], GX[:, 6 * h:6 * h + 6], ALU.mult)
            V("ts", SC[i][:, 0:15], SC[i][:, 0:15], sm[i][:, 4:5], None, ALU.mult)
            for s, ap in enumerate(seg(h)):
                if s != 4:
                    n4[h] = V_("ts", ap, ap, sm[i][:, s:s + 1], None, ALU.mult)

        def a4(h):
            i = h % 4
            PE.wait(free[5], free[6], n4[h])
            for s, B in ((0, bank[5]), (1, bank[6])):
                nc.tensor.transpose(B[:, 0:128], SY[i][:, s * 128:(s + 1) * 128], ident)
                nc.tensor.transpose(B[:, 128:256], SX[i][:, s * 256:s * 256 + 128], ident)
                nc.tensor.transpose(B[:, 256:384], SX[i][:, s * 256 + 128:s * 256 + 256], ident)
            nc.tensor.transpose(bank[5][0:7, 384:512], SC[i][:, 16:23], ident)
            n5[h] = PE.mark(nc.tensor.transpose(bank[6][0:15, 384:512], SC[i][:, 0:15], ident))

        def a5(h):
            i = h % 2
            A_(PA[i][:, 0:384], bank[5][:, 0:384], ACT.Copy, w=[n5[h], prev(n6, h - 2)])
            free[5] = A_(PC[i][0:7, 0:128], bank[5][0:7, 384:512], ACT.Copy)
            A_(PA[i][:, 384:768], bank[6][:, 0:384], ACT.Copy)
            n7[h] = free[6] = A_(PC[i][0:15, 128:256], bank[6][0:15, 384:512], ACT.Copy)

        def a6(h):
            i = h % 2
            Ob = bank[7]
            PE.wait(free[7], n7[h])
            mm(Ob[:, 0:256], VSW[:, 0:128], PA[i][:, 0:256], True, False)
            mm(Ob[:, 128:256], VSW[:, 256:384], PA[i][:, 256:384], False, False)
            mm(Ob[:, 0:256], VSW[:, 128:256], PA[i][:, 384:640], False, False)
            mm(Ob[:, 128:256], VSW[:, 384:512], PA[i][:, 640:768], False, False)
            mm(Ob[:, 0:128], vc[0:7, :], PC[i][0:7, 0:128], False, False)
            n6[h] = PE.mark(mm(Ob[:, 128:256], vc[0:15, :], PC[i][0:15, 128:256], False, True))

        def a7(h):
            g = h // 4
            sl = slice(64 * g, 64 * g + 64)
            free[7] = V_("copy", MIX[sl, (12 + h % 4) * T:(13 + h % 4) * T], bank[7][sl, 0:256], w=[n6[h]])

        AC.wait(PE.last(), DV.last())
        DV.wait(AC.last(), PE.last())
        pipe(8, [a0, a1, a2, a3, a4, a5, a6, a7], bp, 2)
        go(bp)
        dump("MIX", MIX)

        og = PCOL["group_gain"][0]
        AC.wait(DV.last(), PE.last())
        rdy = {}
        tsum = None
        for g in range(4):
            sq = ar(WK + 1024 * (g % 2), 1024)
            t = A(sq, MIX[:, g * 1024:(g + 1) * 1024], ACT.Square, w=[DV.last()])
            ac_, rs_ = ar(WK + 2048 + 256 * g, 256), ar(WK + 3072 + 256 * g, 256)
            t = V("red", ac_, sq.rearrange("p (c t) -> p t c", c=4), AX, ALU.add, w=[t])
            tk = total(ac_, [t])
            t = free[4] = rstd(rs_, bank[4][:, 0:T], 512, 0, w=[tk])
            for k in range(4 * g, 4 * g + 4):
                t2 = V_("stt", blk(MIX, k), blk(MIX, k), pv[:, og + k:og + k + 1], rs_, ALU.mult, ALU.mult, w=[t])
                rdy[k] = halves(blk(MIX, k), blk(XH, k), blk(XL, k), w=[t2])
        FH, FL = ar_r("FH", 11264, 4096), ar_r("FL", 15360, 4096)
        sqx = [ar(19456 + 256 * i, 256) for i in range(2)]
        rsF = ar(21248, 256)
        onf = PCOL["norm_ffn"][0]
        tsx, rdf = {}, {}
        DV.wait(PE.last(), AC.last())

        def ev_x3(n, ps, tk):
            r = V_("tt", blk(X, n), blk(X, n), ps, ALU.add, w=[tk])
            A_(sqx[n % 2], blk(X, n), ACT.Square, w=[r, prev(tsx, n - 2)])
            t = AC.last()
            rdf[n] = halves(blk(X, n), blk(FH, n), blk(FL, n), scale=pv[:, onf + n:onf + n + 1])
            if n == 0:
                tsx[n] = V("copy", acc[:, :], sqx[0], w=[t])
            else:
                tsx[n] = V("tt", acc[:, :], acc[:, :], sqx[n % 2], ALU.add, w=[t])
            return r

        AC.wait(DV.last())
        go(proj(16, XH, XL, 16, ev_x3, ko=KO, rdy=rdy))
        dump("x3", X[:, :])

        def pre_rf():
            tk = total(acc, [tsx[15]])
            free[4] = t = rstd(rsF, bank[4][:, 0:T], DM, 0, w=[tk])
            DV.wait(t)
            nc.scalar.preload_act_table(ACT.Silu)

        NB = FFN_HALF
        AH, AL = ar_r("AH", 0, NB * T), ar_r("AL", NB * T, NB * T)
        sg = [ar(19968 + 256 * i, 256) for i in range(2)]
        fu = [ar(20480 + 256 * i, 256) for i in range(3)]
        tsg, tfu, rda = {}, {}, {}

        def ev_f(half):
            def ev(n, ps, tk):
                i = n // 2
                ii = i + NB * half
                if n % 2 == 0:
                    r = V_("tt", sg[i % 2], ps, rsF, ALU.mult, w=[tk])
                    tsg[ii] = A_(sg[i % 2], sg[i % 2], ACT.Silu, w=[r])
                    return r
                u = fu[i % 3]
                r = V_("tt", u, ps, rsF, ALU.mult, w=[tk, prev(tfu, ii - 3)])
                t = V("tt", u, u, sg[i % 2], ALU.mult, w=[tsg[ii]])
                tfu[ii] = rda[i] = halves(u, blk(AH, i), blk(AL, i), w=[t])
                return r
            return ev

        OUT = ar(11264, 4096)
        n_out = [0]

        def ev_down(half):
            def ev(n, ps, tk):
                if half == 0:
                    return V_("tt", blk(X, n), blk(X, n), ps, ALU.add, w=[tk])
                t = V_("tt", blk(OUT, n), blk(X, n), ps, ALU.add, w=[tk])
                AC.wait(t)
                nc.scalar.dma_start(out[:, n * T:(n + 1) * T], blk(OUT, n)).then_inc(s_fin, 16)
                n_out[0] += 1
                return t
            return ev

        for half in range(2):
            AC.wait(PE.last())
            DV.wait(PE.last())
            if half == 0:
                go(proj(2 * NB, FH, FL, 16, ev_f(0), ko=KO, rdy=rdf, pre=pre_rf))
            else:
                go(proj(2 * NB, FH, FL, 16, ev_f(1)))
            go(proj(16, AH, AL, NB, ev_down(half), ko=KO, rdy=rda))
        nc.scalar.wait_ge(s_fin, 16 * n_out[0])
        nc.sync.wait_ge(s_fin, 16 * n_out[0])
        assert st["tile"] == len(tiles)


def pack(inputs):
    w = {k: np.asarray(v) for k, v in inputs.items()}
    tiles = weight_tiles()
    places, kinds = pack_tiles(tiles)
    W = np.zeros((len(kinds) // 2, 128, 2 * HCOLS), np.float32)
    mix = mix_rows()
    mats = {n: w[n].reshape(w[n].shape[-2:]) for n in
            ("mla_w_in", "mla_w_qb", "mla_w_kvb", "mla_w_out", "ml_w_in", "ml_w_out", "w_in_2", "w_out_2",
             "w_ffn_gate_2", "w_ffn_up_2", "w_ffn_down_2")}
    mats["w_out_2"] = mats["w_out_2"][mix]
    w1 = w["cmp_w1_2"].reshape(2, 32, 64, 64)
    w2 = w["cmp_w2_2"].reshape(2, 64, 64)
    for (src, k, cols, kind), (hf, c) in zip(tiles, places):
        u, c = hf // 2, c + HCOLS * (hf % 2)
        if kind == "bd":
            m = w1[k, cols[0]] if src == "cmp_w1_2" else w2[k]
            W[u, 0:64, c:c + 64] = m
            W[u, 64:128, c + 64:c + 128] = m
        elif cols[-1] - cols[0] == len(cols) - 1 and cols[0] + 1 == cols[1]:
            W[u, :, c:c + len(cols)] = mats[src][k:k + 128, cols[0]:cols[0] + len(cols)]
        else:
            W[u, :, c:c + len(cols)] = mats[src][k:k + 128][:, cols]
    pvec = np.zeros((128, NP), np.float32)

    def put(name, a):
        o, n = PCOL[name]
        pvec[:a.shape[0], o:o + a.shape[1]] = a

    def fm(a):
        return a.reshape(-1, 128).T

    put("q_norm", fm(w["mla_q_norm"]))
    put("kv_norm", fm(w["mla_kv_norm"]))
    put("ln_w", fm(w["ln_w"]))
    put("ln_b", fm(w["ln_b"]))
    put("conv_w", fm(w["ml_conv_w"]))
    put("conv_b", fm(w["ml_conv_b"]))
    put("head_norm", fm(w["ml_head_norm"]))
    put("norm_mix", fm(w["norm_mix_2"]))
    put("norm_ffn", fm(w["norm_ffn_2"]))
    for n in ("q_gain", "k_gain"):
        g = w[n + "_2"].reshape(64, 1)
        put(n, np.concatenate([g, g], 0))
    p = w["cmp_pos_2"].reshape(2, 32, 64).transpose(2, 0, 1).reshape(64, 64)
    put("cmp_pos", np.concatenate([p, p], 0))
    put("conv2", fm(w["conv_w_2"]))
    put("group_gain", fm(w["group_gain_2"].reshape(-1)[mix]))
    gb = w["ml_gate_b"].reshape(16, 1)
    put("ib", gb[0:8])
    put("fb", gb[8:16])
    put("table", w["rel_table_2"])
    sgu = np.concatenate([w["sgu_w_2"].reshape(8, 128, 128).transpose(2, 0, 1).reshape(128, 1024),
                          np.repeat(w["sgu_b_2"].reshape(4, 2, 128).transpose(1, 0, 2), 64, axis=0)
                          .reshape(128, 512)], 1)
    cst, late = constants()
    x = w["x"].reshape(T, 16, 128).transpose(2, 1, 0).reshape(128, 4096)
    return {"W": W, "pv": pvec, "cst": cst, "late": late, "sgu": sgu, "x": np.ascontiguousarray(x),
            "pos": np.ascontiguousarray(w["positions"].reshape(1, T).astype(np.int32))}


DUMPS = {}


def kernel(**inputs):
    import concourse.bacc as _bacc
    from concourse.bass_utils import run_bass_kernel_spmd as _run

    nc = _bacc.Bacc("TRN2", target_bir_lowering=False, num_devices=1)
    arrays = pack(inputs)
    dr = {}
    for name, a in arrays.items():
        dr[name] = nc.dram_tensor("in_" + name, a.shape, I32 if name == "pos" else F32, kind="ExternalInput").ap()
    dr["rv"] = nc.dram_tensor("rv", (8, 383), F32, kind="Internal").ap()
    out = nc.dram_tensor("out_0", (128, 4096), F32, kind="ExternalOutput").ap()
    dumps = {k: nc.dram_tensor("dump_" + k, s, F32, kind="ExternalOutput").ap() for k, s in DUMPS.items()}
    build(nc, dr, out, dumps)
    r = _run(nc, [{"in_" + k: a for k, a in arrays.items()}], core_ids=[0])
    y = np.asarray(r.results[0]["out_0"]).reshape(128, 16, T).transpose(2, 1, 0).reshape(1, T, DM)
    return np.ascontiguousarray(y)
```

```python
from contextlib import ExitStack

import numpy as np
import concourse.bass as bass
from concourse import mybir

F32 = mybir.dt.float32
I32 = mybir.dt.int32
FR = mybir.dt.float32r
ALU = mybir.AluOpType
ACT = mybir.ActivationFunctionType
AX = mybir.AxisListType.X

T = 256
DM = 2048
NEG = -1.0e30
EPS = 1e-6
ALPHA = 4.0 ** 0.25
HCOLS = 1024
NRAW = 4
NW = 4
DEFER = 3
LAG = 1
FFN_HALF = 22


KO = 4


def tile_order(n_blocks, nk, ko):
    order = [(b, k) for k in range(nk) for b in range(ko)]
    return order + [(b, k) for b in range(ko, n_blocks) for k in range(nk)]


def weight_tiles():
    tiles = []

    def t_blocks(src, blocks, rows, ko=0, row0=0):
        for b, k in tile_order(len(blocks), rows // 128, ko):
            tiles.append((src, row0 + k * 128, blocks[b], "w"))

    def r(a, n):
        return list(range(a, a + n))

    t_blocks("mla_w_in", [r(128 * b, 128) for b in range(8)] + [r(1024, 64) * 2], DM, KO)
    t_blocks("mla_w_in", [r(1088 + 128 * b, 128) for b in range(16)], DM)
    for g in range(4):
        t_blocks("mla_w_qb", [[192 * (4 * g + i) + 128 + 32 * half + j for i in range(4) for j in range(32)]
                              for half in range(2)], 512)
        t_blocks("mla_w_qb", [r(192 * (4 * g + i), 128) for i in range(4)], 512)
        t_blocks("mla_w_kvb", [r(256 * (4 * g + i), 128) for i in range(4)], 512)
        t_blocks("mla_w_kvb", [[256 * (4 * g + i) + 128 + j for i in range(4) for j in range(128)]], 512)
    t_blocks("mla_w_out", [r(128 * b, 128) for b in range(16)], DM, KO)

    t_blocks("ml_w_in", [r(128 * b, 128) for b in range(16)], DM, KO)
    t_blocks("ml_w_in", [r(6144, 8) * 4 + r(6152, 8)], DM)
    t_blocks("ml_w_in", [r(2048 + 512 * n, 512) for n in range(4)], DM)
    t_blocks("ml_w_in", [r(4096 + 128 * b, 128) for b in range(16)], DM)
    t_blocks("ml_w_in", [r(6160 + 128 * b, 128) for b in range(16)], DM)
    t_blocks("ml_w_out", [r(128 * b, 128) for b in range(16)], DM, KO)

    kv = 512
    t_blocks("w_in_2", [r(64 * i, 64) + r(64 * (4 + i), 64) for i in range(4)] +
             [r(kv + 128 * i, 128) for i in (0, 1, 2, 4)], DM, KO)
    t_blocks("w_in_2", [r(kv + 128 * 3, 128) + r(kv + 128 * 5, 128) + r(1280, 24)], DM)
    b0 = 1304
    c0 = b0 + 1536
    d0 = c0 + 1024
    for b in range(8):
        t_blocks("w_in_2", [r(d0 + 128 * b, 128)], DM)
        for l in range(8 * b, 8 * b + 8):
            tiles.append(("cmp_w1_2", l // 32, [l % 32], "bd"))
    for b in range(4):
        tiles += [("w_in_2", 512 * b + 128 * k, r(d0 + 1024, 512), "w") for k in range(4)]
        if b == 1:
            tiles.append(("cmp_w2_2", 0, [0], "bd"))
            tiles.append(("cmp_w2_2", 1, [0], "bd"))
    t_blocks("w_in_2", [r(c0 + 128 * b, 128) for b in range(4)], DM)
    t_blocks("w_in_2", [r(c0 + 512, 512)], DM)
    t_blocks("w_in_2", [r(b0 + 128 * b, 128) for b in range(12)], DM)
    t_blocks("w_out_2", [r(128 * b, 128) for b in range(16)], DM, KO)
    for half in range(2):
        blocks = []
        for b in range(FFN_HALF * half, FFN_HALF * (half + 1)):
            blocks += [("w_ffn_gate_2", r(128 * b, 128)), ("w_ffn_up_2", r(128 * b, 128))]
        for b, k in tile_order(len(blocks), 16, 0 if half else KO):
            tiles.append((blocks[b][0], k * 128, blocks[b][1], "w"))
        t_blocks("w_ffn_down_2", [r(128 * b, 128) for b in range(16)], 128 * FFN_HALF, KO,
                 128 * FFN_HALF * half)
    return tiles


def tile_width(t):
    return 128 if t[3] == "bd" else len(t[2])


def pack_tiles(tiles):
    places, kinds, c = [], [tiles[0][3]], 0
    for t in tiles:
        w = tile_width(t)
        if c + w > HCOLS or t[3] != kinds[-1]:
            kinds.append(t[3])
            c = 0
        places.append((len(kinds) - 1, c))
        c += w
    if len(kinds) % 2:
        kinds.append("none")
    return places, kinds


def mix_rows():
    rows = []
    for i in range(4):
        rows += list(range(64 * i, 64 * i + 64)) + list(range(64 * (4 + i), 64 * (4 + i) + 64))
    return np.array(list(range(512, 2048)) + rows)


PCOL = {}
_n = 0
for _name, _w in [("q_norm", 4), ("kv_norm", 4), ("ln_w", 32), ("ln_b", 32), ("conv_w", 64), ("conv_b", 16),
                  ("head_norm", 16), ("norm_mix", 16), ("norm_ffn", 16), ("q_gain", 1), ("k_gain", 1),
                  ("cmp_pos", 64), ("conv2", 12), ("group_gain", 16), ("ib", 1), ("fb", 1), ("table", 8)]:
    PCOL[_name] = (_n, _w)
    _n += _w
NP = _n
CCOL = {}
_n = 0
for _name, _w in [("ident", 128), ("bones", 128), ("U", 128), ("mC", 256), ("mS", 384), ("tril", 128),
                  ("R12", 256), ("u", 128), ("v", 128), ("invf", 1), ("rowv", 1), ("ones", 128), ("J", 128),
                  ("eps", 4)]:
    CCOL[_name] = (_n, _w)
    _n += _w
NC_ = _n

def rel_bucket(n):
    n = np.maximum(n, 0)
    nf = np.maximum(n, 1).astype(np.float32)
    large = 16 + (np.log(nf / np.float32(16)) / np.float32(np.log(64.0)) * np.float32(16)).astype(np.int32)
    return np.where(n < 16, n, np.minimum(large, 31))


def constants():
    c = np.zeros((128, NC_), np.float32)

    def put(name, a):
        a = np.asarray(a, np.float32)
        o, w = CCOL[name]
        c[:a.shape[0], o:o + a.shape[1]] = a

    i = np.arange(128)
    put("ident", np.eye(128))
    put("bones", (i[:, None] // 64) == (i[None, :] // 64))
    put("U", i[:, None] > i[None, :])
    put("mC", np.concatenate([np.where(i[:, None] <= i[None, :], 0.0, NEG), np.zeros((128, 128))], 1))
    strict = (i[:, None] < i[None, :]) * 1.0
    put("mS", np.concatenate([strict, np.ones((128, 128)), strict], 1))
    put("tril", i[:, None] <= i[None, :])
    dist = 255 - np.arange(383)
    hot = (np.arange(32)[:, None] == rel_bucket(dist)[None, :]) & (dist >= 0)[None, :]
    late = np.zeros((32, 766 + 1024), np.float32)
    late[:, 0:383] = hot
    late[0:8, 383:766] = np.where(dist >= 0, 0.0, NEG)
    late[0:8, 766:] = np.repeat(np.eye(8), 128, axis=1)
    r12 = np.zeros((64, 256))
    for m in range(128):
        r12[m % 32, m] = 1.0
        r12[32 + m % 32, 128 + m] = 1.0
    put("R12", r12)
    put("u", (i < 64)[None, :])
    put("v", np.where(i >= 64, NEG, 0.0)[None, :])
    f = (np.float64(10000.0) ** (-np.arange(0, 64, 2, dtype=np.float64) / 64)).astype(np.float32)
    put("invf", np.tile(f, 4)[:, None])
    put("rowv", (i >= 31)[:, None])
    put("ones", np.ones((128, 128)))
    put("J", np.eye(128)[::-1])
    put("eps", np.tile([[1e-6, 1e-5, np.pi / 2, 0.0]], (128, 1)))
    return c, late


class Queue:

    def __init__(self, eng, sem):
        self.eng, self.sem, self.n, self.seen = eng, sem, 0, {}

    def wait(self, *toks):
        for t in toks:
            if t is None:
                continue
            if isinstance(t, list):
                self.wait(*t)
                continue
            s, v = t
            if self.seen.get(id(s), 0) < v:
                self.eng.wait_ge(s, v)
                self.seen[id(s)] = v

    def mark(self, ins):
        ins.then_inc(self.sem, 1)
        self.n += 1
        return (self.sem, self.n)

    def last(self):
        return (self.sem, self.n) if self.n else None


class Ahead(dict):

    def __init__(self, work, n):
        super().__init__()
        self.work, self.n, self.made = work, n, 0

    def __getitem__(self, k):
        while self.made <= k + self.n and next(self.work, "end") != "end":
            self.made += 1
        return super().__getitem__(k)


def build(nc, dr, out, dumps):
    with ExitStack() as ctx:
        def sem(name):
            return ctx.enter_context(nc.semaphore(name))

        top = [nc.sbuf_base + 31 & ~31]

        def sb(name, cols, dt=F32, at=None):
            if at is None:
                at = top[0]
                top[0] += -(-4 * cols // 32) * 32
            return nc.alloc_sbuf_tensor_at(name, [128, cols], dt, offset=at)

        pv = sb("pv", NP)
        cst = sb("cst", NC_)
        small = sb("small", 64)
        mu_acc = sb("mu_acc", 2 * T)
        mu, acc = mu_acc[:, 0:T], mu_acc[:, T:2 * T]
        X = sb("X", 4096)
        xh0 = top[0]
        XH = sb("XH", 4096, FR)
        xl0 = top[0]
        XL = sb("XL", 4096, FR)
        raw = sb("raw", NRAW * 2 * HCOLS)
        WH = sb("WH", NW * HCOLS, FR)
        WL = sb("WL", NW * HCOLS, FR)
        a0_ = top[0]
        n_ar = (nc.sbuf_usable_end - a0_) // 4
        assert n_ar >= 21504, n_ar
        AR = sb("AR", 21504, at=a0_)

        def ar(o, n):
            return AR[:, o:o + n]

        def ar_r(name, o, n):
            return sb(name, n, FR, at=a0_ + 4 * o)

        bank = [ctx.enter_context(nc.psum_tensor(f"bank{i}", [128, 512], F32)) for i in range(8)]
        PE = Queue(nc.tensor, sem("s_pe"))
        DV = Queue(nc.vector, sem("s_dve"))
        AC = Queue(nc.scalar, sem("s_act"))
        SP = Queue(nc.sync, sem("s_sp"))
        s_raw = [sem(f"s_raw{i}") for i in range(NRAW)]
        s_x = [sem(f"s_x{i}") for i in range(4)]
        s_cst, s_pv, s_pos, s_rv, s_bt, s_E, s_oh, s_sgu, s_out, s_fin = (
            sem(n) for n in ("s_cst", "s_pv", "s_pos", "s_rv", "s_bt", "s_E", "s_oh", "s_sgu", "s_out", "s_fin"))

        vec = {"ts": nc.vector.tensor_scalar, "tt": nc.vector.tensor_tensor,
               "stt": nc.vector.scalar_tensor_tensor, "copy": nc.vector.tensor_copy,
               "red": nc.vector.tensor_reduce, "recip": nc.vector.reciprocal,
               "memset": nc.vector.memset, "scan": nc.vector.tensor_tensor_scan,
               "bns": nc.vector.bn_stats, "bna": nc.vector.bn_aggr}

        def V_(name, *a, w=(), **k):
            DV.wait(*w)
            return DV.mark(vec[name](*a, **k))

        def V(name, *a, w=(), **k):
            DV.wait(DV.last())
            return V_(name, *a, w=w, **k)

        def A_(out_, in_, func, w=(), **k):
            AC.wait(*w)
            return AC.mark(nc.scalar.activation(out_, in_, func, **k))

        def A(out_, in_, func, w=(), **k):
            AC.wait(AC.last())
            return A_(out_, in_, func, w=w, **k)

        def mm(o, lhsT, rhs, start, stop):
            return nc.tensor.matmul(o, lhsT, rhs, start=start, stop=stop)

        def P(name, rows=128):
            o, w = PCOL[name]
            return pv[0:rows, o:o + w]

        def C(name, rows=128):
            o, w = CCOL[name]
            return cst[0:rows, o:o + w]

        def blk(t, i, n=1):
            return t[:, i * T:(i + n) * T]

        def prev(d, i):
            return d[i] if i >= 0 else None

        def pipe(n, stages, filler=None, pieces=0, at=(0,)):
            slots, k, done = (n + len(stages) - 1) * len(at), 0, 0
            for step in range(n + len(stages) - 1):
                for s in range(len(stages) - 1, -1, -1):
                    if s in at:
                        k += 1
                        go(filler, pieces * k // slots - done)
                        done = pieces * k // slots
                    if 0 <= step - s < n:
                        stages[s](step - s)

        def then(*gens):
            for g in gens:
                yield from g

        def go(gen, n=None):
            while gen is not None and (n is None or n > 0):
                if next(gen, "end") == "end":
                    return
                n = None if n is None else n - 1

        tiles = weight_tiles()
        places, kinds = pack_tiles(tiles)
        n_units = len(kinds) // 2
        last_tile = {}
        for i, (hf, c) in enumerate(places):
            last_tile[hf] = i
        split_no, n_ = {}, 0
        for hf, kd in enumerate(kinds):
            if kd == "w":
                split_no[hf] = n_
                n_ += 1
        st = {"tile": 0, "split": 0, "loaded": -1}
        left = {u: [kd != "none" for kd in kinds[2 * u:2 * u + 2]].count(True) for u in range(n_units)}
        freed = {u: [] for u in range(n_units)}
        read_by_pe, split_done, half_split = {}, {}, []

        def raw_half(hf):
            o = (hf // 2 % NRAW) * 2 * HCOLS + (hf % 2) * HCOLS
            return raw[:, o:o + HCOLS]

        def landed(hf):
            u = hf // 2
            return (s_raw[u % NRAW], 16 * (u // NRAW + 1))

        def load(u):
            if u >= NRAW:
                SP.wait(freed[u - NRAW])
            o = (u % NRAW) * 2 * HCOLS
            nc.sync.dma_start(raw[:, o:o + 2 * HCOLS], dr["W"][u]).then_inc(s_raw[u % NRAW], 16)
            st["loaded"] = u

        def raw_read(hf, tok):
            u = hf // 2
            left[u] -= 1
            freed[u].append(tok)
            if left[u] == 0 and u + NRAW < n_units:
                load(u + NRAW)

        def pump():
            while st["split"] < len(kinds):
                hf = st["split"]
                if kinds[hf] != "w":
                    st["split"] += 1
                    continue
                i = split_no[hf]
                if hf // 2 > st["loaded"] or (i >= NW and i - NW + LAG not in read_by_pe):
                    return
                o = (i % NW) * HCOLS
                wh, wl = WH[:, o:o + HCOLS], WL[:, o:o + HCOLS]
                free_ = read_by_pe[i - NW] if i >= NW else None
                t = A_(wh, raw_half(hf), ACT.Copy, w=[landed(hf), free_])
                half_split.append((st["tile"], hf, wh, wl, t, free_))
                st["split"] += 1

        def end_splits(n):
            while half_split and st["tile"] - half_split[0][0] >= n:
                _, hf, wh, wl, t, free_ = half_split.pop(0)
                split_done[hf] = V_("tt", wl, raw_half(hf), wh.bitcast(F32), ALU.subtract, w=[t, landed(hf), free_])
                raw_read(hf, split_done[hf])

        def take():
            i = st["tile"]
            st["tile"] += 1
            hf, c = places[i]
            w = tile_width(tiles[i])
            end_splits(DEFER)
            if kinds[hf] == "w":
                if hf not in split_done:
                    end_splits(0)
                PE.wait(split_done[hf])
                o = (split_no[hf] % NW) * HCOLS + c
                return WH[:, o:o + w], WL[:, o:o + w]
            PE.wait(landed(hf))
            return raw_half(hf)[:, c:c + w]

        def used(ins):
            i = st["tile"] - 1
            hf = places[i][0]
            if last_tile[hf] != i:
                return None
            t = PE.mark(ins)
            if kinds[hf] == "w":
                read_by_pe[split_no[hf]] = t
            else:
                raw_read(hf, t)
            pump()
            return t

        free = {i: None for i in range(8)}
        BIG = [0, 1, 2]
        turn = [0]
        busy = set()

        def freed_by(b, tok):
            free[b] = tok
            busy.discard(b)


        def next_bank():
            b = next(b for i in range(3) if (b := BIG[(turn[0] + i) % len(BIG)]) not in busy)
            turn[0] += 1
            busy.add(b)
            PE.wait(free[b])
            return b

        def mul(o, wt, xh, xl, first, last):
            wh, wl = wt
            o = o[0:wh.shape[1], :]
            mm(o, wh, xh, first, False)
            mm(o, wh, xl, False, False)
            return mm(o, wl, xh, False, last)

        def proj(n_blocks, xh, xl, nk, evac, ko=0, rdy=None, pre=None):
            due = []
            last = {}
            kb = [0, 1, 2, 3]
            at = {}
            for n, k in tile_order(n_blocks, nk, ko):
                if k == 0:
                    if n < ko:
                        at[n] = kb[n]
                        PE.wait(free[kb[n]])
                    else:
                        at[n] = next_bank()
                if rdy is not None:
                    PE.wait(rdy[k])
                wt = take()
                ins = mul(bank[at[n]][:, 0:T], wt, blk(xh, k), blk(xl, k), k == 0, k == nk - 1)
                t = used(ins)
                if k == nk - 1:
                    last[n] = t or PE.mark(ins)
                    if n == ko - 1 and pre is not None:
                        pre()
                    if n >= ko:
                        due.append(n)
                    elif n == ko - 1:
                        for m in range(ko):
                            freed_by(at[m], evac(m, bank[at[m]][:, 0:T], last[m]))
                if due and (due[0] < n and k == 3 or n == n_blocks - 1 and k == nk - 1):
                    while due:
                        m = due.pop(0)
                        freed_by(at[m], evac(m, bank[at[m]][:, 0:T], last[m]))
                if k % 4 == 3:
                    yield

        def proj_tm(n_blocks, xh, xl, nk, width, evac, every=4):
            for n in range(n_blocks):
                bs = [next_bank(), next_bank()]
                for k in range(nk):
                    wh, wl = take()
                    for tb in range(2):
                        o = bank[bs[tb]][:, 0:width]
                        s = slice(k * T + tb * 128, k * T + (tb + 1) * 128)
                        mm(o, xh[:, s], wh, k == 0, False)
                        mm(o, xh[:, s], wl, False, False)
                        ins = mm(o, xl[:, s], wh, False, k == nk - 1)
                    t = used(ins)
                    if k % every == every - 1 and k < nk - 1:
                        yield
                tk = t or PE.mark(ins)
                for tb in range(2):
                    freed_by(bs[tb], evac(n, tb, bank[bs[tb]], tk))
                yield

        ones = C("ones")
        ident = C("ident")

        def total(src, w, n=1, b=4):
            PE.wait(free[b], *w)
            for k in range(n):
                ins = mm(bank[b][:, 0:T], ones, src[:, k * T:(k + 1) * T], k == 0, k == n - 1)
            return PE.mark(ins)

        def rstd(dst, src, n, eps_col, w=()):
            o = CCOL["eps"][0] + eps_col
            rows = dst.shape[0]
            A(dst, src, ACT.Ln, scale=1.0 / n, bias=cst[0:rows, o:o + 1], w=w)
            return A(dst, dst, ACT.Exp, scale=-0.5)

        def halves(src, hi, lo, w=(), scale=None):
            if scale is None:
                t = A_(hi, src, ACT.Copy, w=w)
                return V_("tt", lo, src, hi.bitcast(F32), ALU.subtract, w=[t])
            t = A_(hi, src, ACT.Copy, scale=scale, w=w)
            return V_("stt", lo, src, scale, hi.bitcast(F32), ALU.mult, ALU.subtract, w=[t])

        def scaled_halves(src, gains, rs, hi, lo, t):
            th, out_ = {}, []
            for i in range(5):
                if i < 4:
                    t2 = V_("stt", blk(src, i), blk(src, i), gains[:, i:i + 1], rs, ALU.mult, ALU.mult, w=[t])
                    th[i] = A_(blk(hi, i), blk(src, i), ACT.Copy, w=[t2])
                if i > 0:
                    out_.append(V_("tt", blk(lo, i - 1), blk(src, i - 1), blk(hi, i - 1).bitcast(F32),
                                   ALU.subtract, w=[th[i - 1]]))
            return out_

        dump_n = [0]

        def dump(name, ap):
            if name in dumps:
                nc.scalar.wait_ge(DV.sem, DV.n)
                nc.scalar.wait_ge(AC.sem, AC.n)
                nc.scalar.dma_start(dumps[name], ap).then_inc(s_out, 16)
                dump_n[0] += 1
                nc.scalar.wait_ge(s_out, 16 * dump_n[0])
                t = AC.mark(nc.scalar.activation(small[:, 63:64], cst[:, 0:1], ACT.Copy))
                DV.wait(t)
                PE.wait(t)

        for q in range(4):
            nc.sync.dma_start(X[:, q * 1024:(q + 1) * 1024], dr["x"][:, q * 1024:(q + 1) * 1024]).then_inc(s_x[q], 16)
            if q == 0:
                load(0)
        posi = sb("posi", T, I32, at=a0_ + 4 * 19456)
        for u in range(1, NRAW):
            load(u)
        nc.scalar.dma_start(posi[:, :], dr["pos"][0:1, :].broadcast_to([128, T])).then_inc(s_pos, 16)
        nc.scalar.dma_start(pv[:, :], dr["pv"][:, :]).then_inc(s_pv, 16)
        nc.scalar.dma_start(cst[:, :], dr["cst"][:, :]).then_inc(s_cst, 16)
        t_cst, t_pv = (s_cst, 16), (s_pv, 16)
        rdy = {}
        for q in range(4):
            s = slice(q * 1024, (q + 1) * 1024)
            t = halves(X[:, s], XH[:, s], XL[:, s], w=[(s_x[q], 16)])
            if q == 0:
                pump()
                end_splits(0)
            for k in range(4 * q, 4 * q + 4):
                rdy[k] = t

        Vt, Z = ar(0, 4096), ar(4096, 4096)
        CH, CL, KH, KL = (ar_r(n, 8192 + 1024 * i, 1024) for i, n in enumerate(("CH", "CL", "KH", "KL")))
        qr = [ar(12288, 1024), ar(13312, 1024)]
        krm = ar(14336, 2048)
        cos, sin = ar(16384, 256), ar(16640, 256)
        Pm = [ar(o, 384) for o in (16896, 17280, 19712, 20096)]
        PT = [ar(17664 + 384 * i, 384) for i in range(2)]
        gt = [ar(18432 + 256 * i, 256) for i in range(2)]
        rt = [ar(18944 + 256 * i, 256) for i in range(2)]
        posf, ang, tmp = ar(19712, 256), ar(19968, 256), ar(20224, 256)
        rsx, rsy = ar(20480, 256), ar(20736, 256)
        ko_ = ar(20992, 512)
        qn = sb("QN", 4096, at=xh0)
        kn = sb("KN", 4096, at=xl0)
        cq, ckv, sqc, krT, kr12 = ar(0, 1024), ar(1024, 1024), ar(2048, 1024), AR[0:64, 3072:3328], ar(3328, 512)

        def ev_c(n, ps, tk):
            if n == 8:
                return V_("copy", krT, ps[0:64, :], w=[tk])
            return V_("copy", (cq if n < 4 else ckv)[:, n % 4 * T:(n % 4 + 1) * T], ps, w=[tk])

        cp_ = proj(9, XH, XL, 16, ev_c, ko=KO, rdy=rdy)
        go(cp_, 20)
        DV.wait(t_cst, t_pv)
        AC.wait(t_cst, t_pv)
        PE.wait(t_cst, t_pv)

        V("copy", posf, posi[:, :], w=[(s_pos, 16)])
        o = CCOL["invf"][0]
        V("ts", ang, posf, cst[:, o:o + 1], None, ALU.mult)
        two_pi = 2 * np.pi
        p1 = float(np.float32(6.28125))
        p2 = float((np.float32(two_pi - 6.28125).view(np.uint32) & np.uint32(0xFFFFF000)).view(np.float32))
        p3 = float(np.float32(two_pi - p1 - p2))
        magic = 12582912.0
        V("ts", tmp, ang, float(1.0 / two_pi), magic, ALU.mult, ALU.add)
        V("ts", tmp, tmp, magic, None, ALU.subtract)
        for p in (p1, p2, p3):
            V("stt", ang, tmp, -p, ang, ALU.mult, ALU.add)
        V("ts", tmp, ang, 3.1415925, -3.1415925, ALU.min, ALU.max)
        t_sin = A_(sin, tmp, ACT.Sin, w=[DV.last()])
        V("stt", ang, ang, -1.0, ang, ALU.mult, ALU.min)
        V("ts", ang, ang, float(np.pi / 2), None, ALU.add)
        t_cos = A_(cos, ang, ACT.Sin, w=[DV.last()])
        DV.wait(t_cos)
        V("memset", krm, 0.0)
        nc.scalar.preload_act_table_set("natural_log_exp_and_others")
        go(cp_)
        t_c = DV.last()
        raw_z = [0]

        def ev_zm(n, ps, tk):
            if raw_z[0] == n:
                raw_z[0] += 1
                return A_(blk(Z, n), ps, ACT.Copy, w=[tk])
            return A_(blk(Z, n), ps, ACT.Silu, w=[tk])

        zp = proj(16, XH, XL, 16, ev_zm)
        sqc2 = ar(8192 + 4096, 1024)
        t_sq_ = [A_(q, src, ACT.Square, w=[t_c, PE.last()]) for q, src in ((sqc, cq), (sqc2, ckv))]
        go(zp, 2)
        PE.wait(free[5], t_c)
        mm(bank[5][:, 0:T], C("R12", 64)[:, 0:128], krT, True, True)
        tk = PE.mark(mm(bank[5][:, T:2 * T], C("R12", 64)[:, 128:256], krT, True, True))
        t_tot = [total(sqc, [t_sq_[0]], 4, 4), total(sqc2, [t_sq_[1]], 4, 6)]
        t_rs_ = [rstd(rs, bank[b][:, 0:T], 512, 0, w=[t_]) for rs, b, t_ in zip((rsx, rsy), (4, 6), t_tot)]
        free[4], free[6] = t_rs_
        go(zp, 4)
        scaled_halves(cq, P("q_norm"), rsx, CH, CL, t_rs_[0])
        go(zp, 4)
        t_cn = scaled_halves(ckv, P("kv_norm"), rsy, KH, KL, t_rs_[1])[3]
        go(zp, 4)
        free[5] = V("copy", kr12, bank[5][:, :], w=[tk])
        kr1, kr2 = kr12[:, 0:T], kr12[:, T:2 * T]
        V("tt", rt[0], kr1, cos, ALU.mult)
        V_("tt", rt[1], kr2, sin, ALU.mult)
        V("tt", ko_[:, 0:T], rt[0], rt[1], ALU.subtract)
        go(zp, 4)
        V("tt", rt[0], kr1, sin, ALU.mult)
        V_("tt", rt[1], kr2, cos, ALU.mult)
        V("tt", ko_[:, T:2 * T], rt[0], rt[1], ALU.add)
        go(zp, 4)
        DV.wait(DV.last())
        for i in range(4):
            for half in range(2):
                V_("copy", krm[32 * i:32 * i + 32, (2 * i + half) * T:(2 * i + half + 1) * T],
                   ko_[32 * i:32 * i + 32, half * T:(half + 1) * T])
        t_krm = DV.last()
        go(zp, 4)
        nc.scalar.preload_act_table(ACT.Silu)
        n_raw = raw_z[0]
        raw_z[0] = -1
        A(Z[:, 0:n_raw * T], Z[:, 0:n_raw * T], ACT.Silu)
        go(zp)
        t_z = AC.last()
        dump("Z", Z)

        t_grp = {}

        def mla_groups():
            for g in range(4):
                yield from proj(2, CH, CL, 4, lambda n, ps, tk: A_(qr[n][:, g * T:(g + 1) * T], ps, ACT.Copy, w=[tk]))
                x1, x2 = (qr[n][:, g * T:(g + 1) * T] for n in range(2))
                V("tt", rt[0], x2, sin, ALU.mult, w=[AC.last()])
                V_("tt", rt[1], x1, sin, ALU.mult)
                V("tt", x1, x1, cos, ALU.mult)
                V("tt", x1, x1, rt[0], ALU.subtract)
                V("tt", x2, x2, cos, ALU.mult)
                V("tt", x2, x2, rt[1], ALU.add)
                yield from proj(4, CH, CL, 4, lambda n, ps, tk: A_(blk(qn, 4 * g + n), ps, ACT.Copy, w=[tk]))
                yield from proj(4, KH, KL, 4, lambda n, ps, tk: V_("copy", blk(kn, 4 * g + n), ps, w=[tk]))
                yield from proj_tm(1, KH, KL, 4, 512, lambda n, tb, ps, tk:
                                   A_(Vt[:, tb * 2048 + g * 512:tb * 2048 + (g + 1) * 512], ps[:, :], ACT.Copy,
                                      w=[tk]))
                t_grp[g] = [AC.last(), DV.last()]

        DV.wait(PE.last(), t_z)
        AC.wait(PE.last(), DV.last())
        PE.wait(t_cn)
        gen = mla_groups()
        while 0 not in t_grp:
            go(gen, 1)

        sc = float(192 ** -0.5)
        mx = [small[:, 8 * i:8 * i + 2] for i in range(2)]
        ss = [small[:, 16 + 8 * i:16 + 8 * i + 2] for i in range(2)]
        tk_s, tk_e, tk_r, tk_t, tk_c, tk_o, tk_n, tk_h, tk_g, rdy = ({} for _ in range(10))

        def st_scores(h):
            while h // 4 not in t_grp:
                go(gen, 1)
            S = bank[3 + h % 2]
            PE.wait(free[3 + h % 2], t_krm, *t_grp[h // 4])
            g, i = h // 4, h % 4
            a = [blk(qn, h), blk(qr[0], g), blk(qr[1], g)]
            k = [blk(kn, h), blk(krm, 2 * i), blk(krm, 2 * i + 1)]
            for j in range(3):
                mm(S[:, 0:128], a[j][:, 0:128], k[j][:, 0:128], j == 0, False)
            mm(S[:, 0:128], C("u", 1), C("v", 1), False, True)
            for j in range(3):
                mm(S[:, 128:384], a[j][:, 128:256], k[j], j == 0, False)
            tk_s[h] = PE.mark(mm(S[:, 256:384], C("u", 1), C("v", 1), False, True))

        def st_max(h):
            S, m = bank[3 + h % 2], mx[h % 2]
            V_("red", m[:, 0:1], S[:, 0:128], AX, ALU.max, w=[tk_s[h], prev(tk_e, h - 2)])
            V_("red", m[:, 1:2], S[:, 128:384], AX, ALU.max)
            tk_n[h] = V("ts", m, m, -sc, None, ALU.mult)

        def st_exp(h):
            S, m = bank[3 + h % 2], mx[h % 2]
            A_(Pm[h % 4][:, 0:128], S[:, 0:128], ACT.Exp, scale=sc, bias=m[:, 0:1], accum_out=ss[h % 2][:, 0:1],
               w=[tk_n[h], prev(tk_t, h - 4), prev(tk_r, h - 2)])
            tk_e[h] = A_(Pm[h % 4][:, 128:384], S[:, 128:384], ACT.Exp, scale=sc, bias=m[:, 1:2],
                         accum_out=ss[h % 2][:, 1:2])
            free[3 + h % 2] = tk_e[h]

        def st_norm(h):
            s, p = ss[h % 2], Pm[h % 4]
            V_("recip", s, s, w=[tk_e[h]])
            V("ts", p[:, 0:128], p[:, 0:128], s[:, 0:1], None, ALU.mult)
            tk_r[h] = V_("ts", p[:, 128:384], p[:, 128:384], s[:, 1:2], None, ALU.mult)

        def st_turn(h):
            b, p = bank[5 + h % 2], Pm[h % 4]
            PE.wait(free[5 + h % 2], tk_r[h])
            for j in range(3):
                ins = nc.tensor.transpose(b[:, 128 * j:128 * j + 128], p[:, 128 * j:128 * j + 128], ident)
            tk_t[h] = PE.mark(ins)

        def st_copy(h):
            tk_c[h] = free[5 + h % 2] = A_(PT[h % 2], bank[5 + h % 2][:, 0:384], ACT.Copy,
                                           w=[tk_t[h], prev(tk_o, h - 2)])

        def st_pv(h):
            PE.wait(tk_c[h], free[7])
            mm(bank[7][:, 0:T], Vt[:, h * 128:(h + 1) * 128], PT[h % 2][:, 0:256], True, False)
            tk_o[h] = PE.mark(mm(bank[7][:, 128:T], Vt[:, 2048 + h * 128:2048 + (h + 1) * 128],
                                 PT[h % 2][:, 256:384], False, True))

        def st_gate(h):
            tk_g[h] = free[7] = V_("tt", gt[h % 2], bank[7][:, 0:T], blk(Z, h), ALU.mult,
                                   w=[tk_o[h], prev(tk_h, h - 2), t_z])
            rdy[h] = halves(gt[h % 2], blk(XH, h), blk(XL, h), w=[tk_g[h], tk_o[h]])
            tk_h[h] = rdy[h]

        nc.scalar.preload_act_table_set("natural_log_exp_and_others")
        pipe(16, [st_scores, st_max, st_exp, st_norm, st_turn, st_copy, st_pv, st_gate], gen, 92, (0, 4, 6))
        go(gen)
        dump("cos", cos)
        dump("qn", qn[:, :])
        dump("V", Vt)

        def ev_res(D):
            def ev(n, ps, tk):
                t = V_("stt", blk(D, n), blk(X, n), ALPHA, ps, ALU.mult, ALU.add, w=[tk])
                if n == 0:
                    V("copy", acc[:, :], blk(D, 0))
                else:
                    V("tt", acc[:, :], acc[:, :], blk(D, n), ALU.add)
                return t
            return ev

        def layer_norm(layer, D, SQ, gain, after=None):
            tk = total(acc, [DV.last()])
            V("ts", mu[:, :], bank[4][:, 0:T], -1.0 / DM, None, ALU.mult, w=[tk])
            free[4] = DV.last()
            nc.scalar.preload_act_table_set("natural_log_exp_and_others")
            toks = []
            m3_ = mu[:, :].rearrange("p (o t) -> p o t", o=1).broadcast_to([128, 4, T])
            for q in range(4):
                s = slice(q * 1024, (q + 1) * 1024)
                d4 = D[:, s].rearrange("p (c t) -> p c t", c=4)
                t = V_("tt", d4, d4, m3_, ALU.add, w=[DV.last()] if q == 0 else [])
                toks.append(A_(SQ[:, s], D[:, s], ACT.Square, w=[t]))
            t = V_("tt", SQ[:, 2048:3072], SQ[:, 2048:3072], SQ[:, 3072:4096], ALU.add, w=[toks[3]])
            toks[2] = t
            PE.wait(free[4])
            for k in range(12):
                PE.wait(toks[k // 4])
                ins = mm(bank[4][:, 0:T], ones, blk(SQ, k), k == 0, k == 11)
            tk = PE.mark(ins)
            t_r = free[4] = rstd(mu[:, :], bank[4][:, 0:T], DM, 0, w=[tk, DV.last()])
            ow, ob = PCOL["ln_w"][0] + 16 * layer, PCOL["ln_b"][0] + 16 * layer
            AC.wait(PE.last())

            def chunks():
                th = {}
                for k in range(18):
                    if k < 16:
                        t2 = V_("stt", blk(D, k), blk(D, k), pv[:, ow + k:ow + k + 1], mu[:, :], ALU.mult,
                                ALU.mult, w=[t_r])
                        A_(blk(X, k), blk(D, k), ACT.Identity, bias=pv[:, ob + k:ob + k + 1], w=[t2])
                        if gain is None:
                            th[k] = A_(blk(XH, k), blk(D, k), ACT.Identity, bias=pv[:, ob + k:ob + k + 1])
                        else:
                            og = PCOL[gain][0]
                            th[k] = A(blk(XH, k), blk(X, k), ACT.Copy, scale=pv[:, og + k:og + k + 1])
                    j = k - 2
                    if j >= 0:
                        hi = blk(XH, j).bitcast(F32)
                        if gain is None:
                            ready[j] = V_("tt", blk(XL, j), blk(X, j), hi, ALU.subtract, w=[th[j]])
                        else:
                            ready[j] = V_("stt", blk(XL, j), blk(X, j), pv[:, og + j:og + j + 1], hi, ALU.mult,
                                          ALU.subtract, w=[th[j]])
                        if after is not None:
                            after(j, th[j])
                    if k != 1:
                        yield

            ready = Ahead(chunks(), 4)
            return ready

        go(proj(16, XH, XL, 16, ev_res(ar(0, 4096)), ko=KO, rdy=rdy))
        rdy = layer_norm(0, ar(0, 4096), ar(4096, 4096), None)

        QK, Vm, O, HN = ar(0, 4096), ar(4096, 4096), ar(8192, 4096), ar(12288, 4096)
        E8 = AR[0:8, 15360:16384]
        GR = AR[0:8, 20992:21504]
        AC.wait(DV.last())
        nc.scalar.dma_start(E8, dr["late"][0:8, 766:1790]).then_inc(s_E, 16)
        ocw, ocb = PCOL["conv_w"][0], PCOL["conv_b"][0]

        def ev_conv(n, ps, tk):
            y = blk(QK, n)
            cw = lambda i: pv[:, ocw + 16 * i + n:ocw + 16 * i + n + 1]
            V_("ts", y, ps, cw(3), pv[:, ocb + n:ocb + n + 1], ALU.mult, ALU.add, w=[tk])
            for s in (1, 2, 3):
                t = V("stt", y[:, s:T], ps[:, 0:T - s], cw(3 - s), y[:, s:T], ALU.mult, ALU.add)
            A_(y, y, ACT.Silu, w=[t])
            return t

        go(proj(16, XH, XL, 16, ev_conv, ko=KO, rdy=rdy))
        t_qk = AC.last()

        ip, fp, ab, e1, lf, Fc, ai, Mx, one8 = (AR[0:8, 12544 + i * T:12544 + (i + 1) * T] for i in range(9))
        oib, ofb = PCOL["ib"][0], PCOL["fb"][0]

        def ev_gates(n, ps, tk):
            V_("ts", ip, ps[0:8, :], pv[0:8, oib:oib + 1], None, ALU.add, w=[tk])
            return V_("ts", fp, ps[32:40, :], pv[0:8, ofb:ofb + 1], None, ALU.add)

        go(proj(1, XH, XL, 16, ev_gates))
        vp = proj_tm(4, XH, XL, 16, 512, lambda n, tb, ps, tk:
                     A_(Vm[:, tb * 2048 + n * 512:tb * 2048 + (n + 1) * 512], ps[:, :], ACT.Copy, w=[tk]))
        nc.scalar.preload_act_table_set("natural_log_exp_and_others")
        go(vp, 1)
        V("stt", ab, fp, -1.0, fp, ALU.mult, ALU.min)
        A(e1, ab, ACT.Exp, w=[DV.last()])
        t = A(e1, e1, ACT.Ln, bias=cst[0:8, CCOL["ones"][0]:CCOL["ones"][0] + 1])
        go(vp, 1)
        V("ts", lf, fp, 0.0, None, ALU.min)
        V("tt", lf, lf, e1, ALU.subtract, w=[t])
        V("memset", one8, 1.0)
        V("scan", Fc, one8, lf, 0.0, ALU.mult, ALU.add)
        V("tt", ai, ip, Fc, ALU.subtract)
        V("scan", Mx, ai, ai, 0.0, ALU.max, ALU.max)
        V("ts", GR[:, 0:T], Mx, -1.0, None, ALU.mult)
        t_gr = V("tt", GR[:, T:2 * T], GR[:, 0:T], Fc, ALU.subtract)
        go(vp, 2)
        PE.wait(t_gr, free[5])
        nc.tensor.transpose(bank[5][:, 0:8], ai[:, 0:128], ident[0:8, 0:8])
        tk = PE.mark(nc.tensor.transpose(bank[5][:, 8:16], ai[:, 128:256], ident[0:8, 0:8]))
        aT = small[:, 0:16]
        t_aT = free[5] = V("copy", aT, bank[5][:, 0:16], w=[tk])
        go(vp)
        t_v = AC.last()

        dk = float(128 ** -0.5)
        Dt = [ar(16384 + 384 * i, 384) for i in range(2)]
        At = [ar(17152 + 384 * i, 384) for i in range(2)]
        cap = [ar(17920 + 256 * i, 256) for i in range(4)]
        rcp = [ar(18944 + 256 * i, 256) for i in range(2)]
        sqh = [ar(19456 + 512 * i, 512) for i in range(2)]
        rsh = [ar(20480 + 256 * i, 256) for i in range(2)]
        t0, t1, t2, t3, t4, t5, t6, t7, t8 = ({} for _ in range(9))
        mC = C("mC")

        def m0(h):
            PE.wait(free[3], t_gr, (s_E, 16))
            t0[h] = PE.mark(mm(bank[3][:, 0:512], E8[:, 128 * h:128 * (h + 1)], GR, True, True))

        def m1(h):
            D = Dt[h % 2]
            PE.wait(free[4], t_qk, t_v)
            q, k = blk(QK, h), blk(QK, 8 + h)
            mm(bank[4][:, 0:256], k[:, 0:128], q, True, True)
            t1[h] = PE.mark(mm(bank[4][:, 256:384], k[:, 128:256], q[:, 128:256], True, True))
            V_("tt", D[:, 0:256], bank[3][:, 0:256], mC, ALU.add, w=[t0[h]])
            t2[h] = V_("tt", D[:, 256:384], bank[3][:, 128:256], mC[:, 0:128], ALU.add)
            A_(D[:, 0:256], D[:, 0:256], ACT.Exp, bias=aT[:, h:h + 1], w=[t2[h], t_aT])
            A_(D[:, 256:384], D[:, 256:384], ACT.Exp, bias=aT[:, 8 + h:9 + h])
            t4[h] = A_(cap[h % 4], bank[3][:, 256:512], ACT.Exp, w=[prev(t6, h - 4)])
            free[3] = t4[h]

        def m3(h):
            t3[h] = free[4] = V_("stt", At[h % 2], bank[4][:, 0:384], dk, Dt[h % 2], ALU.mult, ALU.mult,
                                 w=[t1[h], t4[h], prev(t5, h - 2)])

        def m4(h):
            N, a = bank[5 + h % 2], At[h % 2]
            PE.wait(t3[h], free[5 + h % 2], free[7])
            for c in range(2):
                vo = h * 256 + c * 128
                mm(N[:, c * T:(c + 1) * T], Vm[:, vo:vo + 128], a[:, 0:256], True, False)
                mm(N[:, c * T + 128:(c + 1) * T], Vm[:, 2048 + vo:2048 + vo + 128], a[:, 256:384], False, True)
            mm(bank[7][:, 0:T], ones, a[:, 0:256], True, False)
            t5[h] = PE.mark(mm(bank[7][:, 128:T], ones, a[:, 256:384], False, True))

        def m5(h):
            r, hv = rcp[h % 2], HN[:, 512 * h:512 * (h + 1)]
            V_("tt", r, bank[7][:, 0:T], cap[h % 4], ALU.max, w=[t5[h]])
            t6[h] = free[7] = V("stt", r, bank[7][:, 0:T], -1.0, r, ALU.mult, ALU.max)
            V("recip", r, r)
            free[5 + h % 2] = V("tt", hv.rearrange("p (c t) -> p c t", c=2),
                                bank[5 + h % 2][:, :].rearrange("p (c t) -> p c t", c=2),
                                r.rearrange("p (o t) -> p o t", o=1).broadcast_to([128, 2, T]), ALU.mult)
            t7[h] = A_(sqh[h % 2], hv, ACT.Square, w=[DV.last(), prev(t8, h - 2)])

        def m6(h):
            PE.wait(t7[h], free[2])
            mm(bank[2][:, 0:T], ones, sqh[h % 2][:, 0:T], True, False)
            t8[h] = PE.mark(mm(bank[2][:, 0:T], ones, sqh[h % 2][:, T:2 * T], False, True))

        def m7(h):
            t = free[2] = rstd(rsh[h % 2], bank[2][:, 0:T], 256, 0, w=[t8[h], DV.last()])
            on = PCOL["head_norm"][0] + 2 * h
            for c in range(2):
                hb = HN[:, 512 * h + c * T:512 * h + (c + 1) * T]
                V_("stt", hb, hb, pv[:, on + c:on + c + 1], rsh[h % 2], ALU.mult, ALU.mult, w=[t])

        def ev_o(n, ps, tk):
            o, e = blk(O, n), eo[n % 2]
            A_(e, ps, ACT.Abs, w=[tk, prev(t_eo, n - 2)])
            r = A_(o, ps, ACT.Copy)
            A(e, e, ACT.Exp, scale=-1.0)
            t = A(e, e, ACT.Ln, bias=ones[:, 0:1])
            t_eo[n] = V_("stt", o, o, 0.0, e, ALU.min, ALU.subtract, w=[t])
            if n % 4 == 3 and n > 4:
                end_o(n - 7)
            return r

        def end_o(n):
            A_(O[:, n * T:(n + 4) * T], O[:, n * T:(n + 4) * T], ACT.Exp, w=[t_eo[n + 3]])

        eo, t_eo = [mu, acc], {}
        BIG[:] = [0, 1]
        op_ = proj(16, XH, XL, 16, ev_o)
        DV.wait(PE.last())
        pipe(8, [m0, m1, m3, m4, m5, m6, m7], op_, 64, (0, 1, 3, 5))
        go(op_)
        end_o(12)
        BIG[:] = [0, 1, 2]
        dump("HN", HN)
        dump("O", O)

        HH, HL = ar_r("HH", 0, 4096), ar_r("HL", 4096, 4096)
        ez = [ar(16384 + 256 * i, 256) for i in range(3)]
        hz = [ar(17152 + 256 * i, 256) for i in range(3)]
        rdy, tq = {}, {}

        def ev_z(n, ps, tk):
            e, h_ = ez[n % 3], hz[n % 3]
            r = A_(e, ps, ACT.Silu, w=[tk, prev(tq, n - 3)])
            tq[n] = V_("tt", e, e, blk(O, n), ALU.mult, w=[r])
            t = V("tt", h_, e, blk(HN, n), ALU.mult)
            rdy[n] = halves(h_, blk(HH, n), blk(HL, n), w=[t])
            return r

        nc.scalar.preload_act_table(ACT.Silu)
        AC.wait(DV.last(), PE.last())
        DV.wait(PE.last(), AC.last())
        go(proj(16, XH, XL, 16, ev_z))
        go(proj(16, HH, HL, 16, ev_res(ar(8192, 4096)), ko=KO, rdy=rdy))
        MIX = ar(0, 4096)
        QZ, RAW, BT, VSW, DVt, DQ, DK = (ar(4096, 2048), ar(6144, 2048), ar(8192, 2048), ar(10240, 512),
                                         ar(10752, 1024), ar(11776, 2048), ar(13824, 1024))
        WK = 14848
        U_, CV, sgw, sgb = ar(WK + 3872, 1024), ar(WK + 4896, 1024), ar(10752, 1024), mu_acc
        kcn, vc, GX, GA, sqk, ge, rsP, rsT = (ar(WK + 6080, 16), AR[0:15, WK + 6096:WK + 6224],
                                              ar(WK + 6224, 48), ar(WK + 6272, 48), ar(WK + 6320, 16),
                                              ar(WK + 6336, 32), ar(WK + 6368, 256), ar(WK + 6624, 2))
        SQ2, SQ3, t_sq, t_rs = ar(12288, 1024), ar(13312, 1024), {}, {}

        def squares(j, tok):
            if j % 4 < 3:
                return
            q = j // 4
            xq = X[:, q * 1024:(q + 1) * 1024]
            if q == 0:
                t_sq[0] = A_(SQ2, xq, ACT.Square, w=[tok, DV.last(), PE.last()])
            else:
                t = t_sq[3] = A_(SQ3, xq, ACT.Square, w=[tok, t_sq[q - 1]])
                if q < 3:
                    t_sq[q] = V_("tt", SQ2, SQ2, SQ3, ALU.add, w=[t, t_sq[0], t_sq[q - 1]])

        def pre_rs():
            PE.wait(free[4], t_sq[2])
            for k in range(8):
                if k == 4:
                    PE.wait(t_sq[3])
                ins = mm(bank[4][:, 0:T], ones, blk(SQ2 if k < 4 else SQ3, k % 4), k == 0, k == 7)
            tk = PE.mark(ins)
            free[4] = t_rs[0] = rstd(rsP, bank[4][:, 0:T], DM, 0, w=[tk])
            DV.wait(t_rs[0])

        rdy = layer_norm(1, ar(8192, 4096), ar(12288, 4096), "norm_mix", squares)

        hot = ar(11776 + 512, 766)
        rv = AR[0:8, 13824:13824 + 383]
        BR = ar(WK, 2048)

        def band_out():
            AC.wait(t_rs[0])
            nc.scalar.dma_start(hot[0:32, :], dr["late"][:, 0:766]).then_inc(s_oh, 16)
            PE.wait((s_oh, 16), free[5])
            tk = PE.mark(mm(bank[5][0:8, 0:383], P("table", 32), hot[0:32, 0:383], True, True))
            t = free[5] = V("tt", rv, bank[5][0:8, 0:383], hot[0:8, 383:766], ALU.add, w=[tk, (s_oh, 16)])
            SP.wait(t)
            nc.sync.dma_start(dr["rv"][:, :], rv).then_inc(s_rv, 16)

        def band_in():
            SP.wait((s_rv, 16))
            DV.wait((s_rv, 16))
            band = bass.AP(dr["rv"].tensor, 0, [[1, 128], [383, 8], [1, 256]])
            nc.sync.dma_start(BR.rearrange("p (h k) -> p h k", h=8), band).then_inc(s_bt, 16)

        def band_turn():
            PE.wait((s_bt, 16))
            for i in range(4):
                b = 5 + i % 2
                PE.wait(free[b])
                tk = PE.mark(mm(bank[b][:, :], C("J"), BR[:, 512 * i:512 * (i + 1)], True, True))
                free[b] = V_("copy", BT[:, 512 * i:512 * (i + 1)], bank[b][:, :], w=[tk])

        p1_ = proj(8, XH, XL, 16, lambda n, ps, tk: V_("tt", blk(RAW, n), ps, rsP, ALU.mult, w=[tk]),
                   ko=KO, rdy=rdy, pre=pre_rs)
        go(p1_, 16)
        band_out()
        go(p1_, 8)
        V_("memset", QZ, 0.0)
        band_in()
        go(p1_, 8)
        V_("memset", DQ, 0.0)
        go(p1_)

        PE.wait(t_rs[0], free[7])
        nc.tensor.transpose(bank[7][:, 0:128], rsP[:, 0:128], ident)
        tk = PE.mark(nc.tensor.transpose(bank[7][:, 128:256], rsP[:, 128:256], ident))
        free[7] = t_rst = V("copy", rsT, bank[7][:, 0:256:128], w=[tk])
        AC.wait(t_rst)

        def ev_vsw(n, tb, ps, tk):
            V_("ts", VSW[:, tb * 256:(tb + 1) * 256], ps[:, 0:256], rsT[:, tb:tb + 1], None, ALU.mult, w=[tk])
            return V_("ts", GA[:, tb * 24:(tb + 1) * 24], ps[:, 256:280], rsT[:, tb:tb + 1], None, ALU.mult)

        pvs = proj_tm(1, XH, XL, 16, 280, ev_vsw)
        go(pvs, 2)
        band_turn()
        go(pvs)
        A(GA, GA, ACT.Exp, scale=-1.0, w=[DV.last()])
        V("ts", GA, GA, 1.0, None, ALU.add, w=[AC.last()])
        V("recip", GA, GA)
        gx3 = GX.rearrange("p (h s) -> p h s", s=6)
        ga3 = [GA[:, tb * 24:(tb + 1) * 24].rearrange("p (h s) -> p h s", s=3) for tb in range(2)]
        for tb, c in ((1, 0), (0, 2)):
            for j in range(2):
                V("copy", gx3[:, :, c + j], ga3[tb][:, :, 1 + j])
        V("copy", gx3[:, :, 4], ga3[1][:, :, 0])
        orv = CCOL["rowv"][0]
        V("ts", gx3[:, :, 5], ga3[0][:, :, 0], cst[:, orv:orv + 1], None, ALU.mult)

        obones = C("bones")
        ksn, kwn = blk(RAW, 6), blk(RAW, 7)
        sq6, rs6 = ar(WK + 3072, 512), ar(WK + 3584, 512)

        def ev_d(n, ps, tk):
            if n >= 4:
                return V_("tt", DK[:, (n - 4) * T:(n - 3) * T], ps, rsP, ALU.mult, w=[tk])
            for half in range(2):
                sl = slice(64 * half, 64 * half + 64)
                h = 2 * n + half
                r = V_("tt", DQ[sl, h * T:(h + 1) * T], ps[sl, :], rsP[sl, :], ALU.mult, w=[tk])
            return r

        tk_cmp = {}

        def d_and_cmp():
            g = proj(8, XH, XL, 16, ev_d)
            for b in range(8):
                for _ in range(4):
                    next(g)
                    yield
                PE.wait(t_zb, free[3])
                i = b // 4
                for l in range(8 * b % 32, 8 * b % 32 + 8):
                    ins = mm(bank[3][:, 16 * i:16 * i + 15], take(), zb[i][:, 15 * l:15 * l + 15], l == 0, l == 31)
                    tu = used(ins)
                tk_cmp[b] = tu or PE.mark(ins)
            go(g)

        dp = d_and_cmp()
        tt_ = None
        go(dp, 1)
        zb = [ar(WK + 2048, 480), ar(WK + 2560, 480)]
        for i in range(2):
            src = blk(RAW, 4 + i)
            win = bass.AP(src.tensor, src.offset, [list(src.ap[0]), [1, 32], [16, 15]])
            opos = PCOL["cmp_pos"][0] + 32 * i
            posb = pv[:, opos:opos + 32].rearrange("p (l o) -> p l o", o=1).broadcast_to([128, 32, 15])
            V("tt", zb[i].rearrange("p (l n) -> p l n", l=32), win, posb, ALU.add, w=[PE.last()])
        t_zb = DV.last()
        for pr in (0, 2, 6):
            t = A(sq6, RAW[:, pr * T:(pr + 2) * T], ACT.Square, w=[tt_, DV.last()])
            go(dp, 3)
            PE.wait(t, free[7])
            tt_ = PE.mark(mm(bank[7][:, :], obones, sq6, True, True))
            t = free[7] = rstd(rs6, bank[7][:, :], 64, 0, w=[tt_, DV.last()])
            go(dp, 3)
            for j in range(2):
                n = pr + j
                src = blk(RAW, n)
                if n < 4:
                    og = PCOL["q_gain"][0]
                    for g in range(2):
                        sl = slice(64 * g, 64 * g + 64)
                        V_("stt", QZ[sl, (n + 4 * g) * T:(n + 4 * g + 1) * T], src[sl, :], pv[sl, og:og + 1],
                           rs6[sl, j * T:(j + 1) * T], ALU.mult, ALU.mult, w=[t])
                else:
                    og = PCOL["k_gain"][0]
                    V_("stt", src, src, pv[:, og:og + 1], rs6[:, j * T:(j + 1) * T], ALU.mult, ALU.mult, w=[t])
        go(dp)

        nc.scalar.preload_act_table(ACT.Gelu_apprx_tanh)
        for i in range(2):
            A(ge[:, 16 * i:16 * i + 15], bank[3][:, 16 * i:16 * i + 15], ACT.Gelu_apprx_tanh, w=[tk_cmp[7]])
        free[3] = t_ge = AC.last()
        nc.scalar.preload_act_table_set("natural_log_exp_and_others")
        dvp = proj_tm(1, XH, XL, 16, 512, lambda n, tb, ps, tk:
                      V_("ts", DVt[:, tb * 512:(tb + 1) * 512], ps[:, :], rsT[:, tb:tb + 1], None, ALU.mult, w=[tk]))
        go(dvp, 2)
        PE.wait(t_ge, free[3])
        used(mm(bank[3][:, 0:15], take(), ge[:, 0:15], True, True))
        ins = mm(bank[3][0:15, 128:256], ge[:, 16:31], take(), True, True)
        tk_kc = used(ins) or PE.mark(ins)
        kcn_, sqk_ = kcn[:, 0:15], sqk[:, 0:15]
        V("copy", vc, bank[3][0:15, 128:256], w=[tk_kc])
        V("copy", kcn_, bank[3][:, 0:15])
        t = A(sqk_, kcn_, ACT.Square, w=[DV.last()])
        go(dvp, 1)
        PE.wait(t, DV.last())
        tk = PE.mark(mm(bank[3][:, 256:271], obones, sqk_, True, True))
        t = free[3] = rstd(sqk_, bank[3][:, 256:271], 64, 0, w=[tk])
        og = PCOL["k_gain"][0]
        t_kc = V("stt", kcn_, kcn_, pv[:, og:og + 1], sqk_, ALU.mult, ALU.mult, w=[t])
        go(dvp)
        t_d = DV.last()
        dump("QZ", QZ)

        def ev_u(n, ps, tk):
            return V_("tt", U_[:, n * T:(n + 1) * T], ps, rsP, ALU.mult, w=[tk])

        def ev_cv(n, tb, ps, tk):
            return A_(CV[:, tb * 512:(tb + 1) * 512], ps[:, :], ACT.Copy, scale=rsT[:, tb:tb + 1], w=[tk])

        def spatial_gating():
            nc.scalar.preload_act_table(ACT.Gelu_apprx_tanh)
            A(U_, U_, ACT.Gelu_apprx_tanh, w=[DV.last()])
            A(CV, CV, ACT.Gelu_apprx_tanh)
            t_cv = AC.last()
            nc.scalar.preload_act_table_set("natural_log_exp_and_others")
            go(bp, 1)
            yield
            for tb in range(2):
                v = CV[:, tb * 512:(tb + 1) * 512]
                V("bns", bst[:, 8 * tb:8 * tb + 6], v, w=[t_cv])
                V("bna", bmv[:, 2 * tb:2 * tb + 2], bst[:, 8 * tb:8 * tb + 6])
            t = DV.last()
            for tb in range(2):
                rstd(bmv[:, 2 * tb + 1:2 * tb + 2], bmv[:, 2 * tb + 1:2 * tb + 2], 1, 1, w=[t])
            t_r = AC.last()
            go(bp, 1)
            yield
            sg3 = sgw.rearrange("p (h q) -> p h q", h=8)
            otr = CCOL["tril"][0]
            tril = cst[:, otr:otr + 128].rearrange("p (o q) -> p o q", o=1).broadcast_to([128, 8, 128])
            V_("tt", sg3, sg3, tril, ALU.mult, w=[(s_sgu, 32)])
            for tb in range(2):
                v = CV[:, tb * 512:(tb + 1) * 512]
                V_("ts", v, v, bmv[:, 2 * tb:2 * tb + 1], bmv[:, 2 * tb + 1:2 * tb + 2], ALU.subtract, ALU.mult,
                   w=[t_r])
            t = DV.last()
            go(bp, 2)
            yield
            for j in range(4):
                b = next_bank()
                PE.wait(t)
                for c in range(2):
                    ins = mm(bank[b][:, c * 256:(c + 1) * 256], CV[:, c * 512 + j * 128:c * 512 + (j + 1) * 128],
                             sgw[:, j * 256:(j + 1) * 256], True, True)
                tk = PE.mark(ins)
                ps3 = bank[b][:, :].rearrange("p (c q) -> p c q", c=2)
                m = blk(MIX, 4 + j)
                d3 = m.rearrange("p (c q) -> p c q", c=2)
                for half in range(2):
                    sl = slice(64 * half, 64 * half + 64)
                    bias = sgb[sl, 128 * j:128 * (j + 1)].rearrange("p (o q) -> p o q", o=1)
                    free[b] = V_("tt", d3[sl], ps3[sl, :, 128 * half:128 * half + 128],
                                 bias.broadcast_to([64, 2, 128]), ALU.add, w=[tk])
                freed_by(b, free[b])
                V("tt", m, m, U_[:, j * T:(j + 1) * T], ALU.mult)
                go(bp, 1)
                yield

        bg, ztmp = RAW[:, 0:1024], blk(RAW, 4)
        o2 = PCOL["conv2"][0]

        def ev_b(n, ps, tk):
            j = n % 4
            if n < 4:
                return V_("tt", bg[:, j * T:(j + 1) * T], ps, rsP, ALU.mult, w=[tk])
            y = blk(MIX, j)
            if n < 8:
                return V_("tt", y, ps, rsP, ALU.mult, w=[tk])
            r = V_("tt", ztmp, ps, rsP, ALU.mult, w=[tk])
            V("tt", ztmp, ztmp, y, ALU.mult)
            cw = lambda i: pv[:, o2 + 4 * i + j:o2 + 4 * i + j + 1]
            V("ts", y, ztmp, cw(2), None, ALU.mult)
            V("stt", y[:, 1:T], ztmp[:, 0:T - 1], cw(1), y[:, 1:T], ALU.mult, ALU.add)
            V("stt", y[:, 2:T], ztmp[:, 0:T - 2], cw(0), y[:, 2:T], ALU.mult, ALU.add)
            V("tt", y, y, bg[:, j * T:(j + 1) * T], ALU.mult)
            return r

        bp = proj(12, XH, XL, 16, ev_b)
        bst, bmv = ar(WK + 5920, 16), ar(WK + 5936, 4)

        def gating_projections():
            yield from proj(4, XH, XL, 16, ev_u)
            yield from proj_tm(1, XH, XL, 16, 512, ev_cv, 1)
            while next(bp, "end") != "end":
                yield


        ds = float(64 ** -0.5)
        zA = [ar(WK + 384 * i, 384) for i in range(4)]
        lA = [ar(WK + 1536 + 384 * i, 384) for i in range(4)]
        eA = [ar(WK + 3072 + 384 * i, 384) for i in range(2)]
        mS = C("mS")
        g1, g2, g3, g4, g5, g6 = ({} for _ in range(6))

        def d0(h):
            S = bank[3 + h % 2]
            PE.wait(free[3 + h % 2], t_d)
            q, k = blk(DQ, h), blk(DK, h // 2)
            mm(S[:, 0:256], k[:, 0:128], q, True, True)
            g1[h] = PE.mark(mm(S[:, 256:384], k[:, 128:256], q[:, 128:256], True, True))

        def d1(h):
            S, z, e = bank[3 + h % 2], zA[h % 4], eA[h % 2]
            A_(z, S[:, 0:384], ACT.Copy, scale=ds, w=[g1[h]])
            free[3 + h % 2] = A_(e, S[:, 0:384], ACT.Abs, scale=ds, w=[prev(g3, h - 2)])
            A(e, e, ACT.Exp, scale=-1.0)
            g2[h] = A(e, e, ACT.Ln, bias=ones[:, 0:1])

        def d2(h):
            z, e, l = zA[h % 4], eA[h % 2], lA[h % 4]
            V_("stt", e, z, 0.0, e, ALU.max, ALU.add, w=[g2[h]])
            V("tt", z, z, e, ALU.subtract)
            g3[h] = V_("stt", l, e, -1.0, mS, ALU.mult, ALU.mult, w=[prev(g5, h - 4)])

        def d3_(h):
            l = lA[h % 4]
            PE.wait(free[5], g3[h])
            mm(bank[5][:, 0:256], C("U"), l[:, 0:256], True, False)
            mm(bank[5][:, 128:256], ones, l[:, 256:384], False, True)
            g4[h] = PE.mark(mm(bank[5][:, 256:384], C("U"), l[:, 256:384], True, True))

        def d4(h):
            z, a = zA[h % 4], lA[h % 4]
            free[5] = V_("tt", z, z, bank[5][:, 0:384], ALU.add, w=[g4[h]])
            t = A_(a, z, ACT.Exp, w=[DV.last()])
            g6[h] = V_("tt", a, a, mS, ALU.mult, w=[t])

        def d5(h):
            a, j = lA[h % 4], h // 2
            PE.wait(free[6 + h % 2], g6[h])
            Ob = bank[6 + h % 2]
            mm(Ob[:, 0:256], DVt[:, j * 128:(j + 1) * 128], a[:, 0:256], True, False)
            g5[h] = PE.mark(mm(Ob[:, 128:256], DVt[:, 512 + j * 128:512 + (j + 1) * 128], a[:, 256:384], False,
                               True))

        def d6(h):
            sl = slice(64 * (h % 2), 64 * (h % 2) + 64)
            free[6 + h % 2] = V_("copy", MIX[sl, (8 + h // 2) * T:(9 + h // 2) * T], bank[6 + h % 2][sl, 0:256],
                                 w=[g5[h]])

        AC.wait(DV.last(), PE.last())
        DV.wait(AC.last(), PE.last())
        cp = gating_projections()
        pipe(8, [d0, d1, d2, d3_, d4, d5, d6], cp, 38, (0, 3, 5))
        SP.wait(g5[7], t_rs[0])
        nc.sync.dma_start(sgw, dr["sgu"][:, 0:1024]).then_inc(s_sgu, 16)
        nc.sync.dma_start(sgb[:, :], dr["sgu"][:, 1024:1536]).then_inc(s_sgu, 16)

        SX = [ar(WK + 1024 * i, 512) for i in range(4)]
        SY = [ar(WK + 1024 * i + 512, 256) for i in range(4)]
        SC = [ar(WK + 1024 * i + 768, 32) for i in range(4)]
        PA = [ar(11776 + 768 * i, 768) for i in range(2)]
        PC = [AR[0:15, 13824 + 256 * i:13824 + 256 * (i + 1)] for i in range(2)]
        nm = [small[:, 8 * i:8 * i + 6] for i in range(4)]
        sm = [small[:, 32 + 8 * i:32 + 8 * i + 6] for i in range(4)]
        n1, n2, n3, n4, n5, n6, n7 = ({} for _ in range(7))

        def seg(h):
            i = h % 4
            return [SX[i][:, 0:256], SX[i][:, 256:512], SY[i][:, 0:128], SY[i][:, 128:256],
                    SC[i][:, 0:15], SC[i][:, 16:23]]

        def a0(h):
            X1, Y1 = bank[3], bank[4]
            PE.wait(free[3], free[4], t_kc)
            q = blk(QZ, h)
            mm(X1[:, 0:256], q[:, 128:256], ksn, True, True)
            mm(X1[:, 256:512], q[:, 128:256], kwn, True, True)
            mm(Y1[:, 0:128], q[:, 0:128], ksn[:, 0:128], True, True)
            mm(Y1[:, 128:256], q[:, 0:128], kwn[:, 0:128], True, True)
            mm(Y1[:, 256:271], q[:, 128:256], kcn_, True, True)
            n1[h] = PE.mark(mm(Y1[:, 272:279], q[:, 0:128], kcn_[:, 0:7], True, True))

        def a1(h):
            i = h % 4
            X1, Y1 = bank[3], bank[4]
            bt = BT[:, h * 256:(h + 1) * 256]
            r2 = lambda ap, n: ap.rearrange("p (s k) -> p s k", s=n)
            V_("stt", r2(SX[i], 2), r2(X1[:, 0:512], 2), ds, r2(bt, 1).broadcast_to([128, 2, 256]), ALU.mult,
               ALU.add, w=[n1[h], prev(n5, h - 4)])
            V_("stt", r2(SY[i], 2), r2(Y1[:, 0:256], 2), ds, r2(bt[:, 128:256], 1).broadcast_to([128, 2, 128]),
               ALU.mult, ALU.add)
            V_("stt", SC[i][:, 0:15], Y1[:, 256:271], ds, bt[:, 31:256:16], ALU.mult, ALU.add)
            V_("stt", SC[i][:, 16:23], Y1[:, 272:279], ds, bt[:, 128 + 31:256:16], ALU.mult, ALU.add)
            free[3] = free[4] = DV.last()
            m = nm[i]
            V("red", m[:, 0:2], r2(SX[i], 2), AX, ALU.max)
            V_("red", m[:, 2:4], r2(SY[i], 2), AX, ALU.max)
            V_("red", m[:, 4:5], SC[i][:, 0:15], AX, ALU.max)
            V_("red", m[:, 5:6], SC[i][:, 16:23], AX, ALU.max)
            n2[h] = V("ts", m, m, -1.0, None, ALU.mult)

        def a2(h):
            i = h % 4
            for s, ap in enumerate(seg(h)):
                n3[h] = A_(ap, ap, ACT.Exp, bias=nm[i][:, s:s + 1], accum_out=sm[i][:, s:s + 1], w=[n2[h]])

        def a3(h):
            i = h % 4
            V("recip", sm[i], sm[i], w=[n3[h]])
            V("tt", sm[i], sm[i], GX[:, 6 * h:6 * h + 6], ALU.mult)
            V("ts", SC[i][:, 0:15], SC[i][:, 0:15], sm[i][:, 4:5], None, ALU.mult)
            for s, ap in enumerate(seg(h)):
                if s != 4:
                    n4[h] = V_("ts", ap, ap, sm[i][:, s:s + 1], None, ALU.mult)

        def a4(h):
            i = h % 4
            PE.wait(free[5], free[6], n4[h])
            for s, B in ((0, bank[5]), (1, bank[6])):
                nc.tensor.transpose(B[:, 0:128], SY[i][:, s * 128:(s + 1) * 128], ident)
                nc.tensor.transpose(B[:, 128:256], SX[i][:, s * 256:s * 256 + 128], ident)
                nc.tensor.transpose(B[:, 256:384], SX[i][:, s * 256 + 128:s * 256 + 256], ident)
            nc.tensor.transpose(bank[5][0:7, 384:512], SC[i][:, 16:23], ident)
            n5[h] = PE.mark(nc.tensor.transpose(bank[6][0:15, 384:512], SC[i][:, 0:15], ident))

        def a5(h):
            i = h % 2
            A_(PA[i][:, 0:384], bank[5][:, 0:384], ACT.Copy, w=[n5[h], prev(n6, h - 2)])
            free[5] = A_(PC[i][0:7, 0:128], bank[5][0:7, 384:512], ACT.Copy)
            A_(PA[i][:, 384:768], bank[6][:, 0:384], ACT.Copy)
            n7[h] = free[6] = A_(PC[i][0:15, 128:256], bank[6][0:15, 384:512], ACT.Copy)

        def a6(h):
            i = h % 2
            Ob = bank[7]
            PE.wait(free[7], n7[h])
            mm(Ob[:, 0:256], VSW[:, 0:128], PA[i][:, 0:256], True, False)
            mm(Ob[:, 128:256], VSW[:, 256:384], PA[i][:, 256:384], False, False)
            mm(Ob[:, 0:256], VSW[:, 128:256], PA[i][:, 384:640], False, False)
            mm(Ob[:, 128:256], VSW[:, 384:512], PA[i][:, 640:768], False, False)
            mm(Ob[:, 0:128], vc[0:7, :], PC[i][0:7, 0:128], False, False)
            n6[h] = PE.mark(mm(Ob[:, 128:256], vc[0:15, :], PC[i][0:15, 128:256], False, True))

        def a7(h):
            g = h // 4
            sl = slice(64 * g, 64 * g + 64)
            free[7] = V_("copy", MIX[sl, (12 + h % 4) * T:(13 + h % 4) * T], bank[7][sl, 0:256], w=[n6[h]])
            if h >= 4:
                gn3[h - 4] = A_(blk(CV, h - 4), blk(MIX, 8 + h), ACT.Square, w=[free[7], DV.last(), PE.last()])

        rdy = {}
        gn3 = {}

        def group_norm(g):
            og = PCOL["group_gain"][0]
            sq = U_ if g < 3 else CV
            ac_, rs_ = ar(10752 + 512 * (g % 2), 256), ar(11008 + 512 * (g % 2), 256)
            b = next_bank() if g < 3 else 4
            if g < 3:
                t = A_(sq, MIX[:, g * 1024:(g + 1) * 1024], ACT.Square, w=[DV.last(), PE.last()])
                t = V_("red", ac_, sq.rearrange("p (c t) -> p t c", c=4), AX, ALU.add, w=[t])
                yield
                tk = total(ac_, [t], 1, b)
            else:
                tk = total(sq, [gn3[j] for j in range(4)], 4, b)
            t = rstd(rs_, bank[b][:, 0:T], 512, 0, w=[tk, DV.last()])
            freed_by(b, t)
            q = slice(g * 1024, (g + 1) * 1024)
            for i, t in enumerate(scaled_halves(MIX[:, q], pv[:, og + 4 * g:og + 4 * g + 4], rs_, XH[:, q],
                                                XL[:, q], t)):
                rdy[4 * g + i] = t
            yield

        FH, FL = ar_r("FH", 11264, 4096), ar_r("FL", 15360, 4096)
        sqx = [ar(19456 + 256 * i, 256) for i in range(2)]
        rsF = ar(21248, 256)
        onf = PCOL["norm_ffn"][0]
        tsx, rdf = {}, {}

        def ev_x3(n, ps, tk):
            r = V_("tt", blk(X, n), blk(X, n), ps, ALU.add, w=[tk])
            A_(sqx[n % 2], blk(X, n), ACT.Square, w=[r, prev(tsx, n - 2)])
            t = AC.last()
            rdf[n] = halves(blk(X, n), blk(FH, n), blk(FL, n), scale=pv[:, onf + n:onf + n + 1])
            if n == 0:
                tsx[n] = V("copy", acc[:, :], sqx[0], w=[t])
            else:
                tsx[n] = V("tt", acc[:, :], acc[:, :], sqx[n % 2], ALU.add, w=[t])
            return r

        wo = proj(16, XH, XL, 16, ev_x3, ko=KO, rdy=rdy)

        def gn_and_out():
            assert 7 in n2
            for g in range(3):
                yield from group_norm(g)
            for _ in range(12):
                next(wo)
                yield

        AC.wait(PE.last(), DV.last())
        DV.wait(AC.last(), PE.last())
        nsa_fill = then(spatial_gating(), bp, gn_and_out())
        pipe(8, [a0, a1, a2, a3, a4, a5, a6, a7], nsa_fill, 56, (0, 4, 6))
        go(nsa_fill)
        dump("MIX", MIX)

        for _ in group_norm(3):
            pass
        DV.wait(PE.last(), AC.last())
        AC.wait(DV.last())
        go(wo)
        dump("x3", X[:, :])

        def pre_rf():
            tk = total(acc, [tsx[15]])
            free[4] = t = rstd(rsF, bank[4][:, 0:T], DM, 0, w=[tk])
            DV.wait(t)
            nc.scalar.preload_act_table(ACT.Silu)

        NB = FFN_HALF
        AH, AL = ar_r("AH", 0, NB * T), ar_r("AL", NB * T, NB * T)
        sg = [ar(19968 + 256 * i, 256) for i in range(2)]
        fu = [ar(20480 + 256 * i, 256) for i in range(3)]
        tsg, tfu, rda = {}, {}, {}

        def ev_f(half):
            def ev(n, ps, tk):
                i = n // 2
                ii = i + NB * half
                if n % 2 == 0:
                    r = V_("tt", sg[i % 2], ps, rsF, ALU.mult, w=[tk])
                    tsg[ii] = A_(sg[i % 2], sg[i % 2], ACT.Silu, w=[r])
                    return r
                u = fu[i % 3]
                r = V_("tt", u, ps, rsF, ALU.mult, w=[tk, prev(tfu, ii - 3)])
                t = V("tt", u, u, sg[i % 2], ALU.mult, w=[tsg[ii]])
                tfu[ii] = rda[i] = halves(u, blk(AH, i), blk(AL, i), w=[t])
                return r
            return ev

        OUT = ar(11264, 4096)
        n_out = [0]

        def ev_down(half):
            def ev(n, ps, tk):
                if half == 0:
                    return V_("tt", blk(X, n), blk(X, n), ps, ALU.add, w=[tk])
                t = V_("tt", blk(OUT, n), blk(X, n), ps, ALU.add, w=[tk])
                AC.wait(t)
                nc.scalar.dma_start(out[:, n * T:(n + 1) * T], blk(OUT, n)).then_inc(s_fin, 16)
                n_out[0] += 1
                return t
            return ev

        for half in range(2):
            AC.wait(PE.last())
            DV.wait(PE.last())
            if half == 0:
                go(proj(2 * NB, FH, FL, 16, ev_f(0), ko=KO, rdy=rdf, pre=pre_rf))
            else:
                go(proj(2 * NB, FH, FL, 16, ev_f(1)))
            go(proj(16, AH, AL, NB, ev_down(half), ko=KO, rdy=rda))
        nc.scalar.wait_ge(s_fin, 16 * n_out[0])
        nc.sync.wait_ge(s_fin, 16 * n_out[0])
        assert st["tile"] == len(tiles)


def pack(inputs):
    w = {k: np.asarray(v) for k, v in inputs.items()}
    tiles = weight_tiles()
    places, kinds = pack_tiles(tiles)
    W = np.zeros((len(kinds) // 2, 128, 2 * HCOLS), np.float32)
    mix = mix_rows()
    mats = {n: w[n].reshape(w[n].shape[-2:]) for n in
            ("mla_w_in", "mla_w_qb", "mla_w_kvb", "mla_w_out", "ml_w_in", "ml_w_out", "w_in_2", "w_out_2",
             "w_ffn_gate_2", "w_ffn_up_2", "w_ffn_down_2")}
    mats["w_out_2"] = mats["w_out_2"][mix]
    w1 = w["cmp_w1_2"].reshape(2, 32, 64, 64)
    w2 = w["cmp_w2_2"].reshape(2, 64, 64)
    for (src, k, cols, kind), (hf, c) in zip(tiles, places):
        u, c = hf // 2, c + HCOLS * (hf % 2)
        if kind == "bd":
            m = w1[k, cols[0]] if src == "cmp_w1_2" else w2[k]
            W[u, 0:64, c:c + 64] = m
            W[u, 64:128, c + 64:c + 128] = m
        elif cols[-1] - cols[0] == len(cols) - 1 and cols[0] + 1 == cols[1]:
            W[u, :, c:c + len(cols)] = mats[src][k:k + 128, cols[0]:cols[0] + len(cols)]
        else:
            W[u, :, c:c + len(cols)] = mats[src][k:k + 128][:, cols]
    pvec = np.zeros((128, NP), np.float32)

    def put(name, a):
        o, n = PCOL[name]
        pvec[:a.shape[0], o:o + a.shape[1]] = a

    def fm(a):
        return a.reshape(-1, 128).T

    put("q_norm", fm(w["mla_q_norm"]))
    put("kv_norm", fm(w["mla_kv_norm"]))
    put("ln_w", fm(w["ln_w"]))
    put("ln_b", fm(w["ln_b"]))
    put("conv_w", fm(w["ml_conv_w"]))
    put("conv_b", fm(w["ml_conv_b"]))
    put("head_norm", fm(w["ml_head_norm"]))
    put("norm_mix", fm(w["norm_mix_2"]))
    put("norm_ffn", fm(w["norm_ffn_2"]))
    for n in ("q_gain", "k_gain"):
        g = w[n + "_2"].reshape(64, 1)
        put(n, np.concatenate([g, g], 0))
    p = w["cmp_pos_2"].reshape(2, 32, 64).transpose(2, 0, 1).reshape(64, 64)
    put("cmp_pos", np.concatenate([p, p], 0))
    put("conv2", fm(w["conv_w_2"]))
    put("group_gain", fm(w["group_gain_2"].reshape(-1)[mix]))
    gb = w["ml_gate_b"].reshape(16, 1)
    put("ib", gb[0:8])
    put("fb", gb[8:16])
    put("table", w["rel_table_2"])
    sgu = np.concatenate([w["sgu_w_2"].reshape(8, 128, 128).transpose(2, 0, 1).reshape(128, 1024),
                          np.repeat(w["sgu_b_2"].reshape(4, 2, 128).transpose(1, 0, 2), 64, axis=0)
                          .reshape(128, 512)], 1)
    cst, late = constants()
    x = w["x"].reshape(T, 16, 128).transpose(2, 1, 0).reshape(128, 4096)
    return {"W": W, "pv": pvec, "cst": cst, "late": late, "sgu": sgu, "x": np.ascontiguousarray(x),
            "pos": np.ascontiguousarray(w["positions"].reshape(1, T).astype(np.int32))}


DUMPS = {}


def kernel(**inputs):
    import concourse.bacc as _bacc
    from concourse.bass_utils import run_bass_kernel_spmd as _run

    nc = _bacc.Bacc("TRN2", target_bir_lowering=False, num_devices=1)
    arrays = pack(inputs)
    dr = {}
    for name, a in arrays.items():
        dr[name] = nc.dram_tensor("in_" + name, a.shape, I32 if name == "pos" else F32, kind="ExternalInput").ap()
    dr["rv"] = nc.dram_tensor("rv", (8, 383), F32, kind="Internal").ap()
    out = nc.dram_tensor("out_0", (128, 4096), F32, kind="ExternalOutput").ap()
    dumps = {k: nc.dram_tensor("dump_" + k, s, F32, kind="ExternalOutput").ap() for k, s in DUMPS.items()}
    build(nc, dr, out, dumps)
    r = _run(nc, [{"in_" + k: a for k, a in arrays.items()}], core_ids=[0])
    y = np.asarray(r.results[0]["out_0"]).reshape(128, 16, T).transpose(2, 1, 0).reshape(1, T, DM)
    return np.ascontiguousarray(y)
```
